# Optimizing a Trainium2 kernel written in Bass

```python
import math
import jax, jax.numpy as jnp
from jax import lax
import numpy as np

D_MODEL = 1024
BATCH = 1
SEQ = 128
DEPTH = 1
DEC_BATCH = 1
DEC_SEQ = 1024
PAST_LEN = 128

GRID_W = 64
D_MIX = D_MODEL
N_HEADS_A = 4
HEAD_DIM_A = 64
V_DIM_A = 2 * HEAD_DIM_A
D_ATTN = N_HEADS_A * V_DIM_A
D_RG = D_MIX - D_ATTN
RG_BLOCKS = 8
RG_BLOCK_W = D_RG // RG_BLOCKS
RG_C = 8.0
CONV_W = 4
CONV_PAD_LEFT = 2
D_FF = 2816
N_MOD = 9
D_IN = 3 * D_ATTN + 2 * D_RG
ROPE_BASE = 10000.0
QBLOCK = 128
EPS = 1e-6

kernel_name = 'hymba_diffattn_rglru_macaron_dit_step'

def _rmsnorm(x, g):
    xf = x.astype(jnp.float32)
    y = xf * lax.rsqrt(jnp.mean(xf * xf, axis=-1, keepdims=True) + EPS)
    return (y * g.astype(jnp.float32)).astype(x.dtype)

def _swiglu(h, w_gate, w_up, w_down):
    return (jax.nn.silu(h @ w_gate) * (h @ w_up)) @ w_down

def _rope_2d(x):
    S = x.shape[1]
    rows = S // GRID_W
    row = jnp.repeat(jnp.arange(rows), GRID_W)
    col = jnp.tile(jnp.arange(GRID_W), rows)
    n_freq = HEAD_DIM_A // 4
    inv_freq = ROPE_BASE ** (-jnp.arange(n_freq, dtype=jnp.float32) / n_freq)

    def rot(xh, pos):
        ang = pos.astype(jnp.float32)[:, None] * inv_freq[None, :]
        cos = jnp.cos(ang)[None, :, None, None, :].astype(x.dtype)
        sin = jnp.sin(ang)[None, :, None, None, :].astype(x.dtype)
        x1, x2 = xh[..., :n_freq], xh[..., n_freq:]
        return jnp.concatenate([x1 * cos - x2 * sin, x1 * sin + x2 * cos], axis=-1)

    half = HEAD_DIM_A // 2
    return jnp.concatenate([rot(x[..., :half], row), rot(x[..., half:], col)], axis=-1)

def _diff_attention(q, k, v, lam):
    B, Sq = q.shape[0], q.shape[1]
    nblk = Sq // QBLOCK
    scale = HEAD_DIM_A ** -0.5
    qb = jnp.moveaxis(q.reshape(B, nblk, QBLOCK, N_HEADS_A, 2, HEAD_DIM_A), 1, 0)

    def block(qi):
        s = jnp.einsum('bqhmd,bkhmd->bhmqk', qi, k, preferred_element_type=jnp.float32) * scale
        p = jax.nn.softmax(s, axis=-1)
        pd = p[:, :, 0] - lam * p[:, :, 1]
        return jnp.einsum('bhqk,bkhv->bqhv', pd.astype(v.dtype), v)

    o = lax.map(block, qb)
    return jnp.moveaxis(o, 0, 1).reshape(B, Sq, N_HEADS_A, V_DIM_A)

def _dwconv(x, w, b):
    S = x.shape[1]
    xp = jnp.pad(x, ((0, 0), (CONV_PAD_LEFT, CONV_W - 1 - CONV_PAD_LEFT), (0, 0)))
    return sum(xp[:, j:j + S] * w[j] for j in range(CONV_W)) + b

def _combine(e1, e2):
    a1, b1 = e1
    a2, b2 = e2
    return a1 * a2, a2 * b1 + b2

def _rglru_dir(xc, w_r, b_r, w_i, b_i, lam, h0, reverse):
    B, S, _ = xc.shape
    xf = xc.astype(jnp.float32)
    xblk = xf.reshape(B, S, RG_BLOCKS, RG_BLOCK_W)
    r = jax.nn.sigmoid(jnp.einsum('bsnc,ncd->bsnd', xblk, w_r.astype(jnp.float32)).reshape(B, S, D_RG) + b_r.astype(jnp.float32))
    i = jax.nn.sigmoid(jnp.einsum('bsnc,ncd->bsnd', xblk, w_i.astype(jnp.float32)).reshape(B, S, D_RG) + b_i.astype(jnp.float32))
    log_a = -RG_C * r * jax.nn.softplus(-lam.astype(jnp.float32))
    a = jnp.exp(log_a)
    bx = jnp.sqrt(-jnp.expm1(2.0 * log_a)) * (i * xf)
    h0 = h0.astype(jnp.float32)
    if reverse:
        bx = bx.at[:, -1].add(a[:, -1] * h0)
    else:
        bx = bx.at[:, 0].add(a[:, 0] * h0)
    _, h = lax.associative_scan(_combine, (a, bx), reverse=reverse, axis=1)
    h_last = h[:, 0] if reverse else h[:, -1]
    return h, h_last

def _rglru(xr, xg, p, l, h0):
    xc = _dwconv(xr, p['conv_w'][l], p['conv_b'][l])
    hf, hf_last = _rglru_dir(xc, p['rg_w_r'][l, 0], p['rg_b_r'][l, 0], p['rg_w_i'][l, 0], p['rg_b_i'][l, 0], p['rg_lambda'][l, 0], h0[:, 0], False)
    hb, hb_last = _rglru_dir(xc, p['rg_w_r'][l, 1], p['rg_b_r'][l, 1], p['rg_w_i'][l, 1], p['rg_b_i'][l, 1], p['rg_lambda'][l, 1], h0[:, 1], True)
    y = ((hf + hb) * jax.nn.gelu(xg.astype(jnp.float32))).astype(xr.dtype)
    return y, jnp.stack([hf_last, hb_last], axis=1).astype(xr.dtype)

def _layer(x, c, p, l, ctx):
    B, S, _ = x.shape
    mod = jax.nn.silu(c) @ p['w_mod'][l] + p['b_mod'][l]
    mod = mod.reshape((-1, 1, N_MOD * D_MODEL))
    sh1, sc1, g1, sh2, sc2, g2, sh3, sc3, g3 = jnp.split(mod, N_MOD, axis=-1)
    ng = p['norm_g'][l]
    h = _rmsnorm(x, ng[0]) * (1.0 + sc1) + sh1
    x = x + g1 * 0.5 * _swiglu(h, p['ffn_w_gate'][l, 0], p['ffn_w_up'][l, 0], p['ffn_w_down'][l, 0])
    h = _rmsnorm(x, ng[1]) * (1.0 + sc2) + sh2
    proj = h @ p['w_in'][l]
    q, k, v, xr, xg = jnp.split(proj, [D_ATTN, 2 * D_ATTN, 3 * D_ATTN, 3 * D_ATTN + D_RG], axis=-1)
    q = q.reshape(B, S, N_HEADS_A, 2, HEAD_DIM_A)
    k = k.reshape(B, S, N_HEADS_A, 2, HEAD_DIM_A)
    v = v.reshape(B, S, N_HEADS_A, V_DIM_A)
    lp = p['diff_lambda'][l].astype(jnp.float32)
    lam_init = 0.8 - 0.6 * math.exp(-0.3 * l)
    lam = jnp.exp(jnp.sum(lp[0] * lp[1])) - jnp.exp(jnp.sum(lp[2] * lp[3])) + lam_init
    if ctx is None:
        k_all, v_all = k, v
        h0 = jnp.zeros((B, 2, D_RG), jnp.float32)
    else:
        k_ctx, v_ctx, h0 = ctx
        q = _rope_2d(q)
        k = _rope_2d(k)
        k_all = jnp.concatenate([k, k_ctx.reshape(B, -1, N_HEADS_A, 2, HEAD_DIM_A).astype(k.dtype)], axis=1)
        v_all = jnp.concatenate([v, v_ctx.astype(v.dtype)], axis=1)
    o = _diff_attention(q, k_all, v_all, lam)
    o = _rmsnorm(o, p['subln_g'][l]) * (1.0 - lam_init)
    rg, h_last = _rglru(xr, xg, p, l, h0)
    mix = jnp.concatenate([o.reshape(B, S, D_ATTN), rg], axis=-1) @ p['w_out'][l]
    x = x + g2 * mix
    h = _rmsnorm(x, ng[2]) * (1.0 + sc3) + sh3
    x = x + g3 * 0.5 * _swiglu(h, p['ffn_w_gate'][l, 1], p['ffn_w_up'][l, 1], p['ffn_w_down'][l, 1])
    return x, k.reshape(B, S, N_HEADS_A, 2 * HEAD_DIM_A), v, h_last

def setup_inputs(seed: int = 0) -> dict:
    key = jax.random.key(seed)
    ks = jax.random.split(key, 32)
    f32 = jnp.float32
    nrm = lambda kk, shape, s: jax.random.normal(kk, shape, f32) * s
    a0 = jax.random.uniform(ks[24], (DEPTH, 2, D_RG), f32, 0.9, 0.999)
    return {
        'x_prompt': nrm(ks[0], (BATCH, SEQ, D_MODEL), 1.0),
        'x_sample': nrm(ks[1], (DEC_BATCH, DEC_SEQ, D_MODEL), 1.0),
        'cache_attn_k': nrm(ks[2], (DEC_BATCH, DEPTH, PAST_LEN, N_HEADS_A, 2 * HEAD_DIM_A), 1.0),
        'cache_attn_v': nrm(ks[3], (DEC_BATCH, DEPTH, PAST_LEN, N_HEADS_A, V_DIM_A), 1.0),
        'state_rglru': nrm(ks[4], (DEC_BATCH, DEPTH, 2, D_RG), 0.5),
        'c': nrm(ks[5], (DEC_BATCH, D_MODEL), 1.0),
        'c_ctx': nrm(ks[6], (D_MODEL,), 1.0),
        'norm_g': 1.0 + nrm(ks[7], (DEPTH, 3, D_MODEL), 0.01),
        'w_mod': nrm(ks[8], (DEPTH, D_MODEL, N_MOD * D_MODEL), D_MODEL ** -0.5),
        'b_mod': nrm(ks[9], (DEPTH, N_MOD * D_MODEL), 0.01),
        'ffn_w_gate': nrm(ks[10], (DEPTH, 2, D_MODEL, D_FF), D_MODEL ** -0.5),
        'ffn_w_up': nrm(ks[11], (DEPTH, 2, D_MODEL, D_FF), D_MODEL ** -0.5),
        'ffn_w_down': nrm(ks[12], (DEPTH, 2, D_FF, D_MODEL), D_FF ** -0.5),
        'w_in': nrm(ks[13], (DEPTH, D_MODEL, D_IN), D_MODEL ** -0.5),
        'w_out': nrm(ks[14], (DEPTH, D_MIX, D_MODEL), D_MIX ** -0.5),
        'diff_lambda': nrm(ks[15], (DEPTH, 4, HEAD_DIM_A), 0.1),
        'subln_g': 1.0 + nrm(ks[16], (DEPTH, V_DIM_A), 0.01),
        'conv_w': nrm(ks[17], (DEPTH, CONV_W, D_RG), CONV_W ** -0.5),
        'conv_b': nrm(ks[18], (DEPTH, D_RG), 0.01),
        'rg_w_r': nrm(ks[19], (DEPTH, 2, RG_BLOCKS, RG_BLOCK_W, RG_BLOCK_W), RG_BLOCK_W ** -0.5),
        'rg_b_r': nrm(ks[20], (DEPTH, 2, D_RG), 0.01),
        'rg_w_i': nrm(ks[21], (DEPTH, 2, RG_BLOCKS, RG_BLOCK_W, RG_BLOCK_W), RG_BLOCK_W ** -0.5),
        'rg_b_i': nrm(ks[22], (DEPTH, 2, D_RG), 0.01),
        'rg_lambda': jnp.log(a0) - jnp.log1p(-a0),
        'final_g': 1.0 + nrm(ks[23], (D_MODEL,), 0.01),
    }

def reference(x_prompt, x_sample, cache_attn_k, cache_attn_v, state_rglru, c, c_ctx,
              norm_g, w_mod, b_mod, ffn_w_gate, ffn_w_up, ffn_w_down, w_in, w_out,
              diff_lambda, subln_g, conv_w, conv_b, rg_w_r, rg_b_r, rg_w_i, rg_b_i,
              rg_lambda, final_g):
    p = dict(norm_g=norm_g, w_mod=w_mod, b_mod=b_mod, ffn_w_gate=ffn_w_gate, ffn_w_up=ffn_w_up,
             ffn_w_down=ffn_w_down, w_in=w_in, w_out=w_out, diff_lambda=diff_lambda,
             subln_g=subln_g, conv_w=conv_w, conv_b=conv_b, rg_w_r=rg_w_r, rg_b_r=rg_b_r,
             rg_w_i=rg_w_i, rg_b_i=rg_b_i, rg_lambda=rg_lambda)
    xp = x_prompt
    k_list, v_list, h_list = [], [], []
    for l in range(DEPTH):
        xp, k_l, v_l, h_l = _layer(xp, c_ctx, p, l, None)
        k_list.append(k_l)
        v_list.append(v_l)
        h_list.append(h_l)
    y_prompt = _rmsnorm(xp, final_g)
    new_cache_attn_k = jnp.stack(k_list, axis=1)
    new_cache_attn_v = jnp.stack(v_list, axis=1)
    new_state_rglru = jnp.stack(h_list, axis=1)
    xs = x_sample
    for l in range(DEPTH):
        xs, _, _, _ = _layer(xs, c, p, l, (cache_attn_k[:, l], cache_attn_v[:, l], state_rglru[:, l]))
    y_sample = _rmsnorm(xs, final_g)
    return (y_prompt, y_sample, new_cache_attn_k, new_cache_attn_v, new_state_rglru)


_drawn_inputs = setup_inputs


def setup_inputs(seed=0):
    import zlib

    import numpy as np

    out = dict(_drawn_inputs(seed))
    spreads = {}
    factors = {'cache_attn_k': 36.832,
     'cache_attn_v': 32.208,
     'state_rglru': 13.732,
     'norm_g': 5.923,
     'b_mod': 2.69,
     'subln_g': 200.0,
     'conv_b': 13.313,
     'rg_b_r': 48.387,
     'rg_b_i': 35.796,
     'final_g': 197.181}
    for name, (base, spread) in spreads.items():
        noise = np.random.default_rng([zlib.crc32(name.encode()), seed]).standard_normal(out[name].shape)
        drawn = base * np.exp(spread * noise) if base else spread * noise
        out[name] = __import__('jax').numpy.asarray(drawn.astype(out[name].dtype))
    for name, factor in factors.items():
        out[name] = (out[name] * factor).astype(out[name].dtype)
    return out
```

```python
import math
from contextlib import ExitStack

import numpy as np

import concourse.bass as bass
from concourse import mybir

F32 = mybir.dt.float32
F32R = mybir.dt.float32r
ACT = mybir.ActivationFunctionType
ALU = mybir.AluOpType
AX = mybir.AxisListType

P = 128
D = 1024
KT = D // P
CTX = 128
LAT = 1024
T = CTX + LAT
CH = 384
NC = T // CH
FF = 2816
FT = FF // P
NG = FT // 2
NH = 4
DH = 64
RGT = 4
NB_MOD = 18
PRE = NB_MOD - NG
SLOTS = 5
EPS = 1e-6
LAM_INIT = 0.8 - 0.6 * math.exp(0.0)
KEYS = T + 128
GRID_W = 64


def chunk(c):
    return slice(c * CH, (c + 1) * CH)


def conds(c):
    if c == 0:
        return [(0, 0, CTX), (1, CTX, CH)]
    return [(1, c * CH, (c + 1) * CH)]


def build(nc, a, out):
    ctx = ExitStack()
    with ctx:
        def sem(name):
            return ctx.enter_context(nc.semaphore(name))

        def sb(name, shape, dt=F32, stack=ctx):
            return stack.enter_context(nc.sbuf_tensor("sb_" + name, shape, dt))

        ones = sb("ones", [P, P])
        mod = sb("mod", [P, 9 * KT, 2])
        bmod = sb("bmod", [P, 9 * KT, 2])
        ng = sb("ng", [P, 3, KT, 2])
        fg = sb("fg", [P, KT])
        eps = sb("eps", [P, 1])
        convw = sb("convw", [P, RGT, 4])
        convb = sb("convb", [P, RGT])
        gbias = sb("gbias", [P, RGT, 2, 2])
        glam = sb("glam", [P, 2, RGT * 2])
        h0 = sb("h0", [P, RGT, 2])
        subg = sb("subg", [P, 1])
        hout = sb("hout", [P, RGT, 2])
        lnorm = sb("lnorm", [P, 32])
        raw = sb("raw", [P, SLOTS, 1024])
        x = sb("x", [P, KT, T])
        tmp = sb("tmp", [P, 4, CH])
        rstd = sb("rstd", [P, CH])
        acts = ExitStack()
        hH = sb("hH", [P, KT, T], F32R, acts)
        hL = sb("hL", [P, KT, T], F32R, acts)
        with ExitStack() as s:
            stage = sb("stage", [P, 2, 4, 1024], F32, s)
        with ExitStack() as s:
            guH = sb("guH", [P, 2, 2, KT, P], F32R, s)
            guL = sb("guL", [P, 2, 2, KT, P], F32R, s)
            dnH = sb("dnH", [P, 2, D], F32R, s)
            dnL = sb("dnL", [P, 2, D], F32R, s)
            hidH = sb("hidH", [P, 2, T], F32R, s)
            hidL = sb("hidL", [P, 2, T], F32R, s)
            modp = sb("modp", [P, 512], F32, s)
            cs = sb("cs", [P, KT, 32], F32, s)
            cin = sb("cin", [P, KT, 2], F32, s)
            sel = sb("sel", [P, 2], F32, s)
        mid = ExitStack()
        v = sb("v", [P, T // P, 512], F32, mid)
        xr = sb("xr", [P, RGT, T], F32, mid)
        xg = sb("xg", [P, RGT, T], F32, mid)
        with ExitStack() as s:
            wiH = sb("wiH", [P, 2, 1024], F32R, s)
            wiL = sb("wiL", [P, 2, 1024], F32R, s)
        with ExitStack() as s:
            cosT = sb("cosT", [P, LAT], F32, s)
            sinT = sb("sinT", [P, LAT], F32, s)
            vc = sb("vc", [P, 512], F32, s)
            kc = sb("kc", [P, NH, P], F32, s)
            ident = sb("ident", [P, P], F32, s)
            mx = sb("mx", [P, 2, 2], F32, s)
            nmx = sb("nmx", [P, 2, 2], F32, s)
            sums = sb("sums", [P, 2, 2], F32, s)
            rec = sb("rec", [P, 2, 2], F32, s)
            coef = sb("coef", [P, 2], F32, s)
            ss = sb("ss", [P, 16], F32, s)
            dl = sb("dl", [P, 4, DH], F32, s)
            lams = sb("lams", [P, 4], F32, s)
            nlam = sb("nlam", [P, 1], F32, s)
        mid.close()
        acts.close()
        with ExitStack() as s:
            qH = sb("qH", [P, T], F32R, s)
            qL = sb("qL", [P, T], F32R, s)
            kH = sb("kH", [P, KEYS], F32R, s)
            kL = sb("kL", [P, KEYS], F32R, s)
            vHL = sb("vHL", [P, KEYS // P, 2, P], F32R, s)
            pr = sb("pr", [P, 2, 2, T], F32, s)
            pTH = sb("pTH", [P, 2, 9, P], F32R, s)
            pTL = sb("pTL", [P, 2, 9, P], F32R, s)
            rot = sb("rot", [P, T], F32, s)
        xd = nc.dram_tensor("x_spilled", [KT, P, T], F32, kind="Internal").ap()
        ps = ctx.enter_context(nc.psum_tensor("ps", [P, 8, 512], F32))

        smalls = sem("smalls")
        cons = sem("cons")
        xin = [sem(f"xin{k}") for k in range(KT)]
        staged = [sem(f"staged{i}") for i in range(2)]
        raw_full = [sem(f"raw_full{s}") for s in range(SLOTS)]
        raw_used = [sem(f"raw_used{s}") for s in range(SLOTS)]
        rl_in = sem("rl_in")
        rl_exp = sem("rl_exp")
        c_ready = sem("c_ready")
        mod_prod = sem("mod_prod")
        mod_copy = sem("mod_copy")
        mod_sum = sem("mod_sum")
        mod_done = sem("mod_done")
        step = sem("step")
        nrm = [{n: sem(f"{n}_{z}") for n in
                ("sq",
                 "sq_used",
                 "sd",
                 "hf",
                 "hi", "h")}
               for z in range(4)]
        ffn = [{n: sem(f"{n}_{z}") for n in
                ("g", "u",
                 "silu",
                 "prod",
                 "hidhi", "hidlo",
                 "d",
                 "x")}
               for z in range(2)]
        w_hi = sem("w_hi")
        spilled = sem("spilled")
        gw_in = sem("gw_in")
        m_ready = sem("m_ready")
        m_ev = sem("m_ev")
        v_ready = sem("v_ready")
        v_ev = sem("v_ev")
        xc_ready = sem("xc_ready")
        gate_ready = sem("gate_ready")
        gate_ev = sem("gate_ev")
        rg_a = sem("rg_a")
        rg_e = sem("rg_e")
        rg_m = sem("rg_m")
        rg_s = sem("rg_s")
        rg_y = sem("rg_y")
        acst = sem("acst")
        outs = sem("outs")
        lam_p = sem("lam_p")
        lam_e = sem("lam_e")
        pp_c = sem("pp_c")
        pp_f = sem("pp_f")
        pp_hi = sem("pp_hi")
        pp_lo = sem("pp_lo")
        s_ready = sem("s_ready")
        mx_ready = sem("mx_ready")
        e_done = sem("e_done")
        pd_ready = sem("pd_ready")
        t_ready = sem("t_ready")
        t_hi = sem("t_hi")
        t_lo = sem("t_lo")
        o_ready = sem("o_ready")
        o_half = sem("o_half")
        o_done = sem("o_done")
        o_ss = sem("o_ss")
        o_sd = sem("o_sd")
        o_nrm = sem("o_nrm")
        ot_ready = sem("ot_ready")
        ot_done = sem("ot_done")
        mix_hi = sem("mix_hi")
        mix_lo = sem("mix_lo")
        xback = sem("xback")
        w_ready = sem("w_ready")
        w_x = sem("w_x")
        y_done = sem("y_done")
        passed = [sem(f'passed{e}') for e in range(2)]
        y_out = sem("y_out")

        gw = tmp[:].rearrange("p a b -> p (a b)")[:, 0:1024]
        o9 = tmp[:].rearrange("p a b -> p (a b)")[:, 0:T]
        SMALLS = ((cin[:], "c"), (bmod[:], "bmod"), (ng[:], "ng"), (fg[:], "fg"), (convw[:], "convw"),
                  (convb[:], "convb"), (gbias[:], "gbias"), (glam[:, 0], "glam"), (h0[:], "h0"),
                  (subg[:], "subg"), (sel[:], "sel"))
        N_SMALL = 16 * len(SMALLS)
        N_ACST = 16 * 6
        FIRST = {"g0": 3, "u0": 4}
        F1 = {"m0": (0, 0), "m1": (1, 0), "m2": (2, 0), "m3": (3, 0), "g1": (4, 0),
              "u1": (0, 1), "d0": (1, 1), "d1": (2, 1), "g0": (3, 1), "u0": (4, 1)}
        F2 = {"g1": (0, 0), "u1": (1, 0), "d0": (2, 0), "d1": (0, 1), "g0": (1, 1), "u0": (2, 1)}
        used_f1 = [0, 0, 0, 1, 1]
        used_in = [2 * NG, 2 * NG, 2 * NG, 2 * NG, 2 * NG]
        used_wo = [used_in[0] + 8, used_in[1] + 8, used_in[2] + 2, used_in[3] + 2, used_in[4]]
        used_f2 = [used_wo[0] + 4, used_wo[1] + 4, used_wo[2]]

        def nth(z, item, i):
            slot, j = (F1, F2)[z][item]
            base = used_f1[slot] if z == 0 else used_f2[slot] + (slot > 0)
            return slot, i * 2 + (base + j)

        def first(z, item):
            if z == 0:
                return FIRST[item], 0
            slot = {"g0": 1, "u0": 2}[item]
            return slot, used_f2[slot]

        blk = ctx.enter_context(nc.Block())


        def alone(eng):
            eng.sem_inc(passed[eng is nc.vector], 1)

        @blk.sync
        def _(sp):
            def load_raw(slot, n, src):
                sp.wait_ge(raw_used[slot], n + 1)
                sp.dma_start(raw[:, slot], src).then_inc(raw_full[slot], 16)

            def ffn_loads(z, i, last):
                if z == 0:
                    for q in range(4):
                        load_raw(*nth(z, f"m{q}", i), a["w_mod"][i + PRE, q])
                load_raw(*nth(z, "g1", i), a["w_gate"][i * 2 + (z * FT + 1)])
                load_raw(*nth(z, "u1", i), a["w_up"][i * 2 + (z * FT + 1)])
                load_raw(*nth(z, "d0", i), a["w_down"][i * 2 + z * FT])
                load_raw(*nth(z, "d1", i), a["w_down"][i * 2 + (z * FT + 1)])
                if not last:
                    load_raw(*nth(z, "g0", i), a["w_gate"][i * 2 + (z * FT + 2)])
                    load_raw(*nth(z, "u0", i), a["w_up"][i * 2 + (z * FT + 2)])

            for dst, name in SMALLS:
                sp.dma_start(dst, a[name]).then_inc(smalls, 16)
            for k in range(KT):
                sp.dma_start(x[:, k], a["x"][k]).then_inc(xin[k], 16)
            for b in range(PRE):
                if b >= 2:
                    sp.wait_ge(mod_prod, b - 1)
                sp.dma_start(stage[:, b % 2], a["w_mod"][b].rearrange("q p n -> p q n")).then_inc(staged[b % 2], 16)
            load_raw(*first(0, "g0"), a["w_gate"][0])
            load_raw(*first(0, "u0"), a["w_up"][0])
            with sp.Fori(0, NG - 1) as i:
                ffn_loads(0, i, False)
            ffn_loads(0, NG - 1, True)
            load_raw(0, used_in[0], a["w_in"][0])
            load_raw(1, used_in[1], a["w_in"][1])
            sp.wait_ge(ffn[0]["x"], 3 + NG * NC * KT)
            for k in range(KT):
                sp.dma_start(xd[k], x[:, k]).then_inc(spilled, 16)
            sp.wait_ge(nrm[1]["h"], NC * KT)
            sp.dma_start(gw, a["gw"]).then_inc(gw_in, 16)
            for e in range(2, 8):
                load_raw(e % 2, used_in[e % 2] + e // 2, a["w_in"][e])
            for n in range(4):
                load_raw(2 + n % 2, used_in[2 + n % 2] + n // 2, a["w_v"][n])
            with sp.Fori(0, 4) as i:
                for f in range(2):
                    load_raw(f, i + (used_in[f] + 4), a["w_in"][i * 2 + (8 + f)])
            sp.wait_ge(rg_y, RGT)
            sp.dma_start(out["h"], hout[:]).then_inc(outs, 16)
            sp.wait_ge(v_ev, 18)
            sp.dma_start(out["v"], v[:, 0]).then_inc(outs, 16)
            sp.wait_ge(m_ev, 6 + 16 * NC)
            sp.dma_start(out["k"].rearrange("h p t -> p h t"), x[:, 4:8, 0:CTX]).then_inc(outs, 16)
            sp.wait_ge(m_ready, 16 * NC)
            for dst, name in ((cosT, "cos"), (sinT, "sin"), (vc, "vc"), (ident, "ident")):
                sp.dma_start(dst[:], a[name]).then_inc(acst, 16)
            sp.dma_start(kc[:], a["kc"].rearrange("h p t -> p h t")).then_inc(acst, 16)
            sp.dma_start(dl[:].rearrange("p a b -> p (a b)"), a["dl"].partition_broadcast(P)).then_inc(acst, 16)
            load_raw(0, used_wo[0], a["w_out"][0])
            load_raw(1, used_wo[1], a["w_out"][1])
            sp.wait_ge(outs, 48)
            sp.wait_ge(spilled, 16 * KT)
            sp.wait_ge(mix_lo, NC * KT)
            for k in range(KT):
                sp.dma_start(x[:, k], xd[k]).then_inc(xback, 16)
            with sp.Fori(0, 3) as i:
                for f in range(2):
                    load_raw(f, i + (used_wo[f] + 1), a["w_out"][i * 2 + (2 + f)])
            load_raw(*first(1, "g0"), a["w_gate"][FT])
            load_raw(*first(1, "u0"), a["w_up"][FT])
            with sp.Fori(0, NG - 1) as i:
                ffn_loads(1, i, False)
            ffn_loads(1, NG - 1, True)
            for c in range(NC):
                for k in range(KT):
                    sp.wait_ge(y_done, c * KT + k + 1)
                    sp.dma_start(out["y"][k, :, chunk(c)], x[:, k, chunk(c)]).then_inc(y_out, 16)
            sp.wait_ge(y_out, 16 * NC * KT)

        @blk.tensor
        def _(pe):
            for z in range(2):
                pe.sem_inc(ffn[z]["u"], 6)
                pe.sem_inc(ffn[z]["d"], 24)

            def three(o, wH, wL, xH, xL, begin, end):
                pe.matmul(o, wH, xH, start=begin, stop=False)
                pe.matmul(o, wH, xL, start=False, stop=False)
                return pe.matmul(o, wL, xH, start=False, stop=end)

            def stats(z, c):
                for k in range(KT):
                    pe.wait_ge(nrm[z]["sq"], c * KT + k + 1)
                    if k == 0 and c > 0:
                        pe.wait_ge(nrm[z]["sd"], c)
                    pe.matmul(ps[:, 6, 0:CH], ones[:], tmp[:, k % 2], start=k == 0,
                              stop=k == KT - 1).then_inc(nrm[z]["sq_used"], 1)

            def mod_partial(src, used):
                for kk in range(2):
                    for q in range(4):
                        m = pe.matmul(ps[32 * q:32 * q + 32, 7, :], cs[:, 2 * q + kk, :], src[:, q, kk * 512:(kk + 1) * 512],
                                      start=kk == 0, stop=kk == 1, tile_position=(0, 32 * q))
                        if kk == 1 and q == 3:
                            m.then_inc(mod_prod, 1)
                        elif kk == 1 and used:
                            m.then_inc(raw_used[q], 1)

            def mod_total():
                for n in range(4):
                    m = pe.matmul(ps[:, 7, 2 * n:2 * n + 2], modp[:, n * P:(n + 1) * P], sel[:], start=True, stop=True)
                m.then_inc(mod_sum, 1)

            pe.wait_ge(cons, 1)
            stats(0, 0)
            pe.wait_ge(c_ready, 1)
            pe.wait_ge(smalls, N_SMALL)
            for b in range(PRE):
                pe.wait_ge(staged[b % 2], 16 * (b // 2 + 1))
                if b:
                    pe.wait_ge(mod_done, b)
                mod_partial(stage[:, b % 2], False)
                pe.wait_ge(mod_copy, b + 1)
                mod_total()
            for c in range(1, NC):
                stats(0, c)

            def ffn_pe(z, i):
                s = ffn[z]
                if z == 0:
                    for q in range(4):
                        slot, n = nth(0, f"m{q}", i)
                        pe.wait_ge(raw_full[slot], n * 16 + 16)
                    pe.wait_ge(mod_done, i + PRE)
                    mod_partial(raw, True)
                for f in range(2):
                    for c in range(NC):
                        b = (f * NC + c) % 2
                        o = i * 6 + (f * NC + c)
                        if c == 0:
                            for w in "gu":
                                slot, n = nth(z, f"{w}{f}", i)
                                pe.wait_ge(raw_used[slot], n + 2 if f else n)
                        pe.wait_ge(nrm[2 * z]["h"], (c + 1) * KT)
                        pe.wait_ge(s["silu"], o + 1)
                        for k in range(KT):
                            m = three(ps[:, b, 0:CH], guH[:, f, 0, k], guL[:, f, 0, k], hH[:, k, chunk(c)],
                                      hL[:, k, chunk(c)], k == 0, k == KT - 1)
                        m.then_inc(s["g"], 1)
                        pe.wait_ge(s["prod"], o + 1)
                        for k in range(KT):
                            m = three(ps[:, 2 + b, 0:CH], guH[:, f, 1, k], guL[:, f, 1, k], hH[:, k, chunk(c)],
                                      hL[:, k, chunk(c)], k == 0, k == KT - 1)
                        m.then_inc(s["u"], 1)
                        if z == 0 and f == 0 and c == 0:
                            pe.wait_ge(mod_copy, i + (PRE + 1))
                            mod_total()
                for w in ("d0", "d1"):
                    slot, n = nth(z, w, i)
                    pe.wait_ge(raw_used[slot], n + 2)
                for c in range(NC):
                    pe.wait_ge(s["hidlo"], i * 6 + (6 + c))
                    for t in range(KT):
                        pe.wait_ge(s["x"], i * 24 + (c * KT + t + 1))
                        for f in range(2):
                            m = three(ps[:, 4 + (c * KT + t) % 3, 0:CH], dnH[:, f, t * P:(t + 1) * P],
                                      dnL[:, f, t * P:(t + 1) * P], hidH[:, f, chunk(c)], hidL[:, f, chunk(c)],
                                      f == 0, f == 1)
                        m.then_inc(s["d"], 1)

            with pe.Fori(0, NG - 1) as i:
                ffn_pe(0, i)
            ffn_pe(0, NG - 1)
            pe.wait_ge(ffn[0]["x"], 3 + NG * 24)
            for c in range(NC):
                stats(1, c)

            def in_tile(i, f, slot_n):
                pe.wait_ge(raw_used[f], slot_n + 2)
                for c in range(NC):
                    pe.wait_ge(nrm[1]["h"], (c + 1) * KT)
                    pe.wait_ge(m_ev, i * 6 + (f * NC + c + 1))
                    for k in range(KT):
                        m = three(ps[:, f * NC + c, 0:CH], wiH[:, f, k * P:(k + 1) * P], wiL[:, f, k * P:(k + 1) * P],
                                  hH[:, k, chunk(c)], hL[:, k, chunk(c)], k == 0, k == KT - 1)
                    m.then_inc(m_ready, 1)

            def gates(j):
                pe.wait_ge(xc_ready, j + 1)
                for n in range(12):
                    c, g = n % NC, n // NC
                    w = slice((j * 4 + g) * DH, (j * 4 + g + 1) * DH)
                    if j * 12 + n >= 2:
                        pe.wait_ge(gate_ev, j * 12 + n - 1)
                    for r in (slice(0, DH), slice(DH, P)):
                        m = pe.matmul(ps[r, 6 + n % 2, 0:CH], gw[r, w], x[r, 0, chunk(c)], start=True, stop=True,
                                      tile_position=(r.start, r.start))
                    m.then_inc(gate_ready, 1)

            with pe.Fori(0, 2) as i:
                for f in range(2):
                    in_tile(i, f, i + used_in[f])
            pe.wait_ge(gw_in, 16)
            for e in range(4, 8):
                in_tile(e // 2, e % 2, e // 2 + used_in[e % 2])
                gates(e - 4)
            pe.wait_ge(m_ev, 6 + 24)
            for hf in range(2):
                for kk in range(2):
                    pe.wait_ge(raw_used[2 + kk], used_in[2 + kk] + hf + 2)
                for t in range(T // P):
                    n = hf * 9 + t
                    if n >= 6:
                        pe.wait_ge(v_ev, n - 5)
                    tk = slice(t * P, (t + 1) * P)
                    for k in range(KT):
                        wv = slice((k % 4) * 256, (k % 4 + 1) * 256)
                        m = three(ps[:, n % 6, 0:256], hH[:, k, tk], hL[:, k, tk], wiH[:, k // 4, wv], wiL[:, k // 4, wv],
                                  k == 0, k == KT - 1)
                    m.then_inc(v_ready, 1)
            pe.wait_ge(v_ev, 18)
            with pe.Fori(0, 4) as i:
                for f in range(2):
                    in_tile(i + 4, f, i + (used_in[f] + 4))

            def scores(q, k0, k1):
                parts = [(c, min(CH, k1 - k0 - c * CH)) for c in range(-(-(k1 - k0) // CH))]
                for c, w in parts:
                    kk = slice(k0 + c * CH, k0 + c * CH + w)
                    for j, (A, B) in enumerate(((qH, kH), (qH, kL), (qL, kH))):
                        for m in range(2):
                            r = slice(m * DH, (m + 1) * DH)
                            mm = pe.matmul(ps[:, 3 * m + c, 0:w], A[r, q * P:(q + 1) * P], B[r, kk],
                                           start=j == 0, stop=j == 2, tile_position=(m * DH, 0))
                            if j == 2 and (c, w) == parts[-1]:
                                mm.then_inc(s_ready, 1)

            pe.wait_ge(m_ev, 6 + 48)
            pe.wait_ge(acst, N_ACST)
            with pe.Fori(0, NH) as hd:
                pe.wait_ge(pp_lo, hd * 7 + 7)
                for n in range(10):
                    if n < 9:
                        if n > 0:
                            pe.wait_ge(e_done, hd * 18 + 2 * n)
                        scores(n, *((0, CTX) if n == 0 else (CTX, KEYS)))
                    if n == 0:
                        continue
                    t = n - 1
                    nk = 1 if t == 0 else 9
                    groups = 1 if t == 0 else 3
                    g0 = 0 if t == 0 else 1 + 3 * (t - 1)
                    pe.wait_ge(pd_ready, hd * 9 + (t + 1))
                    if t == 0:
                        pe.wait_ge(ot_done, hd * 3 + 1)
                    for g in range(groups):
                        pe.wait_ge(t_lo, hd * 25 + (g0 + g + 1))
                        for k in range(3 * g, min(3 * g + 3, nk)):
                            m = pe.transpose(ps[:, 6, (k % 3) * P:(k % 3 + 1) * P], pr[:, t % 2, 0, k * P:(k + 1) * P],
                                             ident[:])
                        m.then_inc(t_ready, 1)
                    pe.wait_ge(t_lo, hd * 25 + (g0 + groups + 1))
                    pe.wait_ge(o_done, hd * 9 + (t + 2))
                    for k in range(nk):
                        rhs = vHL[:, 0 if t == 0 else 1 + k].rearrange("p a b -> p (a b)")
                        pe.matmul(ps[:, 7, 0:256], pTH[:, t % 2, k], rhs, start=k == 0, stop=False)
                        m = pe.matmul(ps[:, 7, 0:256], pTL[:, t % 2, k], rhs, start=False, stop=k == nk - 1)
                    m.then_inc(o_ready, 1)
                pe.wait_ge(o_nrm, hd + 1)
                for g in range(3):
                    pe.wait_ge(ot_done, hd * 3 + (g + 1))
                    for k in range(3):
                        m = pe.transpose(ps[:, 6, k * P:(k + 1) * P], tmp[:, g, k * P:(k + 1) * P], ident[:])
                    m.then_inc(ot_ready, 1)

            pe.wait_ge(mix_lo, NC * KT)
            with pe.Fori(0, 4) as i:
                for f in range(2):
                    pe.wait_ge(raw_used[f], i + (used_wo[f] + 2))
                    for c in range(NC):
                        pe.wait_ge(w_x, i * 6 + (f * NC + c + 1))
                        for k in range(KT):
                            m = three(ps[:, f * NC + c, 0:CH], wiH[:, f, k * P:(k + 1) * P], wiL[:, f, k * P:(k + 1) * P],
                                      hH[:, k, chunk(c)], hL[:, k, chunk(c)], k == 0, k == KT - 1)
                        m.then_inc(w_ready, 1)
            for c in range(NC):
                stats(2, c)
            pe.wait_ge(w_x, 6 + 24)
            with pe.Fori(0, NG - 1) as i:
                ffn_pe(1, i)
            ffn_pe(1, NG - 1)
            pe.wait_ge(ffn[1]["x"], 3 + NG * 24)
            for c in range(NC):
                stats(3, c)

        @blk.scalar
        def _(act):
            for z in range(2):
                act.sem_inc(ffn[z]["silu"], 2)
            act.sem_inc(m_ev, 6)
            act.sem_inc(ot_done, 1)

            def cast(dst, slot, n, free=None):
                act.wait_ge(raw_full[slot], n * 16 + 16)
                if free is not None:
                    act.wait_ge(*free)
                act.activation(dst, raw[:, slot], ACT.Copy).then_inc(w_hi, 1)

            def squares(z, c):
                s = nrm[z]
                for k in range(KT):
                    if z == 0 and c == 0:
                        act.wait_ge(xin[k], 16)
                    n = c * KT + k
                    if n >= 2:
                        act.wait_ge(s["sq_used"], n - 1)
                    act.activation(tmp[:, k % 2], x[:, k, chunk(c)], ACT.Square).then_inc(s["sq"], 1)

            def root(z, c):
                s = nrm[z]
                act.wait_ge(s["sq_used"], (c + 1) * KT)
                if c > 0:
                    act.wait_ge(s["h"], c * KT)
                act.activation(rstd[:], ps[:, 6, 0:CH], ACT.Sqrt, bias=eps[:, 0:1]).then_inc(s["sd"], 1)

            def h_hi(z, c):
                s = nrm[z]
                for k in range(KT):
                    act.wait_ge(s["hf"], c * KT + k + 1)
                    act.activation(hH[:, k, chunk(c)], tmp[:, 2 + k % 2], ACT.Copy).then_inc(s["hi"], 1)

            def norm(z):
                squares(z, 0)
                root(z, 0)
                for c in range(1, NC):
                    squares(z, c)
                    if z < 3:
                        h_hi(z, c - 1)
                    root(z, c)
                if z < 3:
                    h_hi(z, NC - 1)

            def mod_evac(b, used):
                act.wait_ge(mod_prod, b + 1)
                if used:
                    act.sem_inc(raw_used[3], 1)
                act.activation(modp[:], ps[:, 7, :], ACT.Copy).then_inc(mod_copy, 1)

            act.wait_ge(smalls, N_SMALL)
            act.wait_ge(cons, 3)
            act.activation(cs[:, :, 0:2], cin[:], ACT.Silu).then_inc(c_ready, 1)
            act.wait_ge(rl_in, 1)
            act.activation(lnorm[:, 8:16], lnorm[:, 0:8], ACT.Exp).then_inc(rl_exp, 1)
            squares(0, 0)
            root(0, 0)
            for b in range(4):
                mod_evac(b, False)
            h_hi(0, 0)
            for b in range(4, PRE):
                mod_evac(b, False)
            for j, w in enumerate(("g0", "u0")):
                cast(guH[:, 0, j].rearrange("p k n -> p (k n)"), *first(0, w))
            squares(0, 1)
            root(0, 1)
            squares(0, 2)
            h_hi(0, 1)
            root(0, 2)
            h_hi(0, 2)

            def ffn_act(z, i, last):
                s = ffn[z]

                def hidden(f, c):
                    o = i * 6 + (f * NC + c)
                    b = (f * NC + c) % 2
                    act.wait_ge(s["g"], o + 1)
                    act.wait_ge(s["prod"], o + 1)
                    act.activation(tmp[:, b], ps[:, b, 0:CH], ACT.Silu).then_inc(s["silu"], 1)
                    act.wait_ge(s["prod"], o + 3)
                    act.wait_ge(s["d"], i * 24 + 8 * (c + 1))
                    act.activation(hidH[:, f, chunk(c)], tmp[:, 2 + b], ACT.Copy).then_inc(s["hidhi"], 1)

                if z == 0:
                    mod_evac(i + PRE, True)
                for j, w in enumerate(("g1", "u1")):
                    cast(guH[:, 1, j].rearrange("p k n -> p (k n)"), *nth(z, w, i), (s["u"], i * 6 + 6))
                hidden(0, 0)
                for j in range(2):
                    cast(dnH[:, j], *nth(z, f"d{j}", i), (s["d"], i * 24 + 24))
                hidden(0, 1)
                hidden(0, 2)
                if not last:
                    for j, w in enumerate(("g0", "u0")):
                        cast(guH[:, 0, j].rearrange("p k n -> p (k n)"), *nth(z, w, i), (s["u"], i * 6 + 9))
                for c in range(NC):
                    hidden(1, c)

            with act.Fori(0, NG - 1) as i:
                ffn_act(0, i, False)
            ffn_act(0, NG - 1, True)
            act.wait_ge(ffn[0]["x"], 3 + NG * 24)
            act.wait_ge(ffn[0]["d"], 24 + NG * 24)
            for e in range(2):
                cast(wiH[:, e], e, used_in[e])
            norm(1)

            with act.Fori(0, 2) as i:
                for f in range(2):
                    for c in range(NC):
                        act.wait_ge(m_ready, i * 6 + (f * NC + c + 1))
                        alone(act)
                        act.activation(xr[:, i * 2 + f, chunk(c)], ps[:, f * NC + c, 0:CH], ACT.Copy).then_inc(m_ev, 1)
                    cast(wiH[:, f], f, i + (used_in[f] + 1))
            act.wait_ge(spilled, 16 * KT)
            act.wait_ge(nrm[1]["h"], NC * KT)
            for e in range(4, 8):
                j = e - 4
                for c in range(NC):
                    act.wait_ge(m_ready, e * NC + c + 1)
                    act.activation(xg[:, j, chunk(c)], ps[:, (e % 2) * NC + c, 0:CH], ACT.Gelu_apprx_tanh).then_inc(m_ev, 1)
                if e < 6:
                    cast(wiH[:, e % 2], e % 2, e // 2 + 1 + used_in[e % 2])
                else:
                    cast(wiH[:, e - 6], e - 4, used_in[e - 4])
                if j:
                    act.wait_ge(rg_y, j)
                for n in range(12):
                    c, g = n % NC, n // NC
                    act.wait_ge(gate_ready, j * 12 + n + 1)
                    act.activation(x[:, 1 + g, chunk(c)], ps[:, 6 + n % 2, 0:CH], ACT.Sigmoid,
                                   bias=gbias[:, j, g // 2, g % 2:g % 2 + 1]).then_inc(gate_ev, 1)
                act.wait_ge(gate_ev, j * 12 + 12)
                for d in range(2):
                    act.activation(x[:, 5 + d], x[:, 1 + 2 * d], ACT.Exp, scale=glam[:, 0, 2 * j + d:2 * j + d + 1]).then_inc(rg_a, 1)
                act.wait_ge(rg_a, 2 * j + 2)
                for d in range(2):
                    act.activation(x[:, 1 + 2 * d], x[:, 1 + 2 * d], ACT.Tanh,
                                   scale=glam[:, 1, 2 * j + d:2 * j + d + 1]).then_inc(rg_e, 1)
                for d in range(2):
                    act.wait_ge(rg_m, 2 * j + d + 1)
                    act.activation(x[:, 1 + 2 * d], x[:, 1 + 2 * d], ACT.Sqrt).then_inc(rg_s, 1)
            act.wait_ge(v_ready, 9)
            for kk in range(2):
                cast(wiH[:, kk], 2 + kk, used_in[2 + kk] + 1)
            act.wait_ge(v_ready, 18)
            for e in range(2):
                cast(wiH[:, e], e, used_in[e] + 4)
            act.wait_ge(rg_y, RGT)
            def qk_pair(i, last):
                for f in range(2):
                    for c in range(NC):
                        act.wait_ge(m_ready, i * 6 + (24 + f * NC + c + 1))
                        alone(act)
                        act.activation(x[:, i * 2 + f, chunk(c)], ps[:, f * NC + c, 0:CH], ACT.Copy).then_inc(m_ev, 1)
                    if not last:
                        cast(wiH[:, f], f, i + (used_in[f] + 5))
            with act.Fori(0, 3) as i:
                qk_pair(i, False)
            qk_pair(3, True)

            act.wait_ge(m_ev, 6 + 48)
            act.wait_ge(m_ready, 48)
            act.wait_ge(acst, N_ACST)
            act.wait_ge(lam_p, 1)
            act.activation(lams[:, 2:4], lams[:, 0:2], ACT.Exp).then_inc(lam_e, 1)
            with act.Fori(0, NH) as hd:
                act.activation(pr[:, 0, 0, 0:LAT], x[:, hd + 4, CTX:T], ACT.Copy).then_inc(pp_c, 1)
                act.activation(pr[:, 0, 1, 0:LAT], x[:, hd, CTX:T], ACT.Copy).then_inc(pp_c, 1)
                act.activation(vHL[:, 0:9, 0], v[:, :, bass.ds(hd * P, P)], ACT.Copy).then_inc(pp_hi, 1)
                act.activation(vHL[:, 9, 0], vc[:, bass.ds(hd * P, P)], ACT.Copy).then_inc(pp_hi, 1)
                act.activation(kH[:, 0:CTX], x[:, hd + 4, 0:CTX], ACT.Copy).then_inc(pp_hi, 1)
                act.activation(kH[:, T:KEYS], kc[:, hd], ACT.Copy).then_inc(pp_hi, 1)
                act.activation(qH[:, 0:CTX], x[:, hd, 0:CTX], ACT.Copy).then_inc(pp_hi, 1)
                for j, dst in enumerate((kH, qH)):
                    act.wait_ge(pp_f, hd * 2 + (j + 1))
                    act.activation(dst[:, CTX:T], pr[:, 0, j, 0:LAT], ACT.Copy).then_inc(pp_hi, 1)
                for n in range(10):
                    if n < 9:
                        act.wait_ge(mx_ready, hd * 9 + (n + 2))
                        if n == 0:
                            act.wait_ge(pp_lo, hd * 7 + 7)
                        for m in range(2):
                            if n == 0:
                                src, dst = ps[:, 3 * m, 0:CTX], pr[:, 0, m, 0:CTX]
                            else:
                                src = ps[:, 3 * m:3 * m + 3, 0:CH]
                                dst = pr[:, n % 2, m].rearrange("p (c t) -> p c t", c=NC)
                            act.activation(dst, src, ACT.Exp, bias=nmx[:, n % 2, m:m + 1], scale=DH ** -0.5,
                                           accum_out=sums[:, n % 2, m:m + 1]).then_inc(e_done, 1)
                    if n == 0:
                        continue
                    t = n - 1
                    nk = 1 if t == 0 else 9
                    groups = 1 if t == 0 else 3
                    g0 = 0 if t == 0 else 1 + 3 * (t - 1)
                    for g in range(groups):
                        act.wait_ge(t_ready, hd * 25 + (g0 + g + 1))
                        w = min(3, nk - 3 * g)
                        act.activation(pTH[:, t % 2, 3 * g:3 * g + w].rearrange("p k n -> p (k n)"), ps[:, 6, 0:w * P],
                                       ACT.Copy).then_inc(t_hi, 1)
                    act.wait_ge(o_ready, hd * 9 + (t + 1))
                    act.activation(tmp[:, t // 3, (t % 3) * P:(t % 3 + 1) * P], ps[:, 7, 0:P], ACT.Copy,
                                   scale=rec[:, t % 2, 0:1]).then_inc(o_half, 1)
                act.wait_ge(o_ss, hd + 1)
                act.activation(ss[:, 0:9], ss[:, 0:9], ACT.Sqrt, bias=eps[:, 0:1], scale=1.0 / P).then_inc(o_sd, 1)
                for g in range(3):
                    act.wait_ge(ot_ready, hd * 3 + (g + 1))
                    alone(act)
                    act.activation(x[:, hd, g * CH:(g + 1) * CH], ps[:, 6, 0:CH], ACT.Copy,
                                   scale=subg[:, 0:1]).then_inc(ot_done, 1)

            act.wait_ge(ot_done, 1 + 12)
            for k in range(KT):
                src = x[:, k] if k < 4 else xr[:, k - 4]
                for c in range(NC):
                    act.activation(hH[:, k, chunk(c)], src[:, chunk(c)], ACT.Copy).then_inc(mix_hi, 1)
            for e in range(2):
                cast(wiH[:, e], e, used_wo[e])
            with act.Fori(0, 3) as i:
                for f in range(2):
                    cast(wiH[:, f], f, i + (used_wo[f] + 1), (w_ready, i * 6 + (3 * f + 3)))
            act.wait_ge(mix_lo, NC * KT)
            for j, w in enumerate(("g0", "u0")):
                cast(guH[:, 0, j].rearrange("p k n -> p (k n)"), *first(1, w))
            act.wait_ge(w_x, 6 + 24)
            norm(2)
            with act.Fori(0, NG - 1) as i:
                ffn_act(1, i, False)
            ffn_act(1, NG - 1, True)
            act.wait_ge(ffn[1]["x"], 3 + NG * 24)
            norm(3)

        @blk.vector
        def _(dve):
            chain = [0]

            def link(ins):
                chain[0] += 1
                ins.then_inc(step, 1)
                dve.wait_ge(step, chain[0])

            def lo(dst, slot, n, hi, count):
                dve.wait_ge(w_hi, count)
                dve.tensor_tensor(dst, raw[:, slot], hi.bitcast(F32), ALU.subtract).then_inc(raw_used[slot], 1)

            def flat(w):
                return w.rearrange("p k n -> p (k n)")

            for s in range(SLOTS):
                dve.sem_inc(raw_used[s], 1)
            for z in range(2):
                dve.sem_inc(ffn[z]["prod"], 2)
                dve.sem_inc(ffn[z]["x"], 3)
                dve.sem_inc(ffn[z]["hidlo"], 2)
            dve.sem_inc(t_lo, 1)
            dve.sem_inc(o_done, 2)
            dve.sem_inc(mx_ready, 1)
            dve.sem_inc(w_x, 6)
            dve.memset(ones[:], 1.0 / D).then_inc(cons, 1)
            dve.memset(eps[:], EPS).then_inc(cons, 1)
            dve.memset(cs[:], 0.0).then_inc(cons, 1)
            dve.wait_ge(smalls, N_SMALL)
            g0, g1 = glam[:, 0], glam[:, 1]
            lt = hout[:].rearrange("p a b -> p (a b)")
            link(dve.tensor_scalar(lt, g0, -1.0, 0.0, ALU.mult, ALU.max))
            link(dve.tensor_scalar(g1, g0, -1.0, None, ALU.mult))
            link(dve.tensor_tensor(g1, g0, g1, ALU.min))
            dve.tensor_copy(lnorm[:, 0:8], g1).then_inc(rl_in, 1)
            dve.wait_ge(rl_exp, 1)
            y, q, r = lnorm[:, 8:16], lnorm[:, 16:24], lnorm[:, 24:32]
            link(dve.tensor_scalar(q, y, 2.0, None, ALU.add))
            link(dve.reciprocal(q, q))
            link(dve.tensor_tensor(y, y, q, ALU.mult))
            link(dve.tensor_tensor(q, y, y, ALU.mult))
            link(dve.memset(r, 1.0 / 17))
            for n in range(15, 0, -2):
                link(dve.tensor_tensor(r, r, q, ALU.mult))
                link(dve.tensor_scalar(r, r, 1.0 / n, None, ALU.add))
            link(dve.tensor_tensor(r, r, y, ALU.mult))
            link(dve.scalar_tensor_tensor(r, r, 2.0, lt, ALU.mult, ALU.add))
            link(dve.tensor_scalar(g0, r, -8.0, None, ALU.mult))
            link(dve.tensor_scalar(g1, r, 8.0, None, ALU.mult))
            link(dve.tensor_scalar(subg[:], subg[:], 1.0 - LAM_INIT, None, ALU.mult))

            def mod_add(b):
                dve.wait_ge(mod_sum, b + 1)
                at = slice(4 * b, 4 * b + 4) if isinstance(b, int) else bass.ds(b * 4, 4)
                dve.tensor_tensor(mod[:, at], ps[:, 7, 0:8].rearrange("p (n c) -> p n c", c=2), bmod[:, at],
                                  ALU.add).then_inc(mod_done, 1)

            def scale_of(z):
                s = mod[:, (3 * z + 1) * KT:(3 * z + 2) * KT]
                link(dve.scalar_tensor_tensor(s, s, 1.0, ng[:, z], ALU.add, ALU.mult))

            def gate_of(z):
                s = mod[:, (3 * z + 2) * KT:(3 * z + 3) * KT]
                link(dve.tensor_scalar(s, s, 0.5, None, ALU.mult))

            def apply(z, c):
                s = nrm[z]
                dve.wait_ge(s["sd"], c + 1)
                link(dve.reciprocal(rstd[:], rstd[:]))

                def lo_part(k):
                    dve.wait_ge(s["hi"], c * KT + k + 1)
                    dve.tensor_tensor(hL[:, k, chunk(c)], tmp[:, 2 + k % 2], hH[:, k, chunk(c)].bitcast(F32),
                                      ALU.subtract).then_inc(s["h"], 1)

                for k in range(KT):
                    t = tmp[:, 2 + k % 2]
                    if c * KT + k >= 2:
                        dve.wait_ge(s["h"], c * KT + k - 1)
                    link(dve.tensor_tensor(t, x[:, k, chunk(c)], rstd[:], ALU.mult))
                    for cond, b, e in conds(c):
                        m = dve.tensor_scalar(tmp[:, 2 + k % 2, b - c * CH:e - c * CH], tmp[:, 2 + k % 2, b - c * CH:e - c * CH],
                                              mod[:, (3 * z + 1) * KT + k, cond:cond + 1],
                                              mod[:, 3 * z * KT + k, cond:cond + 1], ALU.mult, ALU.add)
                    m.then_inc(s["hf"], 1)
                    if k:
                        lo_part(k - 1)
                lo_part(KT - 1)
                if c == NC - 1:
                    dve.wait_ge(s["h"], NC * KT)

            for b in range(4):
                mod_add(b)
            dve.wait_ge(mod_done, 4)
            scale_of(0)
            for k in range(KT):
                dve.wait_ge(xin[k], 16)
            apply(0, 0)
            for b in range(4, PRE):
                mod_add(b)
            dve.wait_ge(mod_done, PRE)
            gate_of(0)
            for j, w in enumerate(("g0", "u0")):
                slot, n = first(0, w)
                lo(flat(guL[:, 0, j]), slot, n, flat(guH[:, 0, j]), j + 1)
            apply(0, 1)
            apply(0, 2)

            def ffn_dve(z, i, last, w0):
                s = ffn[z]
                gate = (3 * 2 * z + 2) * KT

                def hidden(f, c):
                    o = i * 6 + (f * NC + c)
                    b = (f * NC + c) % 2
                    dve.wait_ge(s["silu"], o + 3)
                    dve.wait_ge(s["hidlo"], o + 1)
                    dve.wait_ge(s["u"], o + 7)
                    dve.tensor_tensor(tmp[:, 2 + b], ps[:, 2 + b, 0:CH], tmp[:, b], ALU.mult).then_inc(s["prod"], 1)
                    dve.wait_ge(s["hidhi"], o + 1)
                    dve.tensor_tensor(hidL[:, f, chunk(c)], tmp[:, 2 + b], hidH[:, f, chunk(c)].bitcast(F32),
                                      ALU.subtract).then_inc(s["hidlo"], 1)

                def weights(dst_lo, dst_hi, item, j):
                    slot, n = nth(z, item, i)
                    lo(dst_lo, slot, n, dst_hi, i * 6 + (w0 + j))

                def add(c):
                    for t in range(KT):
                        dve.wait_ge(s["d"], i * 24 + (c * KT + t + 25))
                        for cond, b, e in conds(c):
                            m = dve.scalar_tensor_tensor(x[:, t, b:e], ps[:, 4 + (c * KT + t) % 3, b - c * CH:e - c * CH],
                                                         mod[:, gate + t, cond:cond + 1], x[:, t, b:e],
                                                         ALU.mult, ALU.add)
                        m.then_inc(s["x"], 1)

                for j, w in enumerate("gu"):
                    weights(flat(guL[:, 1, j]), flat(guH[:, 1, j]), w + "1", j + 1)
                hidden(0, 0)
                if z == 0:
                    mod_add(i + PRE)
                for j in range(2):
                    weights(dnL[:, j], dnH[:, j], f"d{j}", j + 3)
                hidden(0, 1)
                hidden(0, 2)
                if not last:
                    for j, w in enumerate("gu"):
                        weights(flat(guL[:, 0, j]), flat(guH[:, 0, j]), w + "0", j + 5)
                for c in range(NC):
                    hidden(1, c)
                dve.wait_ge(s["x"], i * 24 + 3)
                add(0)
                add(1)
                add(2)

            with dve.Fori(0, NG - 1) as i:
                ffn_dve(0, i, False, 2)
            ffn_dve(0, NG - 1, True, 2)
            whi_in = 2 + 6 * NG - 2
            dve.wait_ge(mod_done, NB_MOD)
            scale_of(1)
            scale_of(2)
            gate_of(2)
            for e in range(2):
                lo(wiL[:, e], e, None, wiH[:, e], whi_in + e + 1)
            dve.wait_ge(ffn[0]["x"], 3 + NG * 24)
            for c in range(NC):
                apply(1, c)

            with dve.Fori(0, 2) as i:
                for f in range(2):
                    lo(wiL[:, f], f, None, wiH[:, f], i * 2 + (whi_in + 3 + f))
            dve.wait_ge(spilled, 16 * KT)
            for j in range(RGT):
                e = j + 4
                dve.wait_ge(m_ev, 6 + 3 * (j + 1))
                link(dve.tensor_scalar(x[:, 0], xr[:, j], convw[:, j, 2:3], convb[:, j:j + 1], ALU.mult, ALU.add))
                for tap, off in ((0, -2), (1, -1), (3, 1)):
                    for b, end in ((0, CTX), (CTX, T)):
                        lo_t, hi_t = max(b, b - off), min(end, end - off)
                        link(dve.scalar_tensor_tensor(x[:, 0, lo_t:hi_t], xr[:, j, lo_t + off:hi_t + off],
                                                      convw[:, j, tap:tap + 1], x[:, 0, lo_t:hi_t], ALU.mult, ALU.add))
                dve.sem_inc(xc_ready, 1)
                if e < 6:
                    lo(wiL[:, e % 2], e % 2, None, wiH[:, e % 2], whi_in + e + 3)
                else:
                    lo(wiL[:, e - 6], e - 4, None, wiH[:, e - 6], whi_in + e + 3)
                dve.wait_ge(gate_ev, 12 * j + 12)
                for d in range(2):
                    link(dve.tensor_tensor(x[:, 2 + 2 * d], x[:, 2 + 2 * d], x[:, 0], ALU.mult))
                for d in range(2):
                    dve.wait_ge(rg_e, 2 * j + d + 1)
                    link(dve.tensor_tensor(x[:, 7], x[:, 5 + d], x[:, 5 + d], ALU.mult))
                    dve.scalar_tensor_tensor(x[:, 1 + 2 * d], x[:, 7], 1.0, x[:, 1 + 2 * d], ALU.add,
                                             ALU.mult).then_inc(rg_m, 1)
                    dve.wait_ge(rg_m, 2 * j + d + 1)
                for d in range(2):
                    dve.wait_ge(rg_s, 2 * j + d + 1)
                    bx, r = x[:, 2 + 2 * d], x[:, 1 + 2 * d]
                    link(dve.tensor_tensor(bx, r, bx, ALU.mult))
                    for b, end, init in ((0, CTX, 0.0), (CTX, T, h0[:, j, d:d + 1])):
                        s = slice(b, end) if d == 0 else slice(end - 1, b - 1 if b else None, -1)
                        link(dve.tensor_tensor_scan(x[:, 1 + 2 * d, s], x[:, 5 + d, s], x[:, 2 + 2 * d, s], init,
                                                    ALU.mult, ALU.add))
                    last_t = CTX - 1 if d == 0 else 0
                    link(dve.tensor_copy(hout[:, j, d:d + 1], x[:, 1 + 2 * d, last_t:last_t + 1]))
                link(dve.tensor_tensor(x[:, 1], x[:, 1], x[:, 3], ALU.add))
                dve.wait_ge(m_ev, 6 + 3 * (e + 1))
                dve.tensor_tensor(xr[:, j], x[:, 1], xg[:, j], ALU.mult).then_inc(rg_y, 1)
            for hf in range(2):
                for t in range(9):
                    n = hf * 9 + t
                    dve.wait_ge(v_ready, n + 1)
                    dve.tensor_copy(v[:, t, hf * 256:(hf + 1) * 256], ps[:, n % 6, 0:256]).then_inc(v_ev, 1)
                for kk in range(2):
                    if hf == 0:
                        lo(wiL[:, kk], 2 + kk, None, wiH[:, kk], whi_in + 11 + kk)
                    else:
                        lo(wiL[:, kk], kk, None, wiH[:, kk], whi_in + 13 + kk)
            with dve.Fori(0, 3) as i:
                for f in range(2):
                    lo(wiL[:, f], f, None, wiH[:, f], i * 2 + (whi_in + 15 + f))

            dve.wait_ge(acst, N_ACST)
            for j in range(2):
                link(dve.tensor_tensor(dl[:, 2 * j], dl[:, 2 * j], dl[:, 2 * j + 1], ALU.mult))
                link(dve.tensor_reduce(lams[:, j:j + 1], dl[:, 2 * j], AX.X, ALU.add))
            dve.sem_inc(lam_p, 1)
            dve.wait_ge(lam_e, 1)
            link(dve.tensor_tensor(nlam[:], lams[:, 3:4], lams[:, 2:3], ALU.subtract))
            link(dve.tensor_scalar(nlam[:], nlam[:], -LAM_INIT, None, ALU.add))
            chain0 = chain[0]
            STEPS = 44
            swap = [(p + 16) % 32 for p in range(32)]
            dve.wait_ge(m_ev, 6 + 48)
            with dve.Fori(0, NH) as hd:
                k_in = [0]

                def hlink(ins):
                    k_in[0] += 1
                    ins.then_inc(step, 1)
                    dve.wait_ge(step, hd * STEPS + (chain0 + k_in[0]))

                for j in range(2):
                    dve.wait_ge(pp_c, hd * 2 + (j + 1))
                    alone(dve)
                    hlink(dve.stream_shuffle(pr[:, 1, j, 0:LAT], pr[:, 0, j, 0:LAT], swap))
                    hlink(dve.tensor_tensor(pr[:, 0, j, 0:LAT], pr[:, 0, j, 0:LAT], cosT[:], ALU.mult))
                    hlink(dve.tensor_tensor(pr[:, 1, j, 0:LAT], pr[:, 1, j, 0:LAT], sinT[:], ALU.mult))
                    dve.tensor_tensor(pr[:, 0, j, 0:LAT], pr[:, 0, j, 0:LAT], pr[:, 1, j, 0:LAT],
                                      ALU.add).then_inc(pp_f, 1)
                dve.wait_ge(pp_f, hd * 2 + 2)
                at = bass.ds(hd * P, P)
                for j, (dst, src, hi) in enumerate((
                        (vHL[:, 0:9, 1], v[:, :, at], vHL[:, 0:9, 0]), (vHL[:, 9, 1], vc[:, at], vHL[:, 9, 0]),
                        (kL[:, 0:CTX], x[:, hd + 4, 0:CTX], kH[:, 0:CTX]), (kL[:, T:KEYS], kc[:, hd], kH[:, T:KEYS]),
                        (qL[:, 0:CTX], x[:, hd, 0:CTX], qH[:, 0:CTX]),
                        (kL[:, CTX:T], pr[:, 0, 0, 0:LAT], kH[:, CTX:T]), (qL[:, CTX:T], pr[:, 0, 1, 0:LAT], qH[:, CTX:T]))):
                    dve.wait_ge(pp_hi, hd * 7 + (j + 1))
                    dve.tensor_tensor(dst, src, hi.bitcast(F32), ALU.subtract).then_inc(pp_lo, 1)
                for n in range(10):
                    if n > 0:
                        t = n - 1
                        w = CTX if t == 0 else T
                        dve.wait_ge(e_done, hd * 18 + (2 * t + 2))
                        dve.wait_ge(o_done, hd * 9 + (t + 1))
                        hlink(dve.reciprocal(rec[:, t % 2], sums[:, t % 2]))
                        hlink(dve.scalar_tensor_tensor(coef[:, t % 2:t % 2 + 1], sums[:, t % 2, 0:1], nlam[:, 0:1],
                                                       rec[:, t % 2, 1:2], ALU.mult, ALU.mult))
                        dve.scalar_tensor_tensor(pr[:, t % 2, 0, 0:w], pr[:, t % 2, 1, 0:w], coef[:, t % 2:t % 2 + 1],
                                                 pr[:, t % 2, 0, 0:w], ALU.mult, ALU.add).then_inc(pd_ready, 1)
                    if n < 9:
                        dve.wait_ge(mx_ready, hd * 9 + (n + 1))
                        for m in range(2):
                            dve.wait_ge(s_ready, hd * 18 + (2 * n + m + 1))
                            src = ps[:, 3 * m, 0:CTX] if n == 0 else ps[:, 3 * m:3 * m + 3, 0:CH]
                            ax = AX.X if n == 0 else AX.XY
                            hlink(dve.tensor_reduce(mx[:, n % 2, m:m + 1], src, ax, ALU.max))
                        dve.tensor_scalar(nmx[:, n % 2], mx[:, n % 2], -DH ** -0.5, None, ALU.mult).then_inc(mx_ready, 1)
                    if n == 0:
                        continue
                    nk = 1 if t == 0 else 9
                    g0_ = 0 if t == 0 else 1 + 3 * (t - 1)
                    for g in range(1 if t == 0 else 3):
                        dve.wait_ge(t_hi, hd * 25 + (g0_ + g + 1))
                        w = min(3, nk - 3 * g)
                        at_k = slice(3 * g, 3 * g + w)
                        dve.tensor_tensor(flat(pTL[:, t % 2, at_k]), ps[:, 6, 0:w * P],
                                          flat(pTH[:, t % 2, at_k]).bitcast(F32), ALU.subtract).then_inc(t_lo, 1)
                    o = tmp[:, t // 3, (t % 3) * P:(t % 3 + 1) * P]
                    dve.wait_ge(o_half, hd * 9 + (t + 1))
                    dve.scalar_tensor_tensor(o, ps[:, 7, P:2 * P], rec[:, t % 2, 0:1], o, ALU.mult,
                                             ALU.add).then_inc(o_done, 1)
                dve.wait_ge(o_done, hd * 9 + 11)
                hlink(dve.tensor_tensor(rot[:], o9, o9, ALU.mult))
                dve.tensor_reduce(ss[:, 0:9], rot[:].rearrange("p (t n) -> p t n", t=9), AX.X, ALU.add).then_inc(o_ss, 1)
                dve.wait_ge(o_sd, hd + 1)
                hlink(dve.reciprocal(ss[:, 0:9], ss[:, 0:9]))
                for t in range(9):
                    o = tmp[:, t // 3, (t % 3) * P:(t % 3 + 1) * P]
                    m = dve.tensor_scalar(o, o, ss[:, t:t + 1], None, ALU.mult)
                m.then_inc(o_nrm, 1)
                assert k_in[0] == STEPS
            chain[0] += NH * STEPS

            dve.wait_ge(ot_done, 1 + 12)
            for k in range(KT):
                src = x[:, k] if k < 4 else xr[:, k - 4]
                for c in range(NC):
                    dve.wait_ge(mix_hi, k * NC + c + 1)
                    dve.tensor_tensor(hL[:, k, chunk(c)], src[:, chunk(c)], hH[:, k, chunk(c)].bitcast(F32),
                                      ALU.subtract).then_inc(mix_lo, 1)
            whi_wo = whi_in + 20
            for e in range(2):
                lo(wiL[:, e], e, None, wiH[:, e], whi_wo + e + 1)

            def w_add(i, f):
                for c in range(NC):
                    dve.wait_ge(w_ready, i * 6 + (f * NC + c + 1))
                    for cond, b, e in conds(c):
                        xt = x[:, i * 2 + f, b:e]
                        m = dve.scalar_tensor_tensor(xt, ps[:, f * NC + c, b - c * CH:e - c * CH],
                                                     mod[:, i * 2 + (5 * KT + f), cond:cond + 1], xt, ALU.mult, ALU.add)
                    m.then_inc(w_x, 1)

            dve.wait_ge(xback, 16 * KT)
            with dve.Fori(0, 3) as i:
                for f in range(2):
                    w_add(i, f)
                    lo(wiL[:, f], f, None, wiH[:, f], i * 2 + (whi_wo + 3 + f))
            for f in range(2):
                w_add(3, f)
            whi_f2 = whi_wo + 8
            for j, w in enumerate(("g0", "u0")):
                slot, n = first(1, w)
                lo(flat(guL[:, 0, j]), slot, n, flat(guH[:, 0, j]), whi_f2 + j + 1)
            dve.wait_ge(w_x, 6 + 24)
            for c in range(NC):
                apply(2, c)
            with dve.Fori(0, NG - 1) as i:
                ffn_dve(1, i, False, whi_f2 + 2)
            ffn_dve(1, NG - 1, True, whi_f2 + 2)
            dve.wait_ge(ffn[1]["x"], 3 + NG * 24)
            for c in range(NC):
                dve.wait_ge(nrm[3]["sd"], c + 1)
                link(dve.reciprocal(rstd[:], rstd[:]))
                for k in range(KT):
                    xt = x[:, k, chunk(c)]
                    dve.scalar_tensor_tensor(xt, xt, fg[:, k:k + 1], rstd[:], ALU.mult, ALU.mult).then_inc(y_done, 1)
                dve.wait_ge(y_done, (c + 1) * KT)
                dve.sem_inc(nrm[3]["h"], KT)
    return nc


def program(nc, shapes):
    a = {name: nc.dram_tensor("in_" + name, list(shape), F32, kind="ExternalInput").ap() for name, shape in shapes.items()}
    out = {name: nc.dram_tensor("out_" + name, list(shape), F32, kind="ExternalOutput").ap()
           for name, shape in (("y", (KT, P, T)), ("k", (NH, P, P)), ("v", (P, 512)), ("h", (P, RGT, 2)))}
    return build(nc, a, out)


def rope_tables():
    n = DH // 4
    inv = (np.float32(10000.0) ** (-np.arange(n, dtype=np.float32) / np.float32(n))).astype(np.float32)
    tok = np.arange(LAT)
    pos = np.stack([tok // GRID_W, tok % GRID_W]).astype(np.float32)
    p = np.arange(P)
    ang = pos[(p % DH) // (DH // 2)] * inv[p % n][:, None]
    sign = np.where(p % (2 * n) < n, -1.0, 1.0).astype(np.float32)[:, None]
    return np.cos(ang).astype(np.float32), (np.sin(ang) * sign).astype(np.float32)


def kernel(x_prompt, x_sample, cache_attn_k, cache_attn_v, state_rglru, c, c_ctx, norm_g, w_mod, b_mod,
           ffn_w_gate, ffn_w_up, ffn_w_down, w_in, w_out, diff_lambda, subln_g, conv_w, conv_b,
           rg_w_r, rg_b_r, rg_w_i, rg_b_i, rg_lambda, final_g):
    import concourse.bacc as bacc
    from concourse.bass_utils import run_bass_kernel_spmd

    def cols(w, n):
        r, m = w.shape
        return w.reshape(r // P, P, m // n, n).transpose(2, 1, 0, 3)

    cos, sin = rope_tables()
    sel = np.zeros((P, 2), np.float32)
    for q in range(4):
        sel[32 * q, 0] = sel[32 * q + 1, 1] = 1.0
    w3 = np.asarray(w_in)[0]
    q_, k_, v_, xr_, xg_ = (w3[:, 512 * n:512 * (n + 1)] for n in range(5))
    bmod = np.asarray(b_mod)[0].reshape(9 * KT, P).T
    ngt = np.asarray(norm_g)[0].reshape(3, KT, P).transpose(2, 0, 1)
    gwt = np.stack([np.asarray(rg_w_r)[0], np.asarray(rg_w_i)[0]])
    ffn_cols = lambda w: np.concatenate([cols(np.asarray(w)[0, z], P) for z in range(2)]).reshape(2 * FT, P, D)
    arrays = {
        "x": np.concatenate([np.asarray(x_prompt)[0], np.asarray(x_sample)[0]]).T.reshape(KT, P, T),
        "c": np.stack([np.asarray(c_ctx), np.asarray(c)[0]]).reshape(2, KT, P).transpose(2, 1, 0),
        "w_mod": cols(np.asarray(w_mod)[0], 512).reshape(NB_MOD, P, 4, 1024).transpose(0, 2, 1, 3),
        "bmod": np.stack([bmod, bmod], axis=2),
        "ng": np.stack([ngt, ngt], axis=3),
        "fg": np.asarray(final_g).reshape(KT, P).T,
        "w_gate": ffn_cols(ffn_w_gate),
        "w_up": ffn_cols(ffn_w_up),
        "w_down": np.asarray(ffn_w_down)[0].reshape(2 * FT, P, D),
        "w_in": cols(np.concatenate([xr_, xg_, q_, k_], axis=1), P).reshape(16, P, D),
        "w_v": cols(v_, 256).reshape(2, P, 2, 1024).transpose(0, 2, 1, 3).reshape(4, P, 1024),
        "w_out": cols(np.asarray(w_out)[0], P).reshape(KT, P, D),
        "kc": np.asarray(cache_attn_k)[0, 0].transpose(1, 2, 0),
        "vc": np.asarray(cache_attn_v)[0, 0].reshape(P, NH * P),
        "h0": np.asarray(state_rglru)[0, 0].reshape(2, RGT, P).transpose(2, 1, 0),
        "dl": np.asarray(diff_lambda)[0].reshape(4 * DH),
        "subg": np.asarray(subln_g)[0].reshape(P, 1),
        "convw": np.asarray(conv_w)[0].reshape(4, RGT, P).transpose(2, 1, 0),
        "convb": np.asarray(conv_b)[0].reshape(RGT, P).T,
        "gw": gwt.reshape(2, 2, RGT, 2, DH, DH).transpose(3, 4, 2, 1, 0, 5).reshape(P, 1024),
        "gbias": np.stack([np.asarray(rg_b_r)[0], np.asarray(rg_b_i)[0]]).reshape(2, 2, RGT, P).transpose(3, 2, 1, 0),
        "glam": np.asarray(rg_lambda)[0].reshape(2, RGT, P).transpose(2, 1, 0).reshape(P, 2 * RGT),
        "cos": cos,
        "sin": sin,
        "sel": sel,
        "ident": np.eye(P, dtype=np.float32),
    }
    arrays = {name: np.ascontiguousarray(v) for name, v in arrays.items()}
    nc = bacc.Bacc("TRN2", target_bir_lowering=False, num_devices=1)
    program(nc, {name: v.shape for name, v in arrays.items()})
    got = run_bass_kernel_spmd(nc, [{"in_" + name: v for name, v in arrays.items()}], core_ids=[0]).results[0]
    y = got["out_y"].reshape(D, T).T
    return (np.ascontiguousarray(y[:CTX])[None], np.ascontiguousarray(y[CTX:])[None],
            np.ascontiguousarray(got["out_k"].transpose(2, 0, 1))[None, None],
            got["out_v"].reshape(1, 1, P, NH, P),
            np.ascontiguousarray(got["out_h"].transpose(2, 1, 0)).reshape(1, 1, 2, RGT * P))
```

```python
import math
from contextlib import ExitStack

import numpy as np

import concourse.bass as bass
from concourse import mybir

F32 = mybir.dt.float32
F32R = mybir.dt.float32r
ACT = mybir.ActivationFunctionType
ALU = mybir.AluOpType
AX = mybir.AxisListType

P = 128
D = 1024
KT = D // P
CTX = 128
LAT = 1024
T = CTX + LAT
CH = 384
NC = T // CH
FF = 2816
FT = FF // P
NG = FT // 2
NH = 4
DH = 64
RGT = 4
NB_MOD = 18
PRE = NB_MOD - NG
SLOTS = 5
EPS = 1e-6
KEY_TILES = [1] + [9] * 8
GROUP0 = [0] + [1 + 3 * t for t in range(9)]
GROUPS = GROUP0[9]
MIX_ORDER = (4, 5, 6, 7, 0, 1, 2, 3)
LAM_INIT = 0.8 - 0.6 * math.exp(0.0)
KEYS = T + 128
GRID_W = 64


XC = (0, 7)


def chunk(c):
    return slice(c * CH, (c + 1) * CH)


def conds(c):
    if c == 0:
        return [(0, 0, CTX), (1, CTX, CH)]
    return [(1, c * CH, (c + 1) * CH)]


def build(nc, a, out):
    ctx = ExitStack()
    with ctx:
        def sem(name):
            return ctx.enter_context(nc.semaphore(name))

        def sb(name, shape, dt=F32, stack=ctx):
            return stack.enter_context(nc.sbuf_tensor("sb_" + name, shape, dt))

        ones = sb("ones", [P, P])
        mod = sb("mod", [P, 9 * KT, 2])
        bmod = sb("bmod", [P, 9 * KT, 2])
        ng = sb("ng", [P, 3, KT, 2])
        fg = sb("fg", [P, KT])
        eps = sb("eps", [P, 1])
        convw = sb("convw", [P, RGT, 4])
        convb = sb("convb", [P, RGT])
        gbias = sb("gbias", [P, RGT, 2, 2])
        glam = sb("glam", [P, 2, RGT * 2])
        h0 = sb("h0", [P, RGT, 2])
        subg = sb("subg", [P, 1])
        hout = sb("hout", [P, RGT, 2])
        lnorm = sb("lnorm", [P, 32])
        raw = sb("raw", [P, SLOTS, 1024])
        x = sb("x", [P, KT, T])
        tmp = sb("tmp", [P, 4, CH])
        rstd = sb("rstd", [P, CH])
        acts = ExitStack()
        with ExitStack() as s:
            stage = [sb(f"stage{b}", [P, 4, 1024], F32, s) for b in range(4)]
        hH = sb("hH", [P, KT, T], F32R, acts)
        hL = sb("hL", [P, KT, T], F32R, acts)
        with ExitStack() as s:
            stage.append(sb("stage4", [P, 4, 1024], F32, s))
            sb("first_gu", [P, 2, 2, 1024], F32, s)
            stage += [sb(f"stage{b}", [P, 4, 1024], F32, s) for b in (5, 6)]
        with ExitStack() as s:
            guH, guL = [None, None], [None, None]
            for f in (1, 0):
                guH[f] = sb(f"guH{f}", [P, 2, KT, P], F32R, s)
                guL[f] = sb(f"guL{f}", [P, 2, KT, P], F32R, s)
            dnH = sb("dnH", [P, 2, D], F32R, s)
            dnL = sb("dnL", [P, 2, D], F32R, s)
            hidH = sb("hidH", [P, 2, T], F32R, s)
            hidL = sb("hidL", [P, 2, T], F32R, s)
            modp = sb("modp", [P, 512], F32, s)
            cs = sb("cs", [P, KT, 32], F32, s)
            cin = sb("cin", [P, KT, 2], F32, s)
            sel = sb("sel", [P, 2], F32, s)
        mid = ExitStack()
        wiH = sb("wiH", [P, 2, 1024], F32R, mid)
        wiL = sb("wiL", [P, 2, 1024], F32R, mid)
        v = sb("v", [P, T // P, 512], F32, mid)
        xr = sb("xr", [P, RGT, T], F32, mid)
        with ExitStack() as s:
            xg = sb("xg", [P, RGT, T], F32, s)
        with ExitStack() as s:
            cosT = sb("cosT", [P, LAT], F32, s)
            sinT = sb("sinT", [P, LAT], F32, s)
            swp = sb("swp", [P, LAT], F32, s)
            vc = sb("vc", [P, 512], F32, s)
            kc = sb("kc", [P, NH, P], F32, s)
            ident = sb("ident", [P, P], F32, s)
            dl = sb("dl", [P, 4, DH], F32, s)
            mx = sb("mx", [P, 2, 2], F32, s)
            nmx = sb("nmx", [P, 2, 2], F32, s)
            sums = sb("sums", [P, 3, 2], F32, s)
            rec = sb("rec", [P, 3, 2], F32, s)
            coef = sb("coef", [P, 3], F32, s)
            ss = sb("ss", [P, NH, 9], F32, s)
            lams = sb("lams", [P, 4], F32, s)
            nlam = sb("nlam", [P, 1], F32, s)
        mid.close()
        acts.close()
        with ExitStack() as s:
            qH = sb("qH", [P, T], F32R, s)
            qL = sb("qL", [P, T], F32R, s)
            kH = sb("kH", [P, KEYS], F32R, s)
            kL = sb("kL", [P, KEYS], F32R, s)
            vHL = sb("vHL", [P, KEYS // P, 2, P], F32R, s)
            pr = sb("pr", [P, 2, 2, T], F32, s)
            pTH = sb("pTH", [P, 2, 9, P], F32R, s)
            pTL = sb("pTL", [P, 2, 9, P], F32R, s)
        xd = nc.dram_tensor("x_spilled", [KT, P, T], F32, kind="Internal").ap()
        ps = ctx.enter_context(nc.psum_tensor("ps", [P, 8, 512], F32))

        smalls = sem("smalls")
        cons = sem("cons")
        xin = [sem(f"xin{k}") for k in range(KT)]
        staged = [sem(f"staged{b}") for b in range(PRE)]
        raw_full = [sem(f"raw_full{s}") for s in range(SLOTS)]
        raw_used = [sem(f"raw_used{s}") for s in range(SLOTS)]
        rl_in = sem("rl_in")
        rl_exp = sem("rl_exp")
        c_ready = sem("c_ready")
        mod_prod = sem("mod_prod")
        mod_copy = sem("mod_copy")
        mod_sum = sem("mod_sum")
        mod_done = sem("mod_done")
        step = sem("step")
        nrm = [{n: sem(f"{n}_{z}") for n in
                ("sq",
                 "sq_used",
                 "sd",
                 "hf",
                 "hi", "h")}
               for z in range(4)]
        ffn = [{n: sem(f"{n}_{z}") for n in
                ("g", "u",
                 "silu",
                 "prod",
                 "hidhi", "hidlo",
                 "d",
                 "x")}
               for z in range(2)]
        w_hi = sem("w_hi")
        spilled = sem("spilled")
        gw_in = sem("gw_in")
        m_ready = sem("m_ready")
        m_ev = sem("m_ev")
        v_ready = sem("v_ready")
        v_ev = sem("v_ev")
        xc_ready = sem("xc_ready")
        gate_ready = sem("gate_ready")
        gate_ev = sem("gate_ev")
        rg_a = sem("rg_a")
        rg_e = sem("rg_e")
        rg_m = sem("rg_m")
        rg_s = sem("rg_s")
        rg_y = sem("rg_y")
        gelu = sem("gelu")
        rg_out = sem("rg_out")
        acst = sem("acst")
        outs = sem("outs")
        lam_p = sem("lam_p")
        lam_e = sem("lam_e")
        roped = sem("roped")
        pp_hi = sem("pp_hi")
        pp_lo = sem("pp_lo")
        s_ready = sem("s_ready")
        mx_ready = sem("mx_ready")
        e_done = sem("e_done")
        pd_ready = sem("pd_ready")
        t_ready = sem("t_ready")
        t_hi = sem("t_hi")
        t_lo = sem("t_lo")
        o_ready = sem("o_ready")
        o_half = sem("o_half")
        o_done = sem("o_done")
        o_ss = sem("o_ss")
        o_sd = sem("o_sd")
        o_nrm = sem("o_nrm")
        ot_ready = sem("ot_ready")
        mix_hi = sem("mix_hi")
        mix_lo = sem("mix_lo")
        xback = sem("xback")
        w_ready = sem("w_ready")
        w_x = sem("w_x")
        y_done = sem("y_done")
        passed = [sem(f'passed{e}') for e in range(2)]
        y_out = sem("y_out")

        gw = tmp[:].rearrange("p a b -> p (a b)")[:, 0:1024]
        SMALLS = ((cin[:], "c"), (bmod[:], "bmod"), (ng[:], "ng"), (fg[:], "fg"), (convw[:], "convw"),
                  (convb[:], "convb"), (gbias[:], "gbias"), (glam[:, 0], "glam"), (h0[:], "h0"),
                  (subg[:], "subg"), (sel[:], "sel"))
        N_SMALL = 16 * len(SMALLS)
        N_ACST = 16 * 6
        FIRST = {"g0": 3, "u0": 4}
        F1 = {"m0": (0, 0), "m1": (1, 0), "m2": (2, 0), "m3": (3, 0), "g1": (4, 0),
              "u1": (0, 1), "d0": (1, 1), "d1": (2, 1), "g0": (3, 1), "u0": (4, 1)}
        F2 = {"g1": (0, 0), "u1": (1, 0), "d0": (2, 0), "d1": (0, 1), "g0": (1, 1), "u0": (2, 1)}
        used_f1 = [0, 0, 0, 1, 1]
        used_in = [2 * NG, 2 * NG, 2 * NG, 2 * NG, 2 * NG]
        used_wo = [used_in[0] + 8, used_in[1] + 8, used_in[2] + 2, used_in[3] + 2, used_in[4]]
        used_f2 = [used_wo[0] + 4, used_wo[1] + 4, used_wo[2]]

        def nth(z, item, i):
            slot, j = (F1, F2)[z][item]
            base = used_f1[slot] if z == 0 else used_f2[slot] + (slot > 0)
            return slot, i * 2 + (base + j)

        def stats_bank(z, c):
            return 4 + c if z == 0 else 7

        def first(z, item):
            if z == 0:
                return FIRST[item], 0
            slot = {"g0": 1, "u0": 2}[item]
            return slot, used_f2[slot]

        blk = ctx.enter_context(nc.Block())


        def alone(eng):
            eng.sem_inc(passed[eng is nc.vector], 1)

        @blk.sync
        def _(sp):
            def load_raw(slot, n, src):
                sp.wait_ge(raw_used[slot], n + 1)
                sp.dma_start(raw[:, slot], src).then_inc(raw_full[slot], 16)

            def ffn_loads(z, i, last):
                if z == 0:
                    for q in range(4):
                        load_raw(*nth(z, f"m{q}", i), a["w_mod"][i + PRE, q])
                load_raw(*nth(z, "g1", i), a["w_gate"][i * 2 + (z * FT + 1)])
                load_raw(*nth(z, "u1", i), a["w_up"][i * 2 + (z * FT + 1)])
                load_raw(*nth(z, "d0", i), a["w_down"][i * 2 + z * FT])
                load_raw(*nth(z, "d1", i), a["w_down"][i * 2 + (z * FT + 1)])
                if not last:
                    load_raw(*nth(z, "g0", i), a["w_gate"][i * 2 + (z * FT + 2)])
                    load_raw(*nth(z, "u0", i), a["w_up"][i * 2 + (z * FT + 2)])

            for dst, name in SMALLS:
                sp.dma_start(dst, a[name]).then_inc(smalls, 16)
            for k in range(KT):
                sp.dma_start(x[:, k], a["x"][k]).then_inc(xin[k], 16)
            for b in range(PRE):
                if b == 4:
                    load_raw(*first(0, "g0"), a["w_gate"][0])
                    load_raw(*first(0, "u0"), a["w_up"][0])
                sp.dma_start(stage[b][:], a["w_mod"][b].rearrange("q p n -> p q n")).then_inc(staged[b], 16)
            with sp.Fori(0, NG - 1) as i:
                ffn_loads(0, i, False)
            ffn_loads(0, NG - 1, True)
            load_raw(0, used_in[0], a["w_in"][0])
            load_raw(1, used_in[1], a["w_in"][1])
            sp.wait_ge(ffn[0]["x"], 3 + NG * NC * KT)
            for k in range(KT):
                sp.dma_start(xd[k], x[:, k]).then_inc(spilled, 16)
            sp.wait_ge(nrm[1]["h"], NC * KT)
            sp.dma_start(gw, a["gw"]).then_inc(gw_in, 16)
            for e in range(2, 8):
                load_raw(e % 2, used_in[e % 2] + e // 2, a["w_in"][e])
            for n in range(4):
                load_raw(2 + n % 2, used_in[2 + n % 2] + n // 2, a["w_v"][n])
            load_raw(0, used_in[0] + 4, a["w_in"][8])
            load_raw(1, used_in[1] + 4, a["w_in"][9])
            sp.wait_ge(rg_out, RGT)
            sp.dma_start(out["h"], hout[:]).then_inc(outs, 16)
            for dst, name in ((cosT, "cos"), (sinT, "sin"), (vc, "vc"), (ident, "ident")):
                sp.dma_start(dst[:], a[name]).then_inc(acst, 16)
            sp.dma_start(kc[:], a["kc"].rearrange("h p t -> p h t")).then_inc(acst, 16)
            sp.dma_start(dl[:].rearrange("p a b -> p (a b)"), a["dl"].partition_broadcast(P)).then_inc(acst, 16)
            with sp.Fori(0, 3) as i:
                for f in range(2):
                    load_raw(f, i + (used_in[f] + 5), a["w_in"][i * 2 + (10 + f)])
            sp.wait_ge(v_ev, 18)
            sp.dma_start(out["v"], v[:, 0]).then_inc(outs, 16)
            sp.wait_ge(m_ev, 6 + 16 * NC)
            sp.dma_start(out["k"].rearrange("h p t -> p h t"), x[:, 4:8, 0:CTX]).then_inc(outs, 16)
            load_raw(0, used_wo[0], a["w_out"][0])
            load_raw(1, used_wo[1], a["w_out"][1])
            sp.wait_ge(outs, 48)
            sp.wait_ge(spilled, 16 * KT)
            sp.wait_ge(pp_lo, NH * 5)
            for k in range(KT):
                sp.dma_start(x[:, k], xd[k]).then_inc(xback, 16)
            with sp.Fori(0, 3) as i:
                for f in range(2):
                    load_raw(f, i + (used_wo[f] + 1), a["w_out"][i * 2 + (2 + f)])
            load_raw(*first(1, "g0"), a["w_gate"][FT])
            load_raw(*first(1, "u0"), a["w_up"][FT])
            with sp.Fori(0, NG - 1) as i:
                ffn_loads(1, i, False)
            ffn_loads(1, NG - 1, True)
            for c in range(NC):
                for k in range(KT):
                    sp.wait_ge(y_done, c * KT + k + 1)
                    sp.dma_start(out["y"][k, :, chunk(c)], x[:, k, chunk(c)]).then_inc(y_out, 16)
            sp.wait_ge(y_out, 16 * NC * KT)

        @blk.tensor
        def _(pe):
            for z in range(2):
                pe.sem_inc(ffn[z]["u"], 6)
                pe.sem_inc(ffn[z]["d"], 24)

            def three(o, wH, wL, xH, xL, begin, end):
                pe.matmul(o, wH, xH, start=begin, stop=False)
                pe.matmul(o, wH, xL, start=False, stop=False)
                return pe.matmul(o, wL, xH, start=False, stop=end)

            def stats(z, c, tiles=range(KT)):
                for k in tiles:
                    pe.wait_ge(nrm[z]["sq"], c * KT + k + 1)
                    if k == 0 and c > 0 and z > 0:
                        pe.wait_ge(nrm[z]["sd"], c)
                    pe.matmul(ps[:, stats_bank(z, c), 0:CH], ones[:], tmp[:, k % 2], start=k == 0,
                              stop=k == KT - 1).then_inc(nrm[z]["sq_used"], 1)

            def mod_partial(src, used):
                for kk in range(2):
                    for q in range(4):
                        m = pe.matmul(ps[32 * q:32 * q + 32, 7, :], cs[:, 2 * q + kk, :], src[:, q, kk * 512:(kk + 1) * 512],
                                      start=kk == 0, stop=kk == 1, tile_position=(0, 32 * q))
                        if kk == 1 and q == 3:
                            m.then_inc(mod_prod, 1)
                        elif kk == 1 and used:
                            m.then_inc(raw_used[q], 1)

            def mod_total():
                for n in range(4):
                    m = pe.matmul(ps[:, 7, 2 * n:2 * n + 2], modp[:, n * P:(n + 1) * P], sel[:], start=True, stop=True)
                m.then_inc(mod_sum, 1)

            def mod_block(b):
                if b < PRE:
                    pe.wait_ge(staged[b], 16)
                else:
                    mod_raw_full(b - PRE)
                if b:
                    pe.wait_ge(mod_done, b)
                mod_partial(stage[b] if b < PRE else raw, b >= PRE)
                pe.wait_ge(mod_copy, b + 1)
                mod_total()

            def mod_raw_full(i):
                for q in range(4):
                    slot, n = nth(0, f"m{q}", i)
                    pe.wait_ge(raw_full[slot], n * 16 + 16)

            pe.wait_ge(cons, 1)
            for c in range(NC):
                stats(0, c)
            pe.wait_ge(c_ready, 1)
            pe.wait_ge(smalls, N_SMALL)
            for b in range(4):
                mod_block(b)

            def ffn_pe(z, i, between=None):
                s = ffn[z]
                last = isinstance(i, int) and i == NG - 1
                with_mod = z == 0 and between is None
                if with_mod:
                    mod_raw_full(i)
                    pe.wait_ge(mod_done, i + PRE)
                    mod_partial(raw, True)
                for f in range(2):
                    for c in range(NC):
                        b = (f * NC + c) % 2
                        o = i * 6 + (f * NC + c)
                        if c == 0:
                            for w in "gu":
                                slot, n = nth(z, f"{w}{f}", i)
                                pe.wait_ge(raw_used[slot], n + 2 if f else n)
                        pe.wait_ge(nrm[2 * z]["h"], (c + 1) * KT)
                        pe.wait_ge(s["silu"], o + 1)
                        for k in range(KT):
                            m = three(ps[:, b, 0:CH], guH[f][:, 0, k], guL[f][:, 0, k], hH[:, k, chunk(c)],
                                      hL[:, k, chunk(c)], k == 0, k == KT - 1)
                        m.then_inc(s["g"], 1)
                        pe.wait_ge(s["prod"], o + 1)
                        for k in range(KT):
                            m = three(ps[:, 2 + b, 0:CH], guH[f][:, 1, k], guL[f][:, 1, k], hH[:, k, chunk(c)],
                                      hL[:, k, chunk(c)], k == 0, k == KT - 1)
                        m.then_inc(s["u"], 1)
                        if with_mod and f == 0 and c == 0:
                            pe.wait_ge(mod_copy, i + (PRE + 1))
                            mod_total()
                        if between is not None and f == 0:
                            between(c)
                for w in ("d0", "d1"):
                    slot, n = nth(z, w, i)
                    pe.wait_ge(raw_used[slot], n + 2)
                for c in range(NC):
                    pe.wait_ge(s["hidlo"], i * 6 + (6 + c))
                    for t in range(KT):
                        pe.wait_ge(s["x"], i * 24 + (c * KT + t + 1))
                        for f in range(2):
                            m = three(ps[:, 4 + (c * KT + t) % 3, 0:CH], dnH[:, f, t * P:(t + 1) * P],
                                      dnL[:, f, t * P:(t + 1) * P], hidH[:, f, chunk(c)], hidL[:, f, chunk(c)],
                                      f == 0, f == 1)
                        m.then_inc(s["d"], 1)
                        if last and c == 2:
                            stats(2 * z + 1, 1, (t,))
                    if last and c == 1:
                        if z == 0:
                            pe.wait_ge(mod_done, NB_MOD)
                        stats(2 * z + 1, 0)

            def first_mods(c):
                if c < 2:
                    mod_block(4 + 2 * c)
                    mod_block(5 + 2 * c)

            ffn_pe(0, 0, first_mods)
            with pe.Fori(1, NG - 1) as i:
                ffn_pe(0, i)
            ffn_pe(0, NG - 1)

            def in_chunk(e, c, o, slot_n):
                f = e % 2 if isinstance(e, int) else e[1]
                b = o % 6 if isinstance(o, int) else f * NC + c
                pe.wait_ge(raw_used[f], slot_n + 2)
                pe.wait_ge(nrm[1]["h"], (c + 1) * KT)
                pe.wait_ge(m_ev, o + 1)
                for k in range(KT):
                    m = three(ps[:, b, 0:CH], wiH[:, f, k * P:(k + 1) * P], wiL[:, f, k * P:(k + 1) * P],
                              hH[:, k, chunk(c)], hL[:, k, chunk(c)], k == 0, k == KT - 1)
                m.then_inc(m_ready, 1)

            def gates(j):
                pe.wait_ge(xc_ready, j + 1)
                for n in range(12):
                    c, g = n % NC, n // NC
                    w = slice((j * 4 + g) * DH, (j * 4 + g + 1) * DH)
                    if j * 12 + n >= 2:
                        pe.wait_ge(gate_ev, j * 12 + n - 1)
                    for r in (slice(0, DH), slice(DH, P)):
                        m = pe.matmul(ps[r, 6 + n % 2, 0:CH], gw[r, w], x[r, XC[j % 2], chunk(c)], start=True, stop=True,
                                      tile_position=(r.start, r.start))
                    m.then_inc(gate_ready, 1)

            for c in range(NC):
                for f in range(2):
                    in_chunk(f, c, 2 * c + f, used_in[f])
                if c == 0:
                    stats(1, NC - 1)
            for e in range(2, 4):
                for c in range(NC):
                    in_chunk(e, c, e * NC + c, e // 2 + used_in[e % 2])
            pe.wait_ge(gw_in, 16)
            for j in range(2):
                gates(j)
                for e in (4 + 2 * j, 5 + 2 * j):
                    for c in range(NC):
                        in_chunk(e, c, e * NC + c, e // 2 + used_in[e % 2])
            for hf in range(2):
                gates(2 + hf)
                pe.wait_ge(m_ev, 6 + 24)
                for kk in range(2):
                    pe.wait_ge(raw_used[2 + kk], used_in[2 + kk] + hf + 2)
                for t in range(T // P):
                    n = hf * 9 + t
                    if n >= 6:
                        pe.wait_ge(v_ev, n - 5)
                    tk = slice(t * P, (t + 1) * P)
                    for k in range(KT):
                        wv = slice((k % 4) * 256, (k % 4 + 1) * 256)
                        m = three(ps[:, n % 6, 0:256], hH[:, k, tk], hL[:, k, tk], wiH[:, k // 4, wv], wiL[:, k // 4, wv],
                                  k == 0, k == KT - 1)
                    m.then_inc(v_ready, 1)
            pe.wait_ge(v_ev, 18)
            with pe.Fori(0, 4) as i:
                for f in range(2):
                    for c in range(NC):
                        in_chunk((i, f), c, i * 6 + (24 + f * NC + c), i + (used_in[f] + 4))

            def scores(q, m):
                k0, k1 = (0, CTX) if q == 0 else (CTX, KEYS)
                r = slice(m * DH, (m + 1) * DH)
                for c in range(-(-(k1 - k0) // CH)):
                    w = min(CH, k1 - k0 - c * CH)
                    kk = slice(k0 + c * CH, k0 + c * CH + w)
                    for j, (A, B) in enumerate(((qH, kH), (qH, kL), (qL, kH))):
                        mm = pe.matmul(ps[:, 3 * m + c, 0:w], A[r, q * P:(q + 1) * P], B[r, kk],
                                       start=j == 0, stop=j == 2, tile_position=(m * DH, 0))
                mm.then_inc(s_ready, 1)

            def group(hd, t, g):
                nk = KEY_TILES[t]
                if 3 * g >= nk:
                    return
                if g == 0:
                    pe.wait_ge(pd_ready, hd * 9 + (t + 1))
                pe.wait_ge(t_lo, hd * GROUPS + (GROUP0[t] + g + 1))
                for k in range(3 * g, min(3 * g + 3, nk)):
                    m = pe.transpose(ps[:, 6, (k % 3) * P:(k % 3 + 1) * P], pr[:, t % 2, 0, k * P:(k + 1) * P],
                                     ident[:])
                m.then_inc(t_ready, 1)

            def values(hd, t):
                nk = KEY_TILES[t]
                pe.wait_ge(t_lo, hd * GROUPS + (GROUP0[t + 1] + 1))
                pe.wait_ge(o_done, hd * 9 + (t + 2))
                for k in range(nk):
                    rhs = vHL[:, 0 if t == 0 else 1 + k].rearrange("p a b -> p (a b)")
                    pe.matmul(ps[:, 7, 0:256], pTH[:, t % 2, k], rhs, start=k == 0, stop=False)
                    m = pe.matmul(ps[:, 7, 0:256], pTL[:, t % 2, k], rhs, start=False, stop=k == nk - 1)
                m.then_inc(o_ready, 1)

            pe.wait_ge(m_ev, 6 + 48)
            pe.wait_ge(acst, N_ACST)
            with pe.Fori(0, NH) as hd:
                pe.wait_ge(pp_lo, hd * 5 + 3)
                for n in range(11):
                    for m in range(2):
                        if n < 9:
                            if n > 0:
                                pe.wait_ge(e_done, hd * 18 + (2 * n + m - 1))
                            scores(n, m)
                        if 0 < n < 10:
                            group(hd, n - 1, m)
                    if n == 2:
                        pe.wait_ge(pp_lo, hd * 5 + 5)
                    if n > 1:
                        values(hd, n - 2)
                    if 0 < n < 10:
                        group(hd, n - 1, 2)

            def out_chunk(i, c, between=None):
                for f in range(2):
                    pe.wait_ge(raw_used[f], i + (used_wo[f] + 2))
                    pe.wait_ge(w_x, i * 6 + (c * 2 + f + 1))
                    for n, k in enumerate(MIX_ORDER):
                        m = three(ps[:, f * NC + c, 0:CH], wiH[:, f, k * P:(k + 1) * P], wiL[:, f, k * P:(k + 1) * P],
                                  hH[:, k, chunk(c)], hL[:, k, chunk(c)], n == 0, n == KT - 1)
                        if n == KT - 1:
                            m.then_inc(w_ready, 1)
                        if between is not None:
                            between(f * KT + n)

            for c in range(NC):
                for hd in range(NH):
                    n = c * NH + hd
                    pe.wait_ge(o_nrm, n + 1)
                    if n >= 2:
                        pe.wait_ge(mix_lo, (n - 2) // NH * KT + RGT + (n - 2) % NH + 1)
                    for k in range(3):
                        m = pe.transpose(ps[:, 6 + n % 2, k * P:(k + 1) * P], v[:, c * 3 + k, hd * P:(hd + 1) * P],
                                         ident[:])
                    m.then_inc(ot_ready, 1)
                if c:
                    out_chunk(0, c - 1)
            pe.wait_ge(mix_lo, NC * KT)
            out_chunk(0, NC - 1)
            with pe.Fori(0, 2) as i:
                for c in range(NC):
                    out_chunk(i + 1, c)
            out_chunk(3, 0)
            out_chunk(3, 1)
            stats(2, 0)
            out_chunk(3, 2, lambda n: stats(2, 1, (n // 2,)) if n % 2 else None)
            ffn_pe(1, 0, lambda c: stats(2, NC - 1) if c == 0 else None)
            with pe.Fori(1, NG - 1) as i:
                ffn_pe(1, i)
            ffn_pe(1, NG - 1)
            stats(3, NC - 1)

        @blk.scalar
        def _(act):
            for z in range(2):
                act.sem_inc(ffn[z]["silu"], 2)
            act.sem_inc(m_ev, 6)
            act.sem_inc(o_ss, 1)

            def cast(dst, slot, n, free=None):
                act.wait_ge(raw_full[slot], n * 16 + 16)
                if free is not None:
                    act.wait_ge(*free)
                act.activation(dst, raw[:, slot], ACT.Copy).then_inc(w_hi, 1)

            def squares(z, c, ready, tiles=range(KT)):
                s = nrm[z]
                for k in tiles:
                    act.wait_ge(*ready(c, k))
                    n = c * KT + k
                    if n >= 2:
                        act.wait_ge(s["sq_used"], n - 1)
                    act.activation(tmp[:, k % 2], x[:, k, chunk(c)], ACT.Square).then_inc(s["sq"], 1)

            def root(z, c):
                s = nrm[z]
                act.wait_ge(s["sq_used"], (c + 1) * KT)
                if c > 0:
                    act.wait_ge(s["h"], c * KT)
                act.activation(rstd[:], ps[:, stats_bank(z, c), 0:CH], ACT.Sqrt, bias=eps[:, 0:1]).then_inc(s["sd"], 1)

            def h_hi(z, c, tiles=range(KT)):
                s = nrm[z]
                for k in tiles:
                    act.wait_ge(s["hf"], c * KT + k + 1)
                    for cond, b, e in conds(c):
                        m = act.activation(hH[:, k, b:e], tmp[:, 2 + k % 2, b - c * CH:e - c * CH], ACT.Identity,
                                           bias=mod[:, 3 * z * KT + k, cond:cond + 1])
                    m.then_inc(s["hi"], 1)

            def norm(z, ready):
                squares(z, 0, ready)
                root(z, 0)
                for k in range(KT):
                    if z < 3:
                        h_hi(z, 0, (k,))
                    squares(z, 1, ready, (k,))
                root(z, 1)
                if z < 3:
                    h_hi(z, 1)
                squares(z, 2, ready)
                root(z, 2)
                if z < 3:
                    h_hi(z, NC - 1)

            def mod_evac(b, used):
                act.wait_ge(mod_prod, b + 1)
                if used:
                    act.sem_inc(raw_used[3], 1)
                act.activation(modp[:], ps[:, 7, :], ACT.Copy).then_inc(mod_copy, 1)

            act.wait_ge(smalls, N_SMALL)
            act.wait_ge(cons, 3)
            act.activation(cs[:, :, 0:2], cin[:], ACT.Silu).then_inc(c_ready, 1)
            act.wait_ge(rl_in, 1)
            act.activation(lnorm[:, 8:16], lnorm[:, 0:8], ACT.Exp).then_inc(rl_exp, 1)
            for c in range(NC):
                squares(0, c, lambda c, k: (xin[k], 16))
            for b in range(4):
                mod_evac(b, False)
            root(0, 0)
            h_hi(0, 0)
            for j, w in enumerate(("g0", "u0")):
                cast(guH[0][:, j].rearrange("p k n -> p (k n)"), *first(0, w))
            root(0, 1)
            h_hi(0, 1)
            for b in range(4, 6):
                mod_evac(b, False)
            root(0, 2)
            h_hi(0, 2)
            for b in range(6, PRE + 1):
                mod_evac(b, b == PRE)

            def ffn_act(z, i, last, with_mod=True):
                s = ffn[z]

                def hidden(f, c):
                    o = i * 6 + (f * NC + c)
                    b = (f * NC + c) % 2
                    act.wait_ge(s["g"], o + 1)
                    act.wait_ge(s["prod"], o + 1)
                    act.activation(tmp[:, b], ps[:, b, 0:CH], ACT.Silu).then_inc(s["silu"], 1)
                    act.wait_ge(s["prod"], o + 3)
                    act.wait_ge(s["d"], i * 24 + 8 * (c + 1))
                    act.activation(hidH[:, f, chunk(c)], tmp[:, 2 + b], ACT.Copy).then_inc(s["hidhi"], 1)

                if z == 0 and with_mod:
                    mod_evac(i + PRE, True)
                for j, w in enumerate(("g1", "u1")):
                    cast(guH[1][:, j].rearrange("p k n -> p (k n)"), *nth(z, w, i), (s["u"], i * 6 + 6))
                hidden(0, 0)
                for j in range(2):
                    cast(dnH[:, j], *nth(z, f"d{j}", i), (s["d"], i * 24 + 24))
                hidden(0, 1)
                hidden(0, 2)
                if not last:
                    for j, w in enumerate(("g0", "u0")):
                        cast(guH[0][:, j].rearrange("p k n -> p (k n)"), *nth(z, w, i), (s["u"], i * 6 + 9))
                for c in range(NC):
                    hidden(1, c)

            ffn_act(0, 0, False, False)
            with act.Fori(1, NG - 1) as i:
                ffn_act(0, i, False)
            ffn_act(0, NG - 1, True)
            act.wait_ge(ffn[0]["u"], 6 + NG * 6)
            for e in range(2):
                cast(wiH[:, e], e, used_in[e])
            norm(1, lambda c, k: (ffn[0]["x"], 3 + (NG - 1) * 24 + c * KT + k + 1))

            def in_evac(dst, o):
                act.wait_ge(m_ready, o + 1)
                act.activation(dst, ps[:, o % 6, 0:CH], ACT.Copy).then_inc(m_ev, 1)

            for c in range(NC):
                for f in range(2):
                    in_evac(xr[:, f, chunk(c)], 2 * c + f)
            for e in range(2, 4):
                cast(wiH[:, e % 2], e % 2, e // 2 + used_in[e % 2])
            for e in range(2, 4):
                for c in range(NC):
                    in_evac(xr[:, e, chunk(c)], e * NC + c)
                cast(wiH[:, e % 2], e % 2, e // 2 + 1 + used_in[e % 2])

            def v_evac(n):
                act.wait_ge(v_ready, n + 1)
                act.activation(v[:, n % 9, n // 9 * 256:(n // 9 + 1) * 256], ps[:, n % 6, 0:256],
                               ACT.Copy).then_inc(v_ev, 1)

            act.wait_ge(spilled, 16 * KT)
            act.wait_ge(nrm[1]["h"], NC * KT)
            for j in range(RGT):
                if j:
                    act.wait_ge(rg_y, j)
                for n in range(12):
                    c, g = n % NC, n // NC
                    act.wait_ge(gate_ready, j * 12 + n + 1)
                    act.activation(x[:, 1 + g, chunk(c)], ps[:, 6 + n % 2, 0:CH], ACT.Sigmoid,
                                   bias=gbias[:, j, g // 2, g % 2:g % 2 + 1]).then_inc(gate_ev, 1)
                act.wait_ge(gate_ev, j * 12 + 12)
                for d in range(2):
                    act.activation(x[:, 5 + d], x[:, 1 + 2 * d], ACT.Exp, scale=glam[:, 0, 2 * j + d:2 * j + d + 1]).then_inc(rg_a, 1)
                act.wait_ge(rg_a, 2 * j + 2)
                for d in range(2):
                    act.activation(x[:, 1 + 2 * d], x[:, 1 + 2 * d], ACT.Tanh,
                                   scale=glam[:, 1, 2 * j + d:2 * j + d + 1]).then_inc(rg_e, 1)

                def roots(j=j):
                    for d in range(2):
                        act.wait_ge(rg_m, 2 * j + d + 1)
                        act.activation(x[:, 1 + 2 * d], x[:, 1 + 2 * d], ACT.Sqrt).then_inc(rg_s, 1)

                if j < 2:
                    for e in (4 + 2 * j, 5 + 2 * j):
                        for c in range(NC):
                            in_evac(xg[:, e - 4, chunk(c)], e * NC + c)
                            if e % 2 == 0 and c == 1:
                                roots()
                        if e < 6:
                            cast(wiH[:, e % 2], e % 2, e // 2 + 1 + used_in[e % 2])
                        else:
                            cast(wiH[:, e - 6], e - 4, used_in[e - 4])
                else:
                    for t in range(9):
                        v_evac((j - 2) * 9 + t)
                        if t == 3:
                            roots()
                    for kk in range(2):
                        if j == 2:
                            cast(wiH[:, kk], 2 + kk, used_in[2 + kk] + 1)
                        else:
                            cast(wiH[:, kk], kk, used_in[kk] + 4)
            for j in range(RGT):
                act.activation(xg[:, j], xg[:, j], ACT.Gelu_apprx_tanh).then_inc(gelu, 1)
            act.wait_ge(rg_y, RGT)
            def qk_pair(i, last):
                for f in range(2):
                    for c in range(NC):
                        act.wait_ge(m_ready, i * 6 + (24 + f * NC + c + 1))
                        alone(act)
                        act.activation(x[:, i * 2 + f, chunk(c)], ps[:, f * NC + c, 0:CH], ACT.Copy).then_inc(m_ev, 1)
                    if not last:
                        cast(wiH[:, f], f, i + (used_in[f] + 5))
            with act.Fori(0, 3) as i:
                qk_pair(i, False)
            qk_pair(3, True)

            act.wait_ge(m_ev, 6 + 48)
            act.wait_ge(m_ready, 48)
            for e in range(2):
                cast(wiH[:, e], e, used_wo[e])
            act.wait_ge(acst, N_ACST)
            act.wait_ge(lam_p, 1)
            act.activation(lams[:, 2:4], lams[:, 0:2], ACT.Exp).then_inc(lam_e, 1)

            def p_hi(hd, t, g):
                w = min(3, KEY_TILES[t] - 3 * g)
                if w > 0:
                    act.wait_ge(t_ready, hd * GROUPS + (GROUP0[t] + g + 1))
                    act.activation(pTH[:, t % 2, 3 * g:3 * g + w].rearrange("p k n -> p (k n)"), ps[:, 6, 0:w * P],
                                   ACT.Copy).then_inc(t_hi, 1)

            def exps(hd, n, m):
                act.wait_ge(mx_ready, hd * 18 + (2 * n + m + 1))
                if n == 0:
                    src, dst = ps[:, 3 * m, 0:CTX], pr[:, 0, m, 0:CTX]
                else:
                    src = ps[:, 3 * m:3 * m + 3, 0:CH]
                    dst = pr[:, n % 2, m].rearrange("p (c t) -> p c t", c=NC)
                act.activation(dst, src, ACT.Exp, bias=nmx[:, n % 2, m:m + 1],
                               accum_out=sums[:, n % 3, m:m + 1]).then_inc(e_done, 1)

            act.wait_ge(roped, KT)
            with act.Fori(0, NH) as hd:
                act.activation(kH[:, 0:T], x[:, hd + 4], ACT.Copy).then_inc(pp_hi, 1)
                act.activation(kH[:, T:KEYS], kc[:, hd], ACT.Copy).then_inc(pp_hi, 1)
                act.activation(qH[:], x[:, hd], ACT.Copy, scale=DH ** -0.5).then_inc(pp_hi, 1)
                act.activation(vHL[:, 0:9, 0], v[:, :, bass.ds(hd * P, P)], ACT.Copy).then_inc(pp_hi, 1)
                act.activation(vHL[:, 9, 0], vc[:, bass.ds(hd * P, P)], ACT.Copy).then_inc(pp_hi, 1)
                for n in range(12):
                    for m in range(2):
                        if 0 < n < 10:
                            p_hi(hd, n - 1, m)
                        if n < 9:
                            exps(hd, n, m)
                    if 2 <= n < 11:
                        t = n - 2
                        act.wait_ge(o_ready, hd * 9 + (t + 1))
                        act.wait_ge(o_done, hd * 9 + (t + 1))
                        act.activation(tmp[:, t % 2, 0:P], ps[:, 7, 0:P], ACT.Copy,
                                       scale=rec[:, t % 3, 0:1]).then_inc(o_half, 1)
                    if 0 < n < 10:
                        p_hi(hd, n - 1, 2)
                    if n >= 3:
                        t = n - 3
                        act.wait_ge(o_done, hd * 9 + (t + 3))
                        act.wait_ge(o_ss, hd * 9 + (t + 1))
                        alone(act)
                        act.activation(tmp[:, 2, 0:P], v[:, t, bass.ds(hd * P, P)], ACT.Square,
                                       accum_out=ss[:, hd, t:t + 1]).then_inc(o_ss, 1)

            act.wait_ge(o_ss, 1 + NH * 9)
            act.activation(ss[:], ss[:], ACT.Sqrt, bias=eps[:, 0:1], scale=1.0 / P).then_inc(o_sd, 1)
            for c in range(NC):
                for k in MIX_ORDER:
                    if k < NH:
                        n = c * NH + k
                        act.wait_ge(ot_ready, n + 1)
                        act.activation(hH[:, k, chunk(c)], ps[:, 6 + n % 2, 0:CH], ACT.Copy,
                                       scale=subg[:, 0:1]).then_inc(mix_hi, 1)
                    else:
                        act.activation(hH[:, k, chunk(c)], xr[:, k - 4, chunk(c)], ACT.Copy).then_inc(mix_hi, 1)
            with act.Fori(0, 3) as i:
                for f in range(2):
                    cast(wiH[:, f], f, i + (used_wo[f] + 1), (w_ready, i * 6 + (5 + f)))
            act.wait_ge(mix_lo, NC * KT)
            for j, w in enumerate(("g0", "u0")):
                cast(guH[0][:, j].rearrange("p k n -> p (k n)"), *first(1, w))
            norm(2, lambda c, k: (w_x, 6 + 18 + 2 * c + (k - 5 if k > 5 else 0)))
            with act.Fori(0, NG - 1) as i:
                ffn_act(1, i, False)
            ffn_act(1, NG - 1, True)
            norm(3, lambda c, k: (ffn[1]["x"], 3 + (NG - 1) * 24 + c * KT + k + 1))

        @blk.vector
        def _(dve):
            chain = [0]

            def link(ins):
                chain[0] += 1
                ins.then_inc(step, 1)
                dve.wait_ge(step, chain[0])

            def lo(dst, slot, n, hi, count):
                dve.wait_ge(w_hi, count)
                dve.tensor_tensor(dst, raw[:, slot], hi.bitcast(F32), ALU.subtract).then_inc(raw_used[slot], 1)

            def flat(w):
                return w.rearrange("p k n -> p (k n)")

            for s in range(SLOTS):
                dve.sem_inc(raw_used[s], 1)
            for z in range(2):
                dve.sem_inc(ffn[z]["prod"], 2)
                dve.sem_inc(ffn[z]["x"], 3)
                dve.sem_inc(ffn[z]["hidlo"], 2)
            dve.sem_inc(t_lo, 1)
            dve.sem_inc(o_done, 2)
            dve.sem_inc(w_x, 6)
            dve.memset(ones[:], 1.0 / D).then_inc(cons, 1)
            dve.memset(eps[:], EPS).then_inc(cons, 1)
            dve.memset(cs[:], 0.0).then_inc(cons, 1)
            dve.wait_ge(smalls, N_SMALL)
            g0, g1 = glam[:, 0], glam[:, 1]
            lt = hout[:].rearrange("p a b -> p (a b)")
            link(dve.tensor_scalar(lt, g0, -1.0, 0.0, ALU.mult, ALU.max))
            link(dve.tensor_scalar(g1, g0, -1.0, None, ALU.mult))
            link(dve.tensor_tensor(g1, g0, g1, ALU.min))
            dve.tensor_copy(lnorm[:, 0:8], g1).then_inc(rl_in, 1)
            dve.wait_ge(rl_exp, 1)
            y, q, r = lnorm[:, 8:16], lnorm[:, 16:24], lnorm[:, 24:32]
            link(dve.tensor_scalar(q, y, 2.0, None, ALU.add))
            link(dve.reciprocal(q, q))
            link(dve.tensor_tensor(y, y, q, ALU.mult))
            link(dve.tensor_tensor(q, y, y, ALU.mult))
            link(dve.memset(r, 1.0 / 17))
            for n in range(15, 0, -2):
                link(dve.tensor_tensor(r, r, q, ALU.mult))
                link(dve.tensor_scalar(r, r, 1.0 / n, None, ALU.add))
            link(dve.tensor_tensor(r, r, y, ALU.mult))
            link(dve.scalar_tensor_tensor(r, r, 2.0, lt, ALU.mult, ALU.add))
            link(dve.tensor_scalar(g0, r, -8.0, None, ALU.mult))
            link(dve.tensor_scalar(g1, r, 8.0, None, ALU.mult))
            link(dve.tensor_scalar(subg[:], subg[:], 1.0 - LAM_INIT, None, ALU.mult))

            def mod_add(b):
                dve.wait_ge(mod_sum, b + 1)
                at = slice(4 * b, 4 * b + 4) if isinstance(b, int) else bass.ds(b * 4, 4)
                dve.tensor_tensor(mod[:, at], ps[:, 7, 0:8].rearrange("p (n c) -> p n c", c=2), bmod[:, at],
                                  ALU.add).then_inc(mod_done, 1)

            def scale_of(z):
                s = mod[:, (3 * z + 1) * KT:(3 * z + 2) * KT]
                link(dve.scalar_tensor_tensor(s, s, 1.0, ng[:, z], ALU.add, ALU.mult))

            def gate_of(z):
                s = mod[:, (3 * z + 2) * KT:(3 * z + 3) * KT]
                link(dve.tensor_scalar(s, s, 0.5, None, ALU.mult))

            def apply(z, c, between=None):
                s = nrm[z]
                dve.wait_ge(s["sd"], c + 1)
                link(dve.reciprocal(rstd[:], rstd[:]))

                def part(k, b, e):
                    return tmp[:, 2 + k % 2, b - c * CH:e - c * CH]

                def lo_part(k):
                    dve.wait_ge(s["hi"], c * KT + k + 1)
                    for cond, b, e in conds(c):
                        m = dve.scalar_tensor_tensor(hL[:, k, b:e], part(k, b, e), mod[:, 3 * z * KT + k, cond:cond + 1],
                                                     hH[:, k, b:e].bitcast(F32), ALU.add, ALU.subtract)
                    m.then_inc(s["h"], 1)

                for k in range(KT):
                    if c * KT + k >= 2:
                        dve.wait_ge(s["h"], c * KT + k - 1)
                    for cond, b, e in conds(c):
                        m = dve.scalar_tensor_tensor(part(k, b, e), x[:, k, b:e],
                                                     mod[:, (3 * z + 1) * KT + k, cond:cond + 1],
                                                     rstd[:, b - c * CH:e - c * CH], ALU.mult, ALU.mult)
                    m.then_inc(s["hf"], 1)
                    if k:
                        lo_part(k - 1)
                    if between is not None:
                        between(k)
                lo_part(KT - 1)
                if c == NC - 1:
                    dve.wait_ge(s["h"], NC * KT)

            def final(c, between=None):
                dve.wait_ge(nrm[3]["sd"], c + 1)
                link(dve.reciprocal(rstd[:], rstd[:]))
                for k in range(KT):
                    xt = x[:, k, chunk(c)]
                    dve.scalar_tensor_tensor(xt, xt, fg[:, k:k + 1], rstd[:], ALU.mult, ALU.mult).then_inc(y_done, 1)
                    if between is not None:
                        between(k)
                dve.wait_ge(y_done, (c + 1) * KT)
                dve.sem_inc(nrm[3]["h"], KT)

            for b in range(4):
                mod_add(b)
            dve.wait_ge(mod_done, 4)
            scale_of(0)
            for k in range(KT):
                dve.wait_ge(xin[k], 16)
            apply(0, 0)
            for j, w in enumerate(("g0", "u0")):
                slot, n = first(0, w)
                lo(flat(guL[0][:, j]), slot, n, flat(guH[0][:, j]), j + 1)
            apply(0, 1)
            for b in range(4, 6):
                mod_add(b)
            apply(0, 2)
            for b in range(6, PRE + 1):
                mod_add(b)
            gate_of(0)

            def ffn_dve(z, i, last, w0, with_mod=True):
                s = ffn[z]
                gate = (3 * 2 * z + 2) * KT

                def hidden(f, c):
                    o = i * 6 + (f * NC + c)
                    b = (f * NC + c) % 2
                    dve.wait_ge(s["silu"], o + 3)
                    dve.wait_ge(s["hidlo"], o + 1)
                    dve.wait_ge(s["u"], o + 7)
                    dve.tensor_tensor(tmp[:, 2 + b], ps[:, 2 + b, 0:CH], tmp[:, b], ALU.mult).then_inc(s["prod"], 1)
                    dve.wait_ge(s["hidhi"], o + 1)
                    dve.tensor_tensor(hidL[:, f, chunk(c)], tmp[:, 2 + b], hidH[:, f, chunk(c)].bitcast(F32),
                                      ALU.subtract).then_inc(s["hidlo"], 1)

                def weights(dst_lo, dst_hi, item, j):
                    slot, n = nth(z, item, i)
                    lo(dst_lo, slot, n, dst_hi, i * 6 + (w0 + j))

                def add(c, t):
                    dve.wait_ge(s["d"], i * 24 + (c * KT + t + 25))
                    for cond, b, e in conds(c):
                        m = dve.scalar_tensor_tensor(x[:, t, b:e], ps[:, 4 + (c * KT + t) % 3, b - c * CH:e - c * CH],
                                                     mod[:, gate + t, cond:cond + 1], x[:, t, b:e],
                                                     ALU.mult, ALU.add)
                    m.then_inc(s["x"], 1)

                for j, w in enumerate("gu"):
                    weights(flat(guL[1][:, j]), flat(guH[1][:, j]), w + "1", j + 1)
                hidden(0, 0)
                if z == 0 and with_mod:
                    mod_add(i + PRE)
                for j in range(2):
                    weights(dnL[:, j], dnH[:, j], f"d{j}", j + 3)
                hidden(0, 1)
                hidden(0, 2)
                if not last:
                    for j, w in enumerate("gu"):
                        weights(flat(guL[0][:, j]), flat(guH[0][:, j]), w + "0", j + 5)
                for c in range(NC):
                    hidden(1, c)
                dve.wait_ge(s["x"], i * 24 + 3)
                if last and z == 0:
                    dve.wait_ge(mod_done, NB_MOD)
                    scale_of(1)
                    scale_of(2)
                    gate_of(2)
                for c in range(2 if last else NC):
                    for t in range(KT):
                        add(c, t)
                    if last and z == 0:
                        lo(wiL[:, c], c, None, wiH[:, c], whi_in + c + 1)
                if last:
                    follow = final if z else lambda c, between=None: apply(1, c, between)
                    dve.wait_ge(s["x"], i * 24 + 3 + 2 * KT)
                    follow(0, lambda k: add(2, k))
                    dve.wait_ge(s["x"], i * 24 + 3 + 3 * KT)
                    follow(1)
                    follow(2)

            whi_in = 2 + 6 * NG - 2
            ffn_dve(0, 0, False, 2, False)
            with dve.Fori(1, NG - 1) as i:
                ffn_dve(0, i, False, 2)
            ffn_dve(0, NG - 1, True, 2)

            def conv(j):
                xc = x[:, XC[j % 2]]
                dve.wait_ge(m_ev, 12 if j < 2 else 6 + 3 * (j + 1))
                link(dve.tensor_scalar(xc, xr[:, j], convw[:, j, 2:3], convb[:, j:j + 1], ALU.mult, ALU.add))
                for tap, off in ((0, -2), (1, -1), (3, 1)):
                    for b, end in ((0, CTX), (CTX, T)):
                        lo_t, hi_t = max(b, b - off), min(end, end - off)
                        link(dve.scalar_tensor_tensor(xc[:, lo_t:hi_t], xr[:, j, lo_t + off:hi_t + off],
                                                      convw[:, j, tap:tap + 1], xc[:, lo_t:hi_t], ALU.mult, ALU.add))
                dve.sem_inc(xc_ready, 1)

            for e in range(2, 4):
                lo(wiL[:, e % 2], e % 2, None, wiH[:, e % 2], whi_in + e + 1)
            dve.wait_ge(spilled, 16 * KT)
            conv(0)
            for e in range(4, 6):
                lo(wiL[:, e % 2], e % 2, None, wiH[:, e % 2], whi_in + e + 1)
            for j in range(RGT):
                xc = x[:, XC[j % 2]]
                dve.wait_ge(gate_ev, 12 * j + 12)
                for d in range(2):
                    link(dve.tensor_tensor(x[:, 2 + 2 * d], x[:, 2 + 2 * d], xc, ALU.mult))
                for d in range(2):
                    dve.wait_ge(rg_e, 2 * j + d + 1)
                    link(dve.tensor_tensor(xr[:, j], x[:, 5 + d], x[:, 5 + d], ALU.mult))
                    dve.scalar_tensor_tensor(x[:, 1 + 2 * d], xr[:, j], 1.0, x[:, 1 + 2 * d], ALU.add,
                                             ALU.mult).then_inc(rg_m, 1)
                    dve.wait_ge(rg_m, 2 * j + d + 1)
                if j + 1 < RGT:
                    conv(j + 1)
                for d in range(2):
                    dve.wait_ge(rg_s, 2 * j + d + 1)
                    bx, r = x[:, 2 + 2 * d], x[:, 1 + 2 * d]
                    link(dve.tensor_tensor(bx, r, bx, ALU.mult))
                    for b, end, init in ((0, CTX, 0.0), (CTX, T, h0[:, j, d:d + 1])):
                        s = slice(b, end) if d == 0 else slice(end - 1, b - 1 if b else None, -1)
                        link(dve.tensor_tensor_scan(x[:, 1 + 2 * d, s], x[:, 5 + d, s], x[:, 2 + 2 * d, s], init,
                                                    ALU.mult, ALU.add))
                    last_t = CTX - 1 if d == 0 else 0
                    link(dve.tensor_copy(hout[:, j, d:d + 1], x[:, 1 + 2 * d, last_t:last_t + 1]))
                dve.tensor_tensor(xr[:, j], x[:, 1], x[:, 3], ALU.add).then_inc(rg_y, 1)
                for kk in range(2):
                    lo(wiL[:, kk], kk if j in (0, 3) else 2 + kk, None, wiH[:, kk], whi_in + 7 + 2 * j + kk)
            for j in range(RGT):
                dve.wait_ge(gelu, j + 1)
                dve.wait_ge(rg_y, j + 1)
                dve.tensor_tensor(xr[:, j], xr[:, j], xg[:, j], ALU.mult).then_inc(rg_out, 1)
            dve.wait_ge(acst, N_ACST)
            for j in range(2):
                link(dve.tensor_tensor(dl[:, 2 * j], dl[:, 2 * j], dl[:, 2 * j + 1], ALU.mult))
                link(dve.tensor_reduce(lams[:, j:j + 1], dl[:, 2 * j], AX.X, ALU.add))
            dve.sem_inc(lam_p, 1)
            swap = [(p + 16) % 32 for p in range(32)]
            for e in range(KT):
                if e < 6:
                    lo(wiL[:, e % 2], e % 2, None, wiH[:, e % 2], whi_in + 15 + e)
                dve.wait_ge(m_ev, 6 + 24 + 3 * (e + 1))
                xt = x[:, e, CTX:T]
                link(dve.stream_shuffle(swp[:], xt, swap))
                link(dve.tensor_tensor(xt, xt, cosT[:], ALU.mult))
                link(dve.tensor_tensor(swp[:], swp[:], sinT[:], ALU.mult))
                link(dve.tensor_tensor(xt, xt, swp[:], ALU.add))
            dve.sem_inc(roped, KT)
            whi_wo = whi_in + 20
            for e in range(2):
                lo(wiL[:, e], e, None, wiH[:, e], whi_wo + e + 1)

            dve.wait_ge(lam_e, 1)
            link(dve.tensor_tensor(nlam[:], lams[:, 3:4], lams[:, 2:3], ALU.subtract))
            link(dve.tensor_scalar(nlam[:], nlam[:], -LAM_INIT, None, ALU.add))
            chain0 = chain[0]
            STEPS = 36
            with dve.Fori(0, NH) as hd:
                k_in = [0]

                def hlink(ins):
                    k_in[0] += 1
                    ins.then_inc(step, 1)
                    dve.wait_ge(step, hd * STEPS + (chain0 + k_in[0]))

                def maxima(n, m):
                    dve.wait_ge(s_ready, hd * 18 + (2 * n + m + 1))
                    src = ps[:, 3 * m, 0:CTX] if n == 0 else ps[:, 3 * m:3 * m + 3, 0:CH]
                    hlink(dve.tensor_reduce(mx[:, n % 2, m:m + 1], src, AX.X if n == 0 else AX.XY, ALU.max))
                    dve.tensor_scalar(nmx[:, n % 2, m:m + 1], mx[:, n % 2, m:m + 1], -1.0, None,
                                      ALU.mult).then_inc(mx_ready, 1)

                def p_lo(t, g):
                    w = min(3, KEY_TILES[t] - 3 * g)
                    if w > 0:
                        dve.wait_ge(t_hi, hd * GROUPS + (GROUP0[t] + g + 1))
                        at_k = slice(3 * g, 3 * g + w)
                        dve.tensor_tensor(flat(pTL[:, t % 2, at_k]), ps[:, 6, 0:w * P],
                                          flat(pTH[:, t % 2, at_k]).bitcast(F32), ALU.subtract).then_inc(t_lo, 1)

                def difference(t):
                    w = CTX if t == 0 else T
                    r = t % 3
                    dve.wait_ge(e_done, hd * 18 + (2 * t + 2))
                    hlink(dve.reciprocal(rec[:, r], sums[:, r]))
                    hlink(dve.scalar_tensor_tensor(coef[:, r:r + 1], sums[:, r, 0:1], nlam[:, 0:1],
                                                   rec[:, r, 1:2], ALU.mult, ALU.mult))
                    dve.scalar_tensor_tensor(pr[:, t % 2, 0, 0:w], pr[:, t % 2, 1, 0:w], coef[:, r:r + 1],
                                             pr[:, t % 2, 0, 0:w], ALU.mult, ALU.add).then_inc(pd_ready, 1)

                at = bass.ds(hd * P, P)
                for j, (dst, src, hi) in enumerate((
                        (kL[:, 0:T], x[:, hd + 4], kH[:, 0:T]), (kL[:, T:KEYS], kc[:, hd], kH[:, T:KEYS]),
                        (qL[:], x[:, hd], qH[:]),
                        (vHL[:, 0:9, 1], v[:, :, at], vHL[:, 0:9, 0]), (vHL[:, 9, 1], vc[:, at], vHL[:, 9, 0]))):
                    dve.wait_ge(pp_hi, hd * 5 + (j + 1))
                    if j == 2:
                        m = dve.scalar_tensor_tensor(dst, src, DH ** -0.5, hi.bitcast(F32), ALU.mult, ALU.subtract)
                    else:
                        m = dve.tensor_tensor(dst, src, hi.bitcast(F32), ALU.subtract)
                    m.then_inc(pp_lo, 1)
                for n in range(11):
                    for m in range(2):
                        if n < 9:
                            maxima(n, m)
                        if 0 < n < 10:
                            p_lo(n - 1, m)
                    if n < 9:
                        difference(n)
                    if n >= 2:
                        t = n - 2
                        dve.wait_ge(o_half, hd * 9 + (t + 1))
                        dve.scalar_tensor_tensor(v[:, t, at], ps[:, 7, P:2 * P], rec[:, t % 3, 0:1], tmp[:, t % 2, 0:P],
                                                 ALU.mult, ALU.add).then_inc(o_done, 1)
                    if 0 < n < 10:
                        p_lo(n - 1, 2)
                assert k_in[0] == STEPS, k_in
            chain[0] += NH * STEPS

            dve.wait_ge(o_sd, 1)
            link(dve.reciprocal(ss[:], ss[:]))

            def sub_norm(c):
                for hd in range(NH):
                    for t in range(3 * c, 3 * c + 3):
                        o = v[:, t, hd * P:(hd + 1) * P]
                        m = dve.tensor_scalar(o, o, ss[:, hd, t:t + 1], None, ALU.mult)
                    m.then_inc(o_nrm, 1)

            sub_norm(0)
            for c in range(NC):
                for j, k in enumerate(MIX_ORDER):
                    dve.wait_ge(mix_hi, c * KT + j + 1)
                    hi = hH[:, k, chunk(c)].bitcast(F32)
                    if k < NH:
                        m = dve.scalar_tensor_tensor(hL[:, k, chunk(c)], ps[:, 6 + (c * NH + k) % 2, 0:CH], subg[:, 0:1], hi,
                                                     ALU.mult, ALU.subtract)
                    else:
                        m = dve.tensor_tensor(hL[:, k, chunk(c)], xr[:, k - 4, chunk(c)], hi, ALU.subtract)
                    m.then_inc(mix_lo, 1)
                    if j == RGT - 1 and c + 1 < NC:
                        sub_norm(c + 1)

            def w_add(i, c, f):
                dve.wait_ge(w_ready, i * 6 + (2 * c + f + 1))
                for cond, b, e in conds(c):
                    xt = x[:, i * 2 + f, b:e]
                    m = dve.scalar_tensor_tensor(xt, ps[:, f * NC + c, b - c * CH:e - c * CH],
                                                 mod[:, i * 2 + (5 * KT + f), cond:cond + 1], xt, ALU.mult, ALU.add)
                m.then_inc(w_x, 1)

            dve.wait_ge(xback, 16 * KT)
            with dve.Fori(0, 3) as i:
                for c in range(NC):
                    for f in range(2):
                        w_add(i, c, f)
                        if c == NC - 1:
                            lo(wiL[:, f], f, None, wiH[:, f], i * 2 + (whi_wo + 3 + f))
            whi_f2 = whi_wo + 8
            for j, w in enumerate(("g0", "u0")):
                slot, n = first(1, w)
                lo(flat(guL[0][:, j]), slot, n, flat(guH[0][:, j]), whi_f2 + j + 1)
            for c in range(2):
                for f in range(2):
                    w_add(3, c, f)
            apply(2, 0, lambda k: w_add(3, 2, k // 6) if k in (5, 7) else None)
            apply(2, 1)
            apply(2, 2)
            with dve.Fori(0, NG - 1) as i:
                ffn_dve(1, i, False, whi_f2 + 2)
            ffn_dve(1, NG - 1, True, whi_f2 + 2)
    return nc


def program(nc, shapes):
    a = {name: nc.dram_tensor("in_" + name, list(shape), F32, kind="ExternalInput").ap() for name, shape in shapes.items()}
    out = {name: nc.dram_tensor("out_" + name, list(shape), F32, kind="ExternalOutput").ap()
           for name, shape in (("y", (KT, P, T)), ("k", (NH, P, P)), ("v", (P, 512)), ("h", (P, RGT, 2)))}
    return build(nc, a, out)


def rope_tables():
    n = DH // 4
    inv = (np.float32(10000.0) ** (-np.arange(n, dtype=np.float32) / np.float32(n))).astype(np.float32)
    tok = np.arange(LAT)
    pos = np.stack([tok // GRID_W, tok % GRID_W]).astype(np.float32)
    p = np.arange(P)
    ang = pos[(p % DH) // (DH // 2)] * inv[p % n][:, None]
    sign = np.where(p % (2 * n) < n, -1.0, 1.0).astype(np.float32)[:, None]
    return np.cos(ang).astype(np.float32), (np.sin(ang) * sign).astype(np.float32)


def kernel(x_prompt, x_sample, cache_attn_k, cache_attn_v, state_rglru, c, c_ctx, norm_g, w_mod, b_mod,
           ffn_w_gate, ffn_w_up, ffn_w_down, w_in, w_out, diff_lambda, subln_g, conv_w, conv_b,
           rg_w_r, rg_b_r, rg_w_i, rg_b_i, rg_lambda, final_g):
    import concourse.bacc as bacc
    from concourse.bass_utils import run_bass_kernel_spmd

    def cols(w, n):
        r, m = w.shape
        return w.reshape(r // P, P, m // n, n).transpose(2, 1, 0, 3)

    cos, sin = rope_tables()
    sel = np.zeros((P, 2), np.float32)
    for q in range(4):
        sel[32 * q, 0] = sel[32 * q + 1, 1] = 1.0
    w3 = np.asarray(w_in)[0]
    q_, k_, v_, xr_, xg_ = (w3[:, 512 * n:512 * (n + 1)] for n in range(5))
    bmod = np.asarray(b_mod)[0].reshape(9 * KT, P).T
    ngt = np.asarray(norm_g)[0].reshape(3, KT, P).transpose(2, 0, 1)
    gwt = np.stack([np.asarray(rg_w_r)[0], np.asarray(rg_w_i)[0]])
    ffn_cols = lambda w: np.concatenate([cols(np.asarray(w)[0, z], P) for z in range(2)]).reshape(2 * FT, P, D)
    arrays = {
        "x": np.concatenate([np.asarray(x_prompt)[0], np.asarray(x_sample)[0]]).T.reshape(KT, P, T),
        "c": np.stack([np.asarray(c_ctx), np.asarray(c)[0]]).reshape(2, KT, P).transpose(2, 1, 0),
        "w_mod": cols(np.asarray(w_mod)[0], 512).reshape(NB_MOD, P, 4, 1024).transpose(0, 2, 1, 3),
        "bmod": np.stack([bmod, bmod], axis=2),
        "ng": np.stack([ngt, ngt], axis=3),
        "fg": np.asarray(final_g).reshape(KT, P).T,
        "w_gate": ffn_cols(ffn_w_gate),
        "w_up": ffn_cols(ffn_w_up),
        "w_down": np.asarray(ffn_w_down)[0].reshape(2 * FT, P, D),
        "w_in": cols(np.concatenate([xr_, xg_, q_, k_], axis=1), P).reshape(16, P, D),
        "w_v": cols(v_, 256).reshape(2, P, 2, 1024).transpose(0, 2, 1, 3).reshape(4, P, 1024),
        "w_out": cols(np.asarray(w_out)[0], P).reshape(KT, P, D),
        "kc": np.asarray(cache_attn_k)[0, 0].transpose(1, 2, 0),
        "vc": np.asarray(cache_attn_v)[0, 0].reshape(P, NH * P),
        "h0": np.asarray(state_rglru)[0, 0].reshape(2, RGT, P).transpose(2, 1, 0),
        "dl": np.asarray(diff_lambda)[0].reshape(4 * DH),
        "subg": np.asarray(subln_g)[0].reshape(P, 1),
        "convw": np.asarray(conv_w)[0].reshape(4, RGT, P).transpose(2, 1, 0),
        "convb": np.asarray(conv_b)[0].reshape(RGT, P).T,
        "gw": gwt.reshape(2, 2, RGT, 2, DH, DH).transpose(3, 4, 2, 1, 0, 5).reshape(P, 1024),
        "gbias": np.stack([np.asarray(rg_b_r)[0], np.asarray(rg_b_i)[0]]).reshape(2, 2, RGT, P).transpose(3, 2, 1, 0),
        "glam": np.asarray(rg_lambda)[0].reshape(2, RGT, P).transpose(2, 1, 0).reshape(P, 2 * RGT),
        "cos": cos,
        "sin": sin,
        "sel": sel,
        "ident": np.eye(P, dtype=np.float32),
    }
    arrays = {name: np.ascontiguousarray(v) for name, v in arrays.items()}
    nc = bacc.Bacc("TRN2", target_bir_lowering=False, num_devices=1)
    program(nc, {name: v.shape for name, v in arrays.items()})
    got = run_bass_kernel_spmd(nc, [{"in_" + name: v for name, v in arrays.items()}], core_ids=[0]).results[0]
    y = got["out_y"].reshape(D, T).T
    return (np.ascontiguousarray(y[:CTX])[None], np.ascontiguousarray(y[CTX:])[None],
            np.ascontiguousarray(got["out_k"].transpose(2, 0, 1))[None, None],
            got["out_v"].reshape(1, 1, P, NH, P),
            np.ascontiguousarray(got["out_h"].transpose(2, 1, 0)).reshape(1, 1, 2, RGT * P))
```

```python
import math
from contextlib import ExitStack

import numpy as np

import concourse.bass as bass
from concourse import mybir

F32 = mybir.dt.float32
F32R = mybir.dt.float32r
ACT = mybir.ActivationFunctionType
ALU = mybir.AluOpType
AX = mybir.AxisListType

P = 128
D = 1024
KT = D // P
CTX = 128
LAT = 1024
T = CTX + LAT
CH = 384
NC = T // CH
FF = 2816
FT = FF // P
NG = FT // 2
NH = 4
DH = 64
RGT = 4
NB_MOD = 18
PRE = NB_MOD - NG
SLOTS = 5
EPS = 1e-6
KEY_TILES = [1] + [9] * 8
GROUP0 = [0] + [1 + 3 * t for t in range(9)]
GROUPS = GROUP0[9]
MIX_ORDER = (4, 5, 6, 7, 0, 1, 2, 3)
LAM_INIT = 0.8 - 0.6 * math.exp(0.0)
KEYS = T + 128
GRID_W = 64


XC = (0, 7)


def count(head, per, k):
    h, off = head
    return h * per + (k + off * per)


def pt_at(t):
    return 18 if t == 0 else t % 2 * 9


def tile_of(h, n):
    return ((h, 0), n) if n >= 0 else ((h, -1), n + 9)


def chunk(c):
    return slice(c * CH, (c + 1) * CH)


def conds(c):
    if c == 0:
        return [(0, 0, CTX), (1, CTX, CH)]
    return [(1, c * CH, (c + 1) * CH)]


def build(nc, a, out):
    ctx = ExitStack()
    with ctx:
        def sem(name):
            return ctx.enter_context(nc.semaphore(name))

        def sb(name, shape, dt=F32, stack=ctx):
            return stack.enter_context(nc.sbuf_tensor("sb_" + name, shape, dt))

        ones = sb("ones", [P, P])
        mod = sb("mod", [P, 9 * KT, 2])
        ng = sb("ng", [P, 3, KT, 2])
        fg = sb("fg", [P, KT])
        eps = sb("eps", [P, 1])
        unused = sb("unused", [P, 1])
        convw = sb("convw", [P, RGT, 4])
        convb = sb("convb", [P, RGT])
        gbias = sb("gbias", [P, RGT, 2, 2])
        glam = sb("glam", [P, 2, RGT * 2])
        h0 = sb("h0", [P, RGT, 2])
        subg = sb("subg", [P, 1])
        hout = sb("hout", [P, RGT, 2])
        lnorm = sb("lnorm", [P, 32])
        raw = sb("raw", [P, SLOTS, 1024])
        x = sb("x", [P, KT, T])
        tmp = sb("tmp", [P, 4, CH])
        rstd = sb("rstd", [P, CH])
        quart = sb("quart", [P, CH // 4])
        rows = sb("rows", [P, 4])
        acts = ExitStack()
        with ExitStack() as s:
            stage = [sb(f"stage{b}", [P, 4, 1024], F32, s) for b in range(4)]
        hH = sb("hH", [P, KT, T], F32R, acts)
        hL = sb("hL", [P, KT, T], F32R, acts)
        with ExitStack() as s:
            stage.append(sb("stage4", [P, 4, 1024], F32, s))
            sb("first_gu", [P, 2, 2, 1024], F32, s)
            stage += [sb(f"stage{b}", [P, 4, 1024], F32, s) for b in (5, 6)]
        with ExitStack() as s:
            guH, guL = [None, None], [None, None]
            for f in (1, 0):
                guH[f] = sb(f"guH{f}", [P, 2, KT, P], F32R, s)
                guL[f] = sb(f"guL{f}", [P, 2, KT, P], F32R, s)
            dnH = sb("dnH", [P, 2, D], F32R, s)
            dnL = sb("dnL", [P, 2, D], F32R, s)
            hidH = sb("hidH", [P, 2, T], F32R, s)
            hidL = sb("hidL", [P, 2, T], F32R, s)
            modp = sb("modp", [P, 512], F32, s)
            cs = sb("cs", [P, KT, 32], F32, s)
            cin = sb("cin", [P, KT, 2], F32, s)
            sel = sb("sel", [P, 2], F32, s)
            bmod = sb("bmod", [P, 9 * KT, 2], F32, s)
        mid = ExitStack()
        wiH = sb("wiH", [P, 2, 1024], F32R, mid)
        wiL = sb("wiL", [P, 2, 1024], F32R, mid)
        v = sb("v", [P, T // P, 512], F32, mid)
        xr = sb("xr", [P, RGT, T], F32, mid)
        with ExitStack() as s:
            xg = sb("xg", [P, RGT, T], F32, s)
        with ExitStack() as s:
            cosT = sb("cosT", [P, LAT], F32, s)
            sinT = sb("sinT", [P, LAT], F32, s)
            swp = sb("swp", [P, LAT], F32, s)
            vc = sb("vc", [P, 512], F32, s)
            kc = sb("kc", [P, NH, P], F32, s)
            ident = sb("ident", [P, P], F32, s)
            dl = sb("dl", [P, 4, DH], F32, s)
            mx = sb("mx", [P, 2, 2], F32, s)
            nmx = sb("nmx", [P, 2, 2], F32, s)
            sums = sb("sums", [P, 3, 2], F32, s)
            rec = sb("rec", [P, 3, 2], F32, s)
            coef = sb("coef", [P, 3], F32, s)
            ss = sb("ss", [P, NH, 9], F32, s)
            lams = sb("lams", [P, 4], F32, s)
            nlam = sb("nlam", [P, 1], F32, s)
        mid.close()
        acts.close()
        with ExitStack() as s:
            qH = sb("qH", [P, T], F32R, s)
            qL = sb("qL", [P, T], F32R, s)
            kH = sb("kH", [P, KEYS], F32R, s)
            kL = sb("kL", [P, KEYS], F32R, s)
            vHL = sb("vHL", [P, KEYS // P, 2, P], F32R, s)
            pr = sb("pr", [P, 2, 2, T], F32, s)
            pr0 = sb("pr0", [P, 2, CTX], F32, s)
            pTH = sb("pTH", [P, 19, P], F32R, s)
            pTL = sb("pTL", [P, 19, P], F32R, s)
        xd = nc.dram_tensor("x_spilled", [KT, P, T], F32, kind="Internal").ap()
        ps = ctx.enter_context(nc.psum_tensor("ps", [P, 8, 512], F32))

        smalls = sem("smalls")
        cons = sem("cons")
        xin = [sem(f"xin{c}") for c in range(NC)]
        staged = [sem(f"staged{b}") for b in range(PRE)]
        raw_full = [sem(f"raw_full{s}") for s in range(SLOTS)]
        raw_used = [sem(f"raw_used{s}") for s in range(SLOTS)]
        rl_in = sem("rl_in")
        rl_exp = sem("rl_exp")
        table = sem("table")
        c_ready = sem("c_ready")
        mod_prod = sem("mod_prod")
        mod_copy = sem("mod_copy")
        mod_sum = sem("mod_sum")
        mod_done = sem("mod_done")
        step = sem("step")
        nrm = [{n: sem(f"{n}_{z}") for n in
                ("sq",
                 "sq_used",
                 "sd",
                "rd",
                "bc",
                "rs",
                 "hf",
                 "hi", "h")}
               for z in range(4)]
        ffn = [{n: sem(f"{n}_{z}") for n in
                ("g", "u",
                 "silu",
                 "prod",
                 "hidhi", "hidlo",
                 "d",
                 "x")}
               for z in range(2)]
        w_hi = sem("w_hi")
        spilled = sem("spilled")
        gw_in = sem("gw_in")
        m_ready = sem("m_ready")
        m_ev = sem("m_ev")
        v_ready = sem("v_ready")
        v_ev = sem("v_ev")
        xc_ready = sem("xc_ready")
        gate_ready = sem("gate_ready")
        gate_ev = sem("gate_ev")
        rg_a = sem("rg_a")
        rg_e = sem("rg_e")
        rg_m = sem("rg_m")
        rg_s = sem("rg_s")
        rg_y = sem("rg_y")
        gelu = sem("gelu")
        rg_out = sem("rg_out")
        acst = sem("acst")
        outs = sem("outs")
        lam_p = sem("lam_p")
        lam_e = sem("lam_e")
        swapped = sem("swapped")
        roped = sem("roped")
        last_rope = sem("last_rope")
        pp_hi = sem("pp_hi")
        pp_lo = sem("pp_lo")
        pp_pool = sem("pp_pool")
        s_ready = sem("s_ready")
        mx_ready = sem("mx_ready")
        e_done = sem("e_done")
        pd_ready = sem("pd_ready")
        t_ready = sem("t_ready")
        t_hi = sem("t_hi")
        t_lo = sem("t_lo")
        o_ready = sem("o_ready")
        o_half = sem("o_half")
        o_done = sem("o_done")
        o_ss = sem("o_ss")
        o_sd = sem("o_sd")
        o_rec = sem("o_rec")
        o_nrm_pool = sem("o_nrm_pool")
        o_nrm = sem("o_nrm")
        ot_ready = sem("ot_ready")
        mix_hi = sem("mix_hi")
        mix_lo = sem("mix_lo")
        xback = sem("xback")
        w_ready = sem("w_ready")
        w_x = sem("w_x")
        y_done = sem("y_done")
        passed = [sem(f'passed{e}') for e in range(2)]
        y_out = sem("y_out")

        ssf = ss[:].rearrange("p h t -> p (h t)")

        def probs(t, m):
            return pr0[:, m] if t == 0 else pr[:, t % 2, m]

        gw = tmp[:].rearrange("p a b -> p (a b)")[:, 0:1024]
        SMALLS = ((cin[:], "c"), (bmod[:], "bmod"), (ng[:], "ng"), (fg[:], "fg"), (convw[:], "convw"),
                  (convb[:], "convb"), (gbias[:], "gbias"), (glam[:, 0], "glam"), (h0[:], "h0"),
                  (subg[:], "subg"), (sel[:], "sel"))
        N_SMALL = 16 * len(SMALLS)
        N_ACST = 16 * 6
        FIRST = {"g0": 3, "u0": 4}
        F1 = {"m0": (0, 0), "m1": (1, 0), "m2": (2, 0), "m3": (3, 0), "g1": (4, 0),
              "u1": (0, 1), "d0": (1, 1), "d1": (2, 1), "g0": (3, 1), "u0": (4, 1)}
        F2 = {"g1": (0, 0), "u1": (1, 0), "d0": (2, 0), "d1": (0, 1), "g0": (1, 1), "u0": (2, 1)}
        used_f1 = [0, 0, 0, 1, 1]
        used_in = [2 * NG, 2 * NG, 2 * NG, 2 * NG, 2 * NG]
        used_wo = [used_in[0] + 8, used_in[1] + 8, used_in[2] + 2, used_in[3] + 2, used_in[4]]
        used_f2 = [used_wo[0] + 4, used_wo[1] + 4, used_wo[2]]

        def nth(z, item, i):
            slot, j = (F1, F2)[z][item]
            base = used_f1[slot] if z == 0 else used_f2[slot] + (slot > 0)
            return slot, i * 2 + (base + j)

        def stats_bank(z, c):
            return 4 + c if z == 0 else 7

        def mod_bank(b):
            return 6 if isinstance(b, int) and b in (1, 3) else 7

        def gate_bank(f, c, first):
            b = (f * NC + c) % 2
            return (4, 5) if first and (f, c) == (0, 2) else (b, 2 + b)

        def first(z, item):
            if z == 0:
                return FIRST[item], 0
            slot = {"g0": 1, "u0": 2}[item]
            return slot, used_f2[slot]

        whi_in = 2 + 6 * NG - 2
        whi_wo = whi_in + 20

        blk = ctx.enter_context(nc.Block())


        def alone(eng):
            eng.sem_inc(passed[eng is nc.vector], 1)

        @blk.sync
        def _(sp):
            def load_raw(slot, n, src):
                sp.wait_ge(raw_used[slot], n + 1)
                sp.dma_start(raw[:, slot], src).then_inc(raw_full[slot], 16)

            def ffn_loads(z, i, last):
                if z == 0:
                    for q in range(4):
                        load_raw(*nth(z, f"m{q}", i), a["w_mod"][i + PRE, q])
                load_raw(*nth(z, "g1", i), a["w_gate"][i * 2 + (z * FT + 1)])
                load_raw(*nth(z, "u1", i), a["w_up"][i * 2 + (z * FT + 1)])
                load_raw(*nth(z, "d0", i), a["w_down"][i * 2 + z * FT])
                load_raw(*nth(z, "d1", i), a["w_down"][i * 2 + (z * FT + 1)])
                if not last:
                    load_raw(*nth(z, "g0", i), a["w_gate"][i * 2 + (z * FT + 2)])
                    load_raw(*nth(z, "u0", i), a["w_up"][i * 2 + (z * FT + 2)])

            def x_load(c):
                sp.dma_start(x[:, :, chunk(c)], a["x"].rearrange("k p t -> p k t")[:, :, chunk(c)]).then_inc(xin[c], 16)

            x_load(0)
            x_load(1)
            for dst, name in SMALLS:
                sp.dma_start(dst, a[name]).then_inc(smalls, 16)
            for b in range(PRE):
                if b == 4:
                    load_raw(*first(0, "g0"), a["w_gate"][0])
                    load_raw(*first(0, "u0"), a["w_up"][0])
                    x_load(2)
                sp.dma_start(stage[b][:], a["w_mod"][b].rearrange("q p n -> p q n")).then_inc(staged[b], 16)
            with sp.Fori(0, NG - 1) as i:
                ffn_loads(0, i, False)
            ffn_loads(0, NG - 1, True)
            load_raw(0, used_in[0], a["w_in"][0])
            load_raw(1, used_in[1], a["w_in"][1])
            sp.wait_ge(ffn[0]["x"], 3 + NG * NC * KT)
            for k in range(KT):
                sp.dma_start(xd[k], x[:, k]).then_inc(spilled, 16)
            sp.wait_ge(nrm[1]["h"], NC * KT)
            sp.dma_start(gw, a["gw"]).then_inc(gw_in, 16)
            for e in range(2, 8):
                load_raw(e % 2, used_in[e % 2] + e // 2, a["w_in"][e])
            for n in range(4):
                load_raw(2 + n % 2, used_in[2 + n % 2] + n // 2, a["w_v"][n])
            load_raw(0, used_in[0] + 4, a["w_in"][8])
            load_raw(1, used_in[1] + 4, a["w_in"][9])
            sp.wait_ge(rg_out, RGT)
            sp.dma_start(out["h"], hout[:]).then_inc(outs, 16)
            for dst, name in ((cosT, "cos"), (sinT, "sin"), (vc, "vc"), (ident, "ident")):
                sp.dma_start(dst[:], a[name]).then_inc(acst, 16)
            sp.dma_start(kc[:], a["kc"].rearrange("h p t -> p h t")).then_inc(acst, 16)
            sp.dma_start(dl[:].rearrange("p a b -> p (a b)"), a["dl"].partition_broadcast(P)).then_inc(acst, 16)
            with sp.Fori(0, 3) as i:
                for f in range(2):
                    load_raw(f, i + (used_in[f] + 5), a["w_in"][i * 2 + (10 + f)])
            sp.wait_ge(v_ev, 18)
            sp.dma_start(out["v"], v[:, 0]).then_inc(outs, 16)
            sp.wait_ge(m_ev, 6 + 16 * NC)
            sp.dma_start(out["k"].rearrange("h p t -> p h t"), x[:, 4:8, 0:CTX]).then_inc(outs, 16)
            load_raw(0, used_wo[0], a["w_out"][0])
            load_raw(1, used_wo[1], a["w_out"][1])
            sp.wait_ge(outs, 48)
            sp.wait_ge(spilled, 16 * KT)
            sp.wait_ge(pp_lo, NH * 2)
            sp.wait_ge(pp_pool, (NH - 1) * 3 + 1)
            for k in range(KT):
                sp.dma_start(x[:, k], xd[k]).then_inc(xback, 16)
            with sp.Fori(0, 3) as i:
                for f in range(2):
                    load_raw(f, i + (used_wo[f] + 1), a["w_out"][i * 2 + (2 + f)])
            load_raw(*first(1, "g0"), a["w_gate"][FT])
            load_raw(*first(1, "u0"), a["w_up"][FT])
            with sp.Fori(0, NG - 1) as i:
                ffn_loads(1, i, False)
            ffn_loads(1, NG - 1, True)
            for c in range(NC):
                for k in range(KT):
                    sp.wait_ge(y_done, c * KT + k + 1)
                    sp.dma_start(out["y"][k, :, chunk(c)], x[:, k, chunk(c)]).then_inc(y_out, 16)
            sp.wait_ge(y_out, 16 * NC * KT)

        @blk.gpsimd
        def _(pool):
            xt = x[:, KT - 1, CTX:T]
            pool.wait_ge(acst, N_ACST)
            pool.wait_ge(swapped, 1)
            pool.tensor_tensor(xt, xt, cosT[:], ALU.mult).then_inc(last_rope, 1)
            pool.tensor_tensor(swp[:], swp[:], sinT[:], ALU.mult).then_inc(last_rope, 1)
            pool.wait_ge(last_rope, 2)
            pool.tensor_tensor(xt, xt, swp[:], ALU.add).then_inc(last_rope, 1)
            def split_v(h):
                at = bass.ds(h * P, P)
                pool.wait_ge(pp_hi, h * 5 + 4)
                pool.tensor_tensor(vHL[:, 0:9, 1], v[:, :, at], vHL[:, 0:9, 0].bitcast(F32),
                                   ALU.subtract).then_inc(pp_pool, 1)
                pool.wait_ge(pp_hi, h * 5 + 5)
                pool.tensor_tensor(vHL[:, 9, 1], vc[:, at], vHL[:, 9, 0].bitcast(F32),
                                   ALU.subtract).then_inc(pp_pool, 1)

            split_v(0)
            with pool.Fori(1, NH) as h:
                pool.wait_ge(pp_hi, h * 5 + 1)
                pool.tensor_tensor(kL[:, 0:T], x[:, h + 4], kH[:, 0:T].bitcast(F32), ALU.subtract).then_inc(pp_pool, 1)
                split_v(h)
            pool.wait_ge(o_rec, 1)
            for c in range(NC):
                for hd in range(NH - 1):
                    for t in range(3 * c, 3 * c + 3):
                        o = v[:, t, hd * P:(hd + 1) * P]
                        m = pool.tensor_scalar(o, o, ss[:, hd, t:t + 1], None, ALU.mult)
                    m.then_inc(o_nrm_pool, 1)
            for e in range(2):
                pool.wait_ge(w_hi, whi_wo + e + 1)
                pool.tensor_tensor(wiL[:, e], raw[:, e], wiH[:, e].bitcast(F32), ALU.subtract).then_inc(raw_used[e], 1)

        @blk.tensor
        def _(pe):
            for z in range(2):
                pe.sem_inc(ffn[z]["u"], 6)
                pe.sem_inc(ffn[z]["d"], 24)

            def three(o, wH, wL, xH, xL, begin, end):
                pe.matmul(o, wH, xH, start=begin, stop=False)
                pe.matmul(o, wH, xL, start=False, stop=False)
                return pe.matmul(o, wL, xH, start=False, stop=end)

            def stats(z, c, tiles=range(KT)):
                for k in tiles:
                    pe.wait_ge(nrm[z]["sq"], c * KT + k + 1)
                    if k == 0 and c > 0 and z > 0:
                        pe.wait_ge(nrm[z]["rs"], c)
                    for q in range(4):
                        m = pe.matmul(ps[32 * q:32 * q + 32, stats_bank(z, c), 0:CH // 4], ones[:, 0:32],
                                      tmp[:, k % 2, q * CH // 4:(q + 1) * CH // 4], start=k == 0, stop=k == KT - 1,
                                      tile_position=(0, 32 * q))
                    m.then_inc(nrm[z]["sq_used"], 1)

            def spread(z, c):
                pe.wait_ge(nrm[z]["rd"], c + 1)
                pe.matmul(ps[:, stats_bank(z, c), 0:CH], ones[:], tmp[:, 0], start=True,
                          stop=True).then_inc(nrm[z]["bc"], 1)

            def mod_partial(src, used, bank=7):
                for kk in range(2):
                    for q in range(4):
                        m = pe.matmul(ps[32 * q:32 * q + 32, bank, :], cs[:, 2 * q + kk, :], src[:, q, kk * 512:(kk + 1) * 512],
                                      start=kk == 0, stop=kk == 1, tile_position=(0, 32 * q))
                        if kk == 1 and q == 3:
                            m.then_inc(mod_prod, 1)
                        elif kk == 1 and used:
                            m.then_inc(raw_used[q], 1)

            def mod_total(bank=7):
                for n in range(4):
                    m = pe.matmul(ps[:, bank, 2 * n:2 * n + 2], modp[:, n * P:(n + 1) * P], sel[:], start=True, stop=True)
                m.then_inc(mod_sum, 1)

            def mod_first(b):
                if b < PRE:
                    pe.wait_ge(staged[b], 16)
                else:
                    mod_raw_full(b - PRE)
                if b > 1:
                    pe.wait_ge(mod_done, b - 1 if b < 4 else b)
                mod_partial(stage[b] if b < PRE else raw, b >= PRE, mod_bank(b))

            def mod_last(b):
                pe.wait_ge(mod_copy, b + 1)
                mod_total(mod_bank(b))

            def mod_raw_full(i):
                for q in range(4):
                    slot, n = nth(0, f"m{q}", i)
                    pe.wait_ge(raw_full[slot], n * 16 + 16)

            pe.wait_ge(cons, 1)
            for c in range(2):
                stats(0, c)
            pe.wait_ge(c_ready, 1)
            pe.wait_ge(smalls, N_SMALL)
            for b in range(4):
                mod_first(b)
                if b:
                    mod_last(b - 1)
            mod_last(3)
            spread(0, 0)

            def ffn_pe(z, i, between=None):
                s = ffn[z]
                last = isinstance(i, int) and i == NG - 1
                with_mod = z == 0 and between is None
                if with_mod:
                    mod_raw_full(i)
                    pe.wait_ge(mod_done, i + PRE)
                    mod_partial(raw, True)
                for f in range(2):
                    for c in range(NC):
                        gb, ub = gate_bank(f, c, between is not None)
                        o = i * 6 + (f * NC + c)

                        def weights_split(w):
                            if c == 0:
                                slot, n = nth(z, f"{w}{f}", i)
                                pe.wait_ge(raw_used[slot], n + 2 if f else n)

                        weights_split("g")
                        if gb != 4:
                            pe.wait_ge(s["silu"], o + 1)
                        if between is None or f:
                            pe.wait_ge(nrm[2 * z]["h"], (c + 1) * KT)
                        for k in range(KT):
                            if between is not None and f == 0:
                                pe.wait_ge(nrm[2 * z]["h"], c * KT + k + 1)
                            m = three(ps[:, gb, 0:CH], guH[f][:, 0, k], guL[f][:, 0, k], hH[:, k, chunk(c)],
                                      hL[:, k, chunk(c)], k == 0, k == KT - 1)
                            if k == KT - 1:
                                m.then_inc(s["g"], 1)
                            if between is not None and f == 0:
                                if c == 1:
                                    stats(2 * z, 2, (k,))
                                elif (z, c, k) == (1, 0, 2):
                                    spread(2, 1)
                        if between is not None:
                            between(f, c, 0)
                        weights_split("u")
                        if ub != 5:
                            pe.wait_ge(s["prod"], o + 1)
                        for k in range(KT):
                            m = three(ps[:, ub, 0:CH], guH[f][:, 1, k], guL[f][:, 1, k], hH[:, k, chunk(c)],
                                      hL[:, k, chunk(c)], k == 0, k == KT - 1)
                            if k == KT - 1:
                                m.then_inc(s["u"], 1)
                            if between is not None and f == 0:
                                if (z, c, k) == (0, 0, 1):
                                    spread(0, 1)
                                elif (c, k) == (1, 4):
                                    spread(2 * z, 2)
                        if with_mod and f == 0 and c == 0:
                            pe.wait_ge(mod_copy, i + (PRE + 1))
                            mod_total()
                        if between is not None:
                            between(f, c, 1)
                for w in ("d0", "d1"):
                    slot, n = nth(z, w, i)
                    pe.wait_ge(raw_used[slot], n + 2)
                for c in range(NC):
                    pe.wait_ge(s["hidlo"], i * 6 + (6 + c))
                    for t in range(KT):
                        pe.wait_ge(s["x"], i * 24 + (c * KT + t + 1))
                        for f in range(2):
                            m = three(ps[:, 4 + (c * KT + t) % 3, 0:CH], dnH[:, f, t * P:(t + 1) * P],
                                      dnL[:, f, t * P:(t + 1) * P], hidH[:, f, chunk(c)], hidL[:, f, chunk(c)],
                                      f == 0, f == 1)
                        m.then_inc(s["d"], 1)
                        if last and c == 1:
                            if z == 0 and t == 0:
                                pe.wait_ge(mod_done, NB_MOD)
                            stats(2 * z + 1, 0, (t,))
                        if last and c == 2:
                            if t == 1:
                                spread(2 * z + 1, 0)
                            if t > 1:
                                stats(2 * z + 1, 1, (t - 2,) if t < KT - 1 else (t - 2, t - 1, t))

            FIRST_MODS = {(0, 0, 1): (4, None), (0, 1, 0): (5, 4), (0, 1, 1): (6, 5), (0, 2, 0): (None, 6),
                          (0, 2, 1): (PRE, None), (1, 0, 0): (None, PRE)}

            def first_mods(f, c, w):
                start, end = FIRST_MODS.get((f, c, w), (None, None))
                if end is not None:
                    mod_last(end)
                if start is not None:
                    mod_first(start)

            ffn_pe(0, 0, first_mods)
            with pe.Fori(1, NG - 1) as i:
                ffn_pe(0, i)
            ffn_pe(0, NG - 1)

            def in_chunk(e, c, o, slot_n):
                f = e % 2 if isinstance(e, int) else e[1]
                b = o % 6 if isinstance(o, int) else f * NC + c
                pe.wait_ge(raw_used[f], slot_n + 2)
                pe.wait_ge(m_ev, o + 1)
                for k in range(KT):
                    if e == 0:
                        pe.wait_ge(nrm[1]["h"], c * KT + k + 1)
                    m = three(ps[:, b, 0:CH], wiH[:, f, k * P:(k + 1) * P], wiL[:, f, k * P:(k + 1) * P],
                              hH[:, k, chunk(c)], hL[:, k, chunk(c)], k == 0, k == KT - 1)
                    if k == KT - 1:
                        m.then_inc(m_ready, 1)
                    if (e, c, k) == (0, 0, 2):
                        spread(1, 1)
                    elif (e, c) == (0, 1):
                        stats(1, 2, (k,))
                    elif (e, c, k) == (1, 1, 4):
                        spread(1, 2)

            def gates(j):
                pe.wait_ge(xc_ready, j + 1)
                for n in range(12):
                    c, g = n % NC, n // NC
                    w = slice((j * 4 + g) * DH, (j * 4 + g + 1) * DH)
                    if j * 12 + n >= 2:
                        pe.wait_ge(gate_ev, j * 12 + n - 1)
                    for r in (slice(0, DH), slice(DH, P)):
                        m = pe.matmul(ps[r, 6 + n % 2, 0:CH], gw[r, w], x[r, XC[j % 2], chunk(c)], start=True, stop=True,
                                      tile_position=(r.start, r.start))
                    m.then_inc(gate_ready, 1)

            for c in range(NC):
                for f in range(2):
                    in_chunk(f, c, 2 * c + f, used_in[f])
            for e in range(2, 4):
                for c in range(NC):
                    in_chunk(e, c, e * NC + c, e // 2 + used_in[e % 2])
            pe.wait_ge(gw_in, 16)
            for j in range(2):
                gates(j)
                for e in (4 + 2 * j, 5 + 2 * j):
                    for c in range(NC):
                        in_chunk(e, c, e * NC + c, e // 2 + used_in[e % 2])
            for hf in range(2):
                gates(2 + hf)
                pe.wait_ge(m_ev, 6 + 24)
                for kk in range(2):
                    pe.wait_ge(raw_used[2 + kk], used_in[2 + kk] + hf + 2)
                for t in range(T // P):
                    n = hf * 9 + t
                    if n >= 6:
                        pe.wait_ge(v_ev, n - 5)
                    tk = slice(t * P, (t + 1) * P)
                    for k in range(KT):
                        wv = slice((k % 4) * 256, (k % 4 + 1) * 256)
                        m = three(ps[:, n % 6, 0:256], hH[:, k, tk], hL[:, k, tk], wiH[:, k // 4, wv], wiL[:, k // 4, wv],
                                  k == 0, k == KT - 1)
                    m.then_inc(v_ready, 1)
            pe.wait_ge(v_ev, 18)
            with pe.Fori(0, 4) as i:
                for f in range(2):
                    for c in range(NC):
                        in_chunk((i, f), c, i * 6 + (24 + f * NC + c), i + (used_in[f] + 4))

            def scores(q, m):
                k0, k1 = (0, CTX) if q == 0 else (CTX, KEYS)
                r = slice(m * DH, (m + 1) * DH)
                for c in range(-(-(k1 - k0) // CH)):
                    w = min(CH, k1 - k0 - c * CH)
                    kk = slice(k0 + c * CH, k0 + c * CH + w)
                    for j, (A, B) in enumerate(((qH, kH), (qH, kL), (qL, kH))):
                        mm = pe.matmul(ps[:, 3 * m + c, 0:w], A[r, q * P:(q + 1) * P], B[r, kk],
                                       start=j == 0, stop=j == 2, tile_position=(m * DH, 0))
                mm.then_inc(s_ready, 1)

            def group(head, t, g):
                if 3 * g >= KEY_TILES[t]:
                    return
                if g == 0:
                    pe.wait_ge(pd_ready, count(head, 9, t + 1))
                pe.wait_ge(t_lo, count(head, GROUPS, GROUP0[t] + g + 1))
                for k in range(3 * g, min(3 * g + 3, KEY_TILES[t])):
                    m = pe.transpose(ps[:, 6, (k % 3) * P:(k % 3 + 1) * P], probs(t, 0)[:, k * P:(k + 1) * P], ident[:])
                m.then_inc(t_ready, 1)

            def values(head, t, part):
                nk = KEY_TILES[t]
                if part == 0:
                    pe.wait_ge(t_lo, count(head, GROUPS, GROUP0[t + 1] + 1))
                    pe.wait_ge(o_done, count(head, 9, t + 2))
                for k in range(5 * part, min(5 + 4 * part, nk)):
                    rhs = vHL[:, 0 if t == 0 else 1 + k].rearrange("p a b -> p (a b)")
                    pe.matmul(ps[:, 7, 0:256], pTH[:, pt_at(t) + k], rhs, start=k == 0, stop=False)
                    m = pe.matmul(ps[:, 7, 0:256], pTL[:, pt_at(t) + k], rhs, start=False, stop=k == nk - 1)
                    if k == nk - 1:
                        m.then_inc(o_ready, 1)

            def attend(h, n, with_scores, before):
                def both_maps():
                    for m in range(2):
                        if n > 0 or before:
                            pe.wait_ge(e_done, count((h, 0), 18, 2 * n + m - 1))
                        scores(n, m)

                if n > 0:
                    both_maps()
                for g in range(3):
                    if n == 0 and with_scores and g == 2:
                        pe.wait_ge(pp_pool, h * 3 + 1)
                        pe.wait_ge(pp_lo, h * 2 + 2)
                        both_maps()
                    if n > 0 or before:
                        group(*tile_of(h, n - 1), g)
                    if g < 2 and (n > 1 or before):
                        if n == 2 and g == 0:
                            pe.wait_ge(pp_pool, h * 3 + 3)
                        values(*tile_of(h, n - 2), g)

            def head(h, before):
                for n in range(9):
                    attend(h, n, True, before)

            pe.wait_ge(m_ev, 6 + 48)
            pe.wait_ge(acst, N_ACST)
            head(0, False)
            with pe.Fori(1, NH) as h:
                head(h, True)
            for n in range(2):
                if n == 0:
                    attend(NH, n, False, True)
                else:
                    for part in range(2):
                        values(*tile_of(NH, n - 2), part)

            def out_chunk(i, c, between=None):
                for f in range(2):
                    pe.wait_ge(raw_used[f], i + (used_wo[f] + 2))
                    pe.wait_ge(w_x, i * 6 + (c * 2 + f + 1))
                    for n, k in enumerate(MIX_ORDER):
                        if isinstance(i, int) and i == 0:
                            pe.wait_ge(mix_lo, c * KT + n + 1)
                        m = three(ps[:, f * NC + c, 0:CH], wiH[:, f, k * P:(k + 1) * P], wiL[:, f, k * P:(k + 1) * P],
                                  hH[:, k, chunk(c)], hL[:, k, chunk(c)], n == 0, n == KT - 1)
                        if n == KT - 1:
                            m.then_inc(w_ready, 1)
                        if between is not None:
                            between(f * KT + n)

            def outputs(c, hd):
                n = c * NH + hd
                if hd < NH - 1:
                    pe.wait_ge(o_nrm_pool, c * (NH - 1) + hd + 1)
                else:
                    pe.wait_ge(o_nrm, c + 1)
                if n >= 2:
                    pe.wait_ge(mix_lo, (n - 2) // NH * KT + RGT + (n - 2) % NH + 1)
                for k in range(3):
                    m = pe.transpose(ps[:, 6 + n % 2, k * P:(k + 1) * P], v[:, c * 3 + k, hd * P:(hd + 1) * P], ident[:])
                m.then_inc(ot_ready, 1)

            pe.wait_ge(o_done, 2 + 9 * NH)
            for hd in range(NH):
                outputs(0, hd)
            for c in range(NC):
                out_chunk(0, c, lambda n: outputs(c + 1, n // 4) if n % 4 == 1 and c + 1 < NC else None)
            with pe.Fori(0, 2) as i:
                for c in range(NC):
                    out_chunk(i + 1, c)
            out_chunk(3, 0)
            out_chunk(3, 1, lambda n: stats(2, 0, (n // 2,)) if n % 2 else None)

            def last_chunk(n):
                if n == 3:
                    spread(2, 0)
                elif n > 3 and n % 2:
                    stats(2, 1, (n // 2 - 2,) if n < 2 * KT - 1 else (KT - 3, KT - 2, KT - 1))

            out_chunk(3, 2, last_chunk)
            ffn_pe(1, 0, lambda f, c, w: None)
            with pe.Fori(1, NG - 1) as i:
                ffn_pe(1, i)
            ffn_pe(1, NG - 1)
            spread(3, 1)
            stats(3, 2)
            spread(3, 2)

        @blk.scalar
        def _(act):
            for z in range(2):
                act.sem_inc(ffn[z]["silu"], 2)
            act.sem_inc(m_ev, 6)
            act.sem_inc(o_ss, 1)

            def cast(dst, slot, n, free=None):
                act.wait_ge(raw_full[slot], n * 16 + 16)
                if free is not None:
                    act.wait_ge(*free)
                act.activation(dst, raw[:, slot], ACT.Copy).then_inc(w_hi, 1)

            def squares(z, c, ready, tiles=range(KT)):
                s = nrm[z]
                for k in tiles:
                    act.wait_ge(*ready(c, k))
                    n = c * KT + k
                    if n >= 2:
                        act.wait_ge(s["sq_used"], n - 1)
                    act.activation(tmp[:, k % 2], x[:, k, chunk(c)], ACT.Square).then_inc(s["sq"], 1)

            def root(z, c):
                s = nrm[z]
                act.wait_ge(s["sq_used"], (2 if z == 0 and c == 0 else c + 1) * KT)
                act.activation(quart[:], ps[:, stats_bank(z, c), 0:CH // 4], ACT.Sqrt, bias=eps[:, 0:1]).then_inc(s["sd"], 1)
                act.wait_ge(s["bc"], c + 1)
                if c > 0:
                    act.wait_ge(s["h"], c * KT)
                act.activation(rstd[:], ps[:, stats_bank(z, c), 0:CH], ACT.Copy).then_inc(s["rs"], 1)

            def h_hi(z, c, tiles=range(KT)):
                s = nrm[z]
                for k in tiles:
                    act.wait_ge(s["hf"], c * KT + k + 1)
                    for cond, b, e in conds(c):
                        m = act.activation(hH[:, k, b:e], tmp[:, 2 + k % 2, b - c * CH:e - c * CH], ACT.Identity,
                                           bias=mod[:, 3 * z * KT + k, cond:cond + 1])
                    m.then_inc(s["hi"], 1)

            def load_root():
                act.activation(unused[:], eps[:, 0:1], ACT.Sqrt).then_inc(table, 1)

            def norm(z, ready):
                load_root()
                squares(z, 0, ready)
                root(z, 0)
                for k in range(KT):
                    if z < 3:
                        h_hi(z, 0, (k,))
                    squares(z, 1, ready, (k,))
                root(z, 1)
                for k in range(KT):
                    if z < 3:
                        h_hi(z, 1, (k,))
                    squares(z, 2, ready, (k,))
                root(z, 2)
                if z < 3:
                    h_hi(z, NC - 1)

            def mod_evac(b, used):
                act.wait_ge(mod_prod, b + 1)
                if used:
                    act.sem_inc(raw_used[3], 1)
                if isinstance(b, int) and 0 < b < 4:
                    act.wait_ge(mod_sum, b)
                act.activation(modp[:], ps[:, mod_bank(b), :], ACT.Copy).then_inc(mod_copy, 1)

            act.wait_ge(cons, 3)
            squares(0, 0, lambda c, k: (xin[c], 16))
            act.wait_ge(smalls, N_SMALL)
            act.activation(cs[:, :, 0:2], cin[:], ACT.Silu).then_inc(c_ready, 1)
            act.wait_ge(rl_in, 1)
            act.activation(lnorm[:, 8:16], lnorm[:, 0:8], ACT.Exp).then_inc(rl_exp, 1)
            squares(0, 1, lambda c, k: (xin[c], 16))
            load_root()
            for b in range(4):
                if b == 3:
                    for j, w in enumerate(("g0", "u0")):
                        cast(guH[0][:, j].rearrange("p k n -> p (k n)"), *first(0, w))
                mod_evac(b, False)
            root(0, 0)
            h_hi(0, 0)
            root(0, 1)
            for k in range(KT):
                h_hi(0, 1, (k,))
                squares(0, 2, lambda c, k: (xin[c], 16), (k,))
            mod_evac(4, False)
            root(0, 2)
            mod_evac(5, False)
            h_hi(0, 2, range(5))
            mod_evac(6, False)
            h_hi(0, 2, range(5, 8))

            def ffn_act(z, i, last, first=False):
                with_mod = not (first and z == 0)
                s = ffn[z]

                def hidden(f, c):
                    o = i * 6 + (f * NC + c)
                    b = (f * NC + c) % 2
                    act.wait_ge(s["g"], o + 1)
                    act.wait_ge(s["prod"], o + 1)
                    act.activation(tmp[:, b], ps[:, gate_bank(f, c, first)[0], 0:CH], ACT.Silu).then_inc(s["silu"], 1)
                    act.wait_ge(s["prod"], o + 3)
                    act.wait_ge(s["d"], i * 24 + 8 * (c + 1))
                    act.activation(hidH[:, f, chunk(c)], tmp[:, 2 + b], ACT.Copy).then_inc(s["hidhi"], 1)

                def gu1(j):
                    cast(guH[1][:, j].rearrange("p k n -> p (k n)"), *nth(z, "gu"[j] + "1", i), (s["u"], i * 6 + 6))

                if with_mod:
                    if z == 0:
                        mod_evac(i + PRE, True)
                    gu1(0)
                    gu1(1)
                    hidden(0, 0)
                else:
                    hidden(0, 0)
                    gu1(0)
                    hidden(0, 1)
                    mod_evac(PRE, True)
                    gu1(1)
                for j in range(2):
                    cast(dnH[:, j], *nth(z, f"d{j}", i), (s["d"], i * 24 + 24))
                if with_mod:
                    hidden(0, 1)
                hidden(0, 2)
                if not last:
                    for j, w in enumerate(("g0", "u0")):
                        cast(guH[0][:, j].rearrange("p k n -> p (k n)"), *nth(z, w, i), (s["u"], i * 6 + 9))
                for c in range(NC):
                    hidden(1, c)

            ffn_act(0, 0, False, True)
            with act.Fori(1, NG - 1) as i:
                ffn_act(0, i, False)
            ffn_act(0, NG - 1, True)
            act.wait_ge(ffn[0]["u"], 6 + NG * 6)
            for e in range(2):
                cast(wiH[:, e], e, used_in[e])
            norm(1, lambda c, k: (ffn[0]["x"], 3 + (NG - 1) * 24 + c * KT + k + 1))

            def in_evac(dst, o):
                act.wait_ge(m_ready, o + 1)
                act.activation(dst, ps[:, o % 6, 0:CH], ACT.Copy).then_inc(m_ev, 1)

            for c in range(NC):
                for f in range(2):
                    in_evac(xr[:, f, chunk(c)], 2 * c + f)
            for e in range(2, 4):
                cast(wiH[:, e % 2], e % 2, e // 2 + used_in[e % 2])
            for e in range(2, 4):
                for c in range(NC):
                    in_evac(xr[:, e, chunk(c)], e * NC + c)
                cast(wiH[:, e % 2], e % 2, e // 2 + 1 + used_in[e % 2])

            def v_evac(n):
                act.wait_ge(v_ready, n + 1)
                act.activation(v[:, n % 9, n // 9 * 256:(n // 9 + 1) * 256], ps[:, n % 6, 0:256],
                               ACT.Copy).then_inc(v_ev, 1)

            act.wait_ge(spilled, 16 * KT)
            act.wait_ge(nrm[1]["h"], NC * KT)
            for j in range(RGT):
                if j:
                    act.wait_ge(rg_y, j)
                for n in range(12):
                    c, g = n % NC, n // NC
                    act.wait_ge(gate_ready, j * 12 + n + 1)
                    act.activation(x[:, 1 + g, chunk(c)], ps[:, 6 + n % 2, 0:CH], ACT.Sigmoid,
                                   bias=gbias[:, j, g // 2, g % 2:g % 2 + 1]).then_inc(gate_ev, 1)
                act.wait_ge(gate_ev, j * 12 + 12)
                for d in range(2):
                    act.activation(x[:, 5 + d], x[:, 1 + 2 * d], ACT.Exp, scale=glam[:, 0, 2 * j + d:2 * j + d + 1]).then_inc(rg_a, 1)
                act.wait_ge(rg_a, 2 * j + 2)
                for d in range(2):
                    act.activation(x[:, 1 + 2 * d], x[:, 1 + 2 * d], ACT.Tanh,
                                   scale=glam[:, 1, 2 * j + d:2 * j + d + 1]).then_inc(rg_e, 1)

                def roots(j=j):
                    for d in range(2):
                        act.wait_ge(rg_m, 2 * j + d + 1)
                        act.activation(x[:, 1 + 2 * d], x[:, 1 + 2 * d], ACT.Sqrt).then_inc(rg_s, 1)

                if j < 2:
                    for e in (4 + 2 * j, 5 + 2 * j):
                        for c in range(NC):
                            in_evac(xg[:, e - 4, chunk(c)], e * NC + c)
                            if e % 2 == 0 and c == 1:
                                roots()
                        if e < 6:
                            cast(wiH[:, e % 2], e % 2, e // 2 + 1 + used_in[e % 2])
                        else:
                            cast(wiH[:, e - 6], e - 4, used_in[e - 4])
                else:
                    for t in range(9):
                        v_evac((j - 2) * 9 + t)
                        if t == 3:
                            roots()
                    for kk in range(2):
                        if j == 2:
                            cast(wiH[:, kk], 2 + kk, used_in[2 + kk] + 1)
                        else:
                            cast(wiH[:, kk], kk, used_in[kk] + 4)
            for j in range(RGT):
                act.activation(xg[:, j], xg[:, j], ACT.Gelu_apprx_tanh).then_inc(gelu, 1)
            act.wait_ge(rg_y, RGT)
            def qk_pair(i, last):
                for f in range(2):
                    for c in range(NC):
                        act.wait_ge(m_ready, i * 6 + (24 + f * NC + c + 1))
                        alone(act)
                        act.activation(x[:, i * 2 + f, chunk(c)], ps[:, f * NC + c, 0:CH], ACT.Copy).then_inc(m_ev, 1)
                    if not last:
                        cast(wiH[:, f], f, i + (used_in[f] + 5))
            with act.Fori(0, 3) as i:
                qk_pair(i, False)
            qk_pair(3, True)

            act.wait_ge(m_ev, 6 + 48)
            act.wait_ge(m_ready, 48)
            act.wait_ge(acst, N_ACST)
            act.wait_ge(lam_p, 1)
            act.activation(lams[:, 2:4], lams[:, 0:2], ACT.Exp).then_inc(lam_e, 1)

            def p_hi(head, t, g):
                w = min(3, KEY_TILES[t] - 3 * g)
                if w > 0:
                    act.wait_ge(t_ready, count(head, GROUPS, GROUP0[t] + g + 1))
                    at = pt_at(t) + 3 * g
                    act.activation(pTH[:, at:at + w].rearrange("p k n -> p (k n)"), ps[:, 6, 0:w * P],
                                   ACT.Copy).then_inc(t_hi, 1)

            def exps(h, n, m):
                act.wait_ge(mx_ready, h * 18 + (2 * n + m + 1))
                if n == 0:
                    src, dst = ps[:, 3 * m, 0:CTX], probs(0, m)
                else:
                    src = ps[:, 3 * m:3 * m + 3, 0:CH]
                    dst = probs(n, m).rearrange("p (c t) -> p c t", c=NC)
                act.activation(dst, src, ACT.Exp, bias=nmx[:, n % 2, m:m + 1],
                               accum_out=sums[:, n % 3, m:m + 1]).then_inc(e_done, 1)

            def split_k(hd):
                act.activation(kH[:, 0:T], x[:, hd + 4], ACT.Copy).then_inc(pp_hi, 1)
                act.activation(kH[:, T:KEYS], kc[:, hd], ACT.Copy).then_inc(pp_hi, 1)

            def split_q(hd):
                act.activation(qH[:], x[:, hd], ACT.Copy, scale=DH ** -0.5).then_inc(pp_hi, 1)

            def split_v(hd):
                act.activation(vHL[:, 0:9, 0], v[:, :, bass.ds(hd * P, P)], ACT.Copy).then_inc(pp_hi, 1)
                act.activation(vHL[:, 9, 0], vc[:, bass.ds(hd * P, P)], ACT.Copy).then_inc(pp_hi, 1)

            def out_half(head, t):
                act.wait_ge(o_ready, count(head, 9, t + 1))
                act.wait_ge(o_done, count(head, 9, t + 1))
                act.activation(tmp[:, t % 3, 0:P], ps[:, 7, 0:P], ACT.Copy, scale=rec[:, t % 3, 0:1]).then_inc(o_half, 1)

            def out_squares(head, t):
                act.wait_ge(o_done, count(head, 9, t + 3))
                act.wait_ge(o_ss, count(head, 9, t + 1))
                alone(act)
                act.activation(tmp[:, 3, 0:P], v[:, t, bass.ds(count(head, P, 0), P)], ACT.Square,
                               accum_out=ssf[:, bass.ds(count(head, 9, t), 1)]).then_inc(o_ss, 1)

            def attend(h, n, with_scores, before):
                if n == 0:
                    if with_scores:
                        split_k(h)
                    if before:
                        p_hi((h, -1), 8, 0)
                    if with_scores:
                        split_q(h)
                    if before:
                        p_hi((h, -1), 8, 1)
                        out_half((h, -1), 7)
                    if with_scores:
                        exps(h, 0, 0)
                    if before:
                        p_hi((h, -1), 8, 2)
                    if with_scores:
                        exps(h, 0, 1)
                else:
                    for m in range(2):
                        p_hi((h, 0), n - 1, m)
                        exps(h, n, m)
                    p_hi((h, 0), n - 1, 2)
                    if n > 1 or before:
                        out_half(*tile_of(h, n - 2))
                if n > 2 or before:
                    out_squares(*tile_of(h, n - 3))

            def head(h, before, last=False):
                for n in range(9):
                    attend(h, n, True, before)
                    if n == 1:
                        split_v(h)
                    if last and n == 3:
                        roots_of_outputs(0, NH - 1)
                    if last and n in (5, 6):
                        cast(wiH[:, n - 5], n - 5, used_wo[n - 5])

            def roots_of_outputs(h0_, h1):
                act.wait_ge(o_ss, 1 + h1 * 9)
                act.activation(ss[:, h0_:h1], ss[:, h0_:h1], ACT.Sqrt, bias=eps[:, 0:1], scale=1.0 / P).then_inc(o_sd, 1)

            act.wait_ge(roped, 1)
            head(0, False)
            act.wait_ge(last_rope, 3)
            with act.Fori(1, NH - 1) as h:
                head(h, True)
            head(NH - 1, True, True)
            attend(NH, 0, False, True)
            out_half((NH, -1), 8)
            for t in (7, 8):
                out_squares((NH, -1), t)

            roots_of_outputs(NH - 1, NH)
            for c in range(NC):
                for k in MIX_ORDER:
                    if k < NH:
                        n = c * NH + k
                        act.wait_ge(ot_ready, n + 1)
                        act.activation(hH[:, k, chunk(c)], ps[:, 6 + n % 2, 0:CH], ACT.Copy,
                                       scale=subg[:, 0:1]).then_inc(mix_hi, 1)
                    else:
                        act.activation(hH[:, k, chunk(c)], xr[:, k - 4, chunk(c)], ACT.Copy).then_inc(mix_hi, 1)
            with act.Fori(0, 3) as i:
                for f in range(2):
                    cast(wiH[:, f], f, i + (used_wo[f] + 1), (w_ready, i * 6 + (5 + f)))
            act.wait_ge(mix_lo, NC * KT)
            for j, w in enumerate(("g0", "u0")):
                cast(guH[0][:, j].rearrange("p k n -> p (k n)"), *first(1, w))
            norm(2, lambda c, k: (w_x, 6 + 18 + 2 * c + (k - 5 if k > 5 else 0)))
            ffn_act(1, 0, False, True)
            with act.Fori(1, NG - 1) as i:
                ffn_act(1, i, False)
            ffn_act(1, NG - 1, True)
            norm(3, lambda c, k: (ffn[1]["x"], 3 + (NG - 1) * 24 + c * KT + k + 1))

        @blk.vector
        def _(dve):
            chain = [0]

            def link(ins):
                chain[0] += 1
                ins.then_inc(step, 1)
                dve.wait_ge(step, chain[0])

            def lo(dst, slot, n, hi, count):
                dve.wait_ge(w_hi, count)
                dve.tensor_tensor(dst, raw[:, slot], hi.bitcast(F32), ALU.subtract).then_inc(raw_used[slot], 1)

            def flat(w):
                return w.rearrange("p k n -> p (k n)")

            for s in range(SLOTS):
                dve.sem_inc(raw_used[s], 1)
            for z in range(2):
                dve.sem_inc(ffn[z]["prod"], 2)
                dve.sem_inc(ffn[z]["x"], 3)
                dve.sem_inc(ffn[z]["hidlo"], 2)
            dve.sem_inc(t_lo, 1)
            dve.sem_inc(o_done, 2)
            dve.sem_inc(w_x, 6)
            link(dve.memset(rows[:], 0.0))
            for q in range(4):
                link(dve.memset(rows[32 * q:32 * q + 1, q:q + 1], float(D)))
            dve.memset(ones[:], 1.0 / D).then_inc(cons, 1)
            dve.memset(eps[:], EPS).then_inc(cons, 1)
            dve.memset(cs[:], 0.0).then_inc(cons, 1)
            dve.wait_ge(smalls, N_SMALL)
            g0, g1 = glam[:, 0], glam[:, 1]
            lt = hout[:].rearrange("p a b -> p (a b)")
            link(dve.tensor_scalar(lt, g0, -1.0, 0.0, ALU.mult, ALU.max))
            link(dve.tensor_scalar(g1, g0, -1.0, None, ALU.mult))
            link(dve.tensor_tensor(g1, g0, g1, ALU.min))
            dve.tensor_copy(lnorm[:, 0:8], g1).then_inc(rl_in, 1)
            dve.wait_ge(rl_exp, 1)
            y, q, r = lnorm[:, 8:16], lnorm[:, 16:24], lnorm[:, 24:32]
            link(dve.tensor_scalar(q, y, 2.0, None, ALU.add))
            link(dve.reciprocal(q, q))
            link(dve.tensor_tensor(y, y, q, ALU.mult))
            link(dve.tensor_tensor(q, y, y, ALU.mult))
            link(dve.memset(r, 1.0 / 17))
            for n in range(15, 0, -2):
                link(dve.tensor_tensor(r, r, q, ALU.mult))
                link(dve.tensor_scalar(r, r, 1.0 / n, None, ALU.add))
            link(dve.tensor_tensor(r, r, y, ALU.mult))
            link(dve.scalar_tensor_tensor(r, r, 2.0, lt, ALU.mult, ALU.add))
            link(dve.tensor_scalar(g0, r, -8.0, None, ALU.mult))
            link(dve.tensor_scalar(g1, r, 8.0, None, ALU.mult))
            link(dve.tensor_scalar(subg[:], subg[:], 1.0 - LAM_INIT, None, ALU.mult))

            def mod_add(b):
                dve.wait_ge(mod_sum, b + 1)
                at = slice(4 * b, 4 * b + 4) if isinstance(b, int) else bass.ds(b * 4, 4)
                dve.tensor_tensor(mod[:, at], ps[:, mod_bank(b), 0:8].rearrange("p (n c) -> p n c", c=2), bmod[:, at],
                                  ALU.add).then_inc(mod_done, 1)

            def scale_of(z):
                s = mod[:, (3 * z + 1) * KT:(3 * z + 2) * KT]
                link(dve.scalar_tensor_tensor(s, s, 1.0, ng[:, z], ALU.add, ALU.mult))

            def gate_of(z):
                s = mod[:, (3 * z + 2) * KT:(3 * z + 3) * KT]
                link(dve.tensor_scalar(s, s, 0.5, None, ALU.mult))

            def inverse(s, c):
                dve.wait_ge(s["sd"], c + 1)
                link(dve.reciprocal(quart[:], quart[:]))
                dve.tensor_tensor(tmp[:, 0].rearrange("p (q n) -> p q n", q=4),
                                  quart[:].unsqueeze(1).to_broadcast([P, 4, CH // 4]),
                                  rows[:].unsqueeze(2).to_broadcast([P, 4, CH // 4]), ALU.mult).then_inc(s["rd"], 1)
                dve.wait_ge(s["rs"], c + 1)

            def apply(z, c, between=None):
                s = nrm[z]
                inverse(s, c)

                def part(k, b, e):
                    return tmp[:, 2 + k % 2, b - c * CH:e - c * CH]

                def lo_part(k):
                    dve.wait_ge(s["hi"], c * KT + k + 1)
                    for cond, b, e in conds(c):
                        m = dve.scalar_tensor_tensor(hL[:, k, b:e], part(k, b, e), mod[:, 3 * z * KT + k, cond:cond + 1],
                                                     hH[:, k, b:e].bitcast(F32), ALU.add, ALU.subtract)
                    m.then_inc(s["h"], 1)

                for k in range(KT):
                    if c * KT + k >= 2:
                        dve.wait_ge(s["h"], c * KT + k - 1)
                    for cond, b, e in conds(c):
                        m = dve.scalar_tensor_tensor(part(k, b, e), x[:, k, b:e],
                                                     mod[:, (3 * z + 1) * KT + k, cond:cond + 1],
                                                     rstd[:, b - c * CH:e - c * CH], ALU.mult, ALU.mult)
                    m.then_inc(s["hf"], 1)
                    if k:
                        lo_part(k - 1)
                    if between is not None:
                        between(k)
                lo_part(KT - 1)
                if c == NC - 1:
                    dve.wait_ge(s["h"], NC * KT)

            def final(c, between=None):
                inverse(nrm[3], c)
                for k in range(KT):
                    xt = x[:, k, chunk(c)]
                    dve.scalar_tensor_tensor(xt, xt, fg[:, k:k + 1], rstd[:], ALU.mult, ALU.mult).then_inc(y_done, 1)
                    if between is not None:
                        between(k)
                dve.wait_ge(y_done, (c + 1) * KT)
                dve.sem_inc(nrm[3]["h"], KT)

            for b in range(4):
                if b == 3:
                    for j, w in enumerate(("g0", "u0")):
                        slot, n = first(0, w)
                        lo(flat(guL[0][:, j]), slot, n, flat(guH[0][:, j]), j + 1)
                mod_add(b)
            dve.wait_ge(mod_done, 4)
            scale_of(0)
            for c in range(NC):
                dve.wait_ge(xin[c], 16)
                apply(0, c, (lambda k: mod_add(5) if k == 1 else None) if c == 2 else None)
                if c == 1:
                    mod_add(4)
            dve.wait_ge(mod_done, 6)
            gate_of(0)

            def ffn_dve(z, i, last, w0, first=False):
                s = ffn[z]
                gate = (3 * 2 * z + 2) * KT
                with_mod = not (first and z == 0)

                def hidden(f, c):
                    o = i * 6 + (f * NC + c)
                    b = (f * NC + c) % 2
                    dve.wait_ge(s["silu"], o + 3)
                    dve.wait_ge(s["hidlo"], o + 1)
                    dve.wait_ge(s["u"], o + 7)
                    dve.tensor_tensor(tmp[:, 2 + b], ps[:, gate_bank(f, c, first)[1], 0:CH], tmp[:, b], ALU.mult).then_inc(s["prod"], 1)
                    dve.wait_ge(s["hidhi"], o + 1)
                    dve.tensor_tensor(hidL[:, f, chunk(c)], tmp[:, 2 + b], hidH[:, f, chunk(c)].bitcast(F32),
                                      ALU.subtract).then_inc(s["hidlo"], 1)

                def weights(dst_lo, dst_hi, item, j):
                    slot, n = nth(z, item, i)
                    lo(dst_lo, slot, n, dst_hi, i * 6 + (w0 + j))

                def add(c, t):
                    dve.wait_ge(s["d"], i * 24 + (c * KT + t + 25))
                    for cond, b, e in conds(c):
                        m = dve.scalar_tensor_tensor(x[:, t, b:e], ps[:, 4 + (c * KT + t) % 3, b - c * CH:e - c * CH],
                                                     mod[:, gate + t, cond:cond + 1], x[:, t, b:e],
                                                     ALU.mult, ALU.add)
                    m.then_inc(s["x"], 1)

                def gu1(j):
                    weights(flat(guL[1][:, j]), flat(guH[1][:, j]), "gu"[j] + "1", j + 1)

                if with_mod:
                    gu1(0)
                    gu1(1)
                    hidden(0, 0)
                    if z == 0:
                        mod_add(i + PRE)
                else:
                    hidden(0, 0)
                    mod_add(6)
                    gu1(0)
                    hidden(0, 1)
                    gu1(1)
                    mod_add(PRE)
                for j in range(2):
                    weights(dnL[:, j], dnH[:, j], f"d{j}", j + 3)
                if with_mod:
                    hidden(0, 1)
                hidden(0, 2)
                if not last:
                    for j, w in enumerate("gu"):
                        weights(flat(guL[0][:, j]), flat(guH[0][:, j]), w + "0", j + 5)
                for c in range(NC):
                    hidden(1, c)
                dve.wait_ge(s["x"], i * 24 + 3)
                if last and z == 0:
                    dve.wait_ge(mod_done, NB_MOD)
                    scale_of(1)
                    scale_of(2)
                    gate_of(2)
                for c in range(2 if last else NC):
                    for t in range(KT):
                        add(c, t)
                    if last and z == 0:
                        lo(wiL[:, c], c, None, wiH[:, c], whi_in + c + 1)
                if last:
                    follow = final if z else lambda c, between=None: apply(1, c, between)
                    dve.wait_ge(s["x"], i * 24 + 3 + 2 * KT)
                    follow(0, lambda k: add(2, k))
                    dve.wait_ge(s["x"], i * 24 + 3 + 3 * KT)
                    follow(1)
                    follow(2)

            ffn_dve(0, 0, False, 2, True)
            with dve.Fori(1, NG - 1) as i:
                ffn_dve(0, i, False, 2)
            ffn_dve(0, NG - 1, True, 2)

            def conv(j):
                xc = x[:, XC[j % 2]]
                dve.wait_ge(m_ev, 12 if j < 2 else 6 + 3 * (j + 1))
                link(dve.tensor_scalar(xc, xr[:, j], convw[:, j, 2:3], convb[:, j:j + 1], ALU.mult, ALU.add))
                for tap, off in ((0, -2), (1, -1), (3, 1)):
                    for b, end in ((0, CTX), (CTX, T)):
                        lo_t, hi_t = max(b, b - off), min(end, end - off)
                        link(dve.scalar_tensor_tensor(xc[:, lo_t:hi_t], xr[:, j, lo_t + off:hi_t + off],
                                                      convw[:, j, tap:tap + 1], xc[:, lo_t:hi_t], ALU.mult, ALU.add))
                dve.sem_inc(xc_ready, 1)

            for e in range(2, 4):
                lo(wiL[:, e % 2], e % 2, None, wiH[:, e % 2], whi_in + e + 1)
            dve.wait_ge(spilled, 16 * KT)
            conv(0)
            for e in range(4, 6):
                lo(wiL[:, e % 2], e % 2, None, wiH[:, e % 2], whi_in + e + 1)
            for j in range(RGT):
                xc = x[:, XC[j % 2]]
                dve.wait_ge(gate_ev, 12 * j + 12)
                for d in range(2):
                    link(dve.tensor_tensor(x[:, 2 + 2 * d], x[:, 2 + 2 * d], xc, ALU.mult))
                for d in range(2):
                    dve.wait_ge(rg_e, 2 * j + d + 1)
                    link(dve.tensor_tensor(xr[:, j], x[:, 5 + d], x[:, 5 + d], ALU.mult))
                    dve.scalar_tensor_tensor(x[:, 1 + 2 * d], xr[:, j], 1.0, x[:, 1 + 2 * d], ALU.add,
                                             ALU.mult).then_inc(rg_m, 1)
                    dve.wait_ge(rg_m, 2 * j + d + 1)
                if j + 1 < RGT:
                    conv(j + 1)
                for d in range(2):
                    dve.wait_ge(rg_s, 2 * j + d + 1)
                    bx, r = x[:, 2 + 2 * d], x[:, 1 + 2 * d]
                    link(dve.tensor_tensor(bx, r, bx, ALU.mult))
                    for b, end, init in ((0, CTX, 0.0), (CTX, T, h0[:, j, d:d + 1])):
                        s = slice(b, end) if d == 0 else slice(end - 1, b - 1 if b else None, -1)
                        link(dve.tensor_tensor_scan(x[:, 1 + 2 * d, s], x[:, 5 + d, s], x[:, 2 + 2 * d, s], init,
                                                    ALU.mult, ALU.add))
                    last_t = CTX - 1 if d == 0 else 0
                    link(dve.tensor_copy(hout[:, j, d:d + 1], x[:, 1 + 2 * d, last_t:last_t + 1]))
                dve.tensor_tensor(xr[:, j], x[:, 1], x[:, 3], ALU.add).then_inc(rg_y, 1)
                for kk in range(2):
                    lo(wiL[:, kk], kk if j in (0, 3) else 2 + kk, None, wiH[:, kk], whi_in + 7 + 2 * j + kk)
            for j in range(RGT):
                dve.wait_ge(gelu, j + 1)
                dve.wait_ge(rg_y, j + 1)
                dve.tensor_tensor(xr[:, j], xr[:, j], xg[:, j], ALU.mult).then_inc(rg_out, 1)
            dve.wait_ge(acst, N_ACST)
            for j in range(2):
                link(dve.tensor_tensor(dl[:, 2 * j], dl[:, 2 * j], dl[:, 2 * j + 1], ALU.mult))
                link(dve.tensor_reduce(lams[:, j:j + 1], dl[:, 2 * j], AX.X, ALU.add))
            dve.sem_inc(lam_p, 1)
            swap = [(p + 16) % 32 for p in range(32)]
            for e in range(KT):
                if e < 6:
                    lo(wiL[:, e % 2], e % 2, None, wiH[:, e % 2], whi_in + 15 + e)
                dve.wait_ge(m_ev, 6 + 24 + 3 * (e + 1))
                xt = x[:, e, CTX:T]
                if e == KT - 1:
                    dve.stream_shuffle(swp[:], xt, swap).then_inc(swapped, 1)
                    break
                link(dve.stream_shuffle(swp[:], xt, swap))
                link(dve.tensor_tensor(xt, xt, cosT[:], ALU.mult))
                link(dve.tensor_tensor(swp[:], swp[:], sinT[:], ALU.mult))
                link(dve.tensor_tensor(xt, xt, swp[:], ALU.add))
            dve.sem_inc(roped, 1)

            dve.wait_ge(lam_e, 1)
            link(dve.tensor_tensor(nlam[:], lams[:, 3:4], lams[:, 2:3], ALU.subtract))
            link(dve.tensor_scalar(nlam[:], nlam[:], -LAM_INIT, None, ALU.add))
            chain0 = chain[0]
            STEPS = 36

            def split_qk(hd):
                if isinstance(hd, int) and hd == 0:
                    dve.wait_ge(pp_hi, 1)
                    dve.tensor_tensor(kL[:, 0:T], x[:, 4], kH[:, 0:T].bitcast(F32), ALU.subtract).then_inc(pp_pool, 1)
                dve.wait_ge(pp_hi, hd * 5 + 2)
                dve.tensor_tensor(kL[:, T:KEYS], kc[:, hd], kH[:, T:KEYS].bitcast(F32), ALU.subtract).then_inc(pp_lo, 1)
                dve.wait_ge(pp_hi, hd * 5 + 3)
                dve.scalar_tensor_tensor(qL[:], x[:, hd], DH ** -0.5, qH[:].bitcast(F32), ALU.mult,
                                         ALU.subtract).then_inc(pp_lo, 1)

            def p_lo(head, t, g):
                w = min(3, KEY_TILES[t] - 3 * g)
                if w > 0:
                    dve.wait_ge(t_hi, count(head, GROUPS, GROUP0[t] + g + 1))
                    at = slice(pt_at(t) + 3 * g, pt_at(t) + 3 * g + w)
                    dve.tensor_tensor(flat(pTL[:, at]), ps[:, 6, 0:w * P], flat(pTH[:, at]).bitcast(F32),
                                      ALU.subtract).then_inc(t_lo, 1)

            def output(head, t):
                dve.wait_ge(o_half, count(head, 9, t + 1))
                dve.scalar_tensor_tensor(v[:, t, bass.ds(count(head, P, 0), P)], ps[:, 7, P:2 * P], rec[:, t % 3, 0:1],
                                         tmp[:, t % 3, 0:P], ALU.mult, ALU.add).then_inc(o_done, 1)

            def head(h, before, last=False):
                k_in = [0]

                def hlink(ins):
                    k_in[0] += 1
                    ins.then_inc(step, 1)
                    dve.wait_ge(step, h * STEPS + (chain0 + k_in[0]))

                def maxima(n, m):
                    dve.wait_ge(s_ready, h * 18 + (2 * n + m + 1))
                    src = ps[:, 3 * m, 0:CTX] if n == 0 else ps[:, 3 * m:3 * m + 3, 0:CH]
                    hlink(dve.tensor_reduce(mx[:, n % 2, m:m + 1], src, AX.X if n == 0 else AX.XY, ALU.max))
                    dve.tensor_scalar(nmx[:, n % 2, m:m + 1], mx[:, n % 2, m:m + 1], -1.0, None,
                                      ALU.mult).then_inc(mx_ready, 1)

                def difference(t):
                    r = t % 3
                    dve.wait_ge(e_done, h * 18 + (2 * t + 2))
                    hlink(dve.reciprocal(rec[:, r], sums[:, r]))
                    hlink(dve.scalar_tensor_tensor(coef[:, r:r + 1], sums[:, r, 0:1], nlam[:, 0:1],
                                                   rec[:, r, 1:2], ALU.mult, ALU.mult))
                    dve.scalar_tensor_tensor(probs(t, 0), probs(t, 1), coef[:, r:r + 1], probs(t, 0), ALU.mult,
                                             ALU.add).then_inc(pd_ready, 1)

                for n in range(9):
                    if n == 0:
                        if before:
                            p_lo((h, -1), 8, 0)
                        split_qk(h)
                        if before:
                            p_lo((h, -1), 8, 1)
                            output((h, -1), 7)
                        for m in range(2):
                            maxima(0, m)
                        if before:
                            p_lo((h, -1), 8, 2)
                        difference(0)
                        continue
                    for m in range(2):
                        maxima(n, m)
                        p_lo((h, 0), n - 1, m)
                    difference(n)
                    p_lo((h, 0), n - 1, 2)
                    if n > 1 or before:
                        output(*tile_of(h, n - 2))
                    if last and n == 5:
                        dve.wait_ge(o_sd, 1)
                        dve.reciprocal(ss[:, 0:NH - 1], ss[:, 0:NH - 1]).then_inc(o_rec, 1)
                assert k_in[0] == STEPS, k_in

            dve.wait_ge(outs, 48)
            head(0, False)
            dve.wait_ge(last_rope, 3)
            with dve.Fori(1, NH - 1) as h:
                head(h, True)
            head(NH - 1, True, True)
            for g in range(3):
                p_lo((NH, -1), 8, g)
            output((NH, -1), 7)
            output((NH, -1), 8)
            chain[0] += NH * STEPS

            dve.wait_ge(o_sd, 2)
            link(dve.reciprocal(ss[:, NH - 1], ss[:, NH - 1]))

            def sub_norm(c):
                for t in range(3 * c, 3 * c + 3):
                    o = v[:, t, (NH - 1) * P:NH * P]
                    m = dve.tensor_scalar(o, o, ss[:, NH - 1, t:t + 1], None, ALU.mult)
                m.then_inc(o_nrm, 1)

            sub_norm(0)
            for c in range(NC):
                for j, k in enumerate(MIX_ORDER):
                    dve.wait_ge(mix_hi, c * KT + j + 1)
                    hi = hH[:, k, chunk(c)].bitcast(F32)
                    if k < NH:
                        m = dve.scalar_tensor_tensor(hL[:, k, chunk(c)], ps[:, 6 + (c * NH + k) % 2, 0:CH], subg[:, 0:1], hi,
                                                     ALU.mult, ALU.subtract)
                    else:
                        m = dve.tensor_tensor(hL[:, k, chunk(c)], xr[:, k - 4, chunk(c)], hi, ALU.subtract)
                    m.then_inc(mix_lo, 1)
                    if j == RGT - 1 and c + 1 < NC:
                        sub_norm(c + 1)

            def w_add(i, c, f):
                dve.wait_ge(w_ready, i * 6 + (2 * c + f + 1))
                for cond, b, e in conds(c):
                    xt = x[:, i * 2 + f, b:e]
                    m = dve.scalar_tensor_tensor(xt, ps[:, f * NC + c, b - c * CH:e - c * CH],
                                                 mod[:, i * 2 + (5 * KT + f), cond:cond + 1], xt, ALU.mult, ALU.add)
                m.then_inc(w_x, 1)

            dve.wait_ge(xback, 16 * KT)
            with dve.Fori(0, 3) as i:
                for c in range(NC):
                    for f in range(2):
                        w_add(i, c, f)
                        if c == NC - 1:
                            lo(wiL[:, f], f, None, wiH[:, f], i * 2 + (whi_wo + 3 + f))
            whi_f2 = whi_wo + 8
            for j, w in enumerate(("g0", "u0")):
                slot, n = first(1, w)
                lo(flat(guL[0][:, j]), slot, n, flat(guH[0][:, j]), whi_f2 + j + 1)
            for c in range(2):
                for f in range(2):
                    w_add(3, c, f)
            apply(2, 0, lambda k: w_add(3, 2, k // 6) if k in (5, 7) else None)
            apply(2, 1)
            apply(2, 2)
            ffn_dve(1, 0, False, whi_f2 + 2, True)
            with dve.Fori(1, NG - 1) as i:
                ffn_dve(1, i, False, whi_f2 + 2)
            ffn_dve(1, NG - 1, True, whi_f2 + 2)
    return nc


def program(nc, shapes):
    a = {name: nc.dram_tensor("in_" + name, list(shape), F32, kind="ExternalInput").ap() for name, shape in shapes.items()}
    out = {name: nc.dram_tensor("out_" + name, list(shape), F32, kind="ExternalOutput").ap()
           for name, shape in (("y", (KT, P, T)), ("k", (NH, P, P)), ("v", (P, 512)), ("h", (P, RGT, 2)))}
    return build(nc, a, out)


def rope_tables():
    n = DH // 4
    inv = (np.float32(10000.0) ** (-np.arange(n, dtype=np.float32) / np.float32(n))).astype(np.float32)
    tok = np.arange(LAT)
    pos = np.stack([tok // GRID_W, tok % GRID_W]).astype(np.float32)
    p = np.arange(P)
    ang = pos[(p % DH) // (DH // 2)] * inv[p % n][:, None]
    sign = np.where(p % (2 * n) < n, -1.0, 1.0).astype(np.float32)[:, None]
    return np.cos(ang).astype(np.float32), (np.sin(ang) * sign).astype(np.float32)


def kernel(x_prompt, x_sample, cache_attn_k, cache_attn_v, state_rglru, c, c_ctx, norm_g, w_mod, b_mod,
           ffn_w_gate, ffn_w_up, ffn_w_down, w_in, w_out, diff_lambda, subln_g, conv_w, conv_b,
           rg_w_r, rg_b_r, rg_w_i, rg_b_i, rg_lambda, final_g):
    import concourse.bacc as bacc
    from concourse.bass_utils import run_bass_kernel_spmd

    def cols(w, n):
        r, m = w.shape
        return w.reshape(r // P, P, m // n, n).transpose(2, 1, 0, 3)

    cos, sin = rope_tables()
    sel = np.zeros((P, 2), np.float32)
    for q in range(4):
        sel[32 * q, 0] = sel[32 * q + 1, 1] = 1.0
    w3 = np.asarray(w_in)[0]
    q_, k_, v_, xr_, xg_ = (w3[:, 512 * n:512 * (n + 1)] for n in range(5))
    bmod = np.asarray(b_mod)[0].reshape(9 * KT, P).T
    ngt = np.asarray(norm_g)[0].reshape(3, KT, P).transpose(2, 0, 1)
    gwt = np.stack([np.asarray(rg_w_r)[0], np.asarray(rg_w_i)[0]])
    ffn_cols = lambda w: np.concatenate([cols(np.asarray(w)[0, z], P) for z in range(2)]).reshape(2 * FT, P, D)
    arrays = {
        "x": np.concatenate([np.asarray(x_prompt)[0], np.asarray(x_sample)[0]]).T.reshape(KT, P, T),
        "c": np.stack([np.asarray(c_ctx), np.asarray(c)[0]]).reshape(2, KT, P).transpose(2, 1, 0),
        "w_mod": cols(np.asarray(w_mod)[0], 512).reshape(NB_MOD, P, 4, 1024).transpose(0, 2, 1, 3),
        "bmod": np.stack([bmod, bmod], axis=2),
        "ng": np.stack([ngt, ngt], axis=3),
        "fg": np.asarray(final_g).reshape(KT, P).T,
        "w_gate": ffn_cols(ffn_w_gate),
        "w_up": ffn_cols(ffn_w_up),
        "w_down": np.asarray(ffn_w_down)[0].reshape(2 * FT, P, D),
        "w_in": cols(np.concatenate([xr_, xg_, q_, k_], axis=1), P).reshape(16, P, D),
        "w_v": cols(v_, 256).reshape(2, P, 2, 1024).transpose(0, 2, 1, 3).reshape(4, P, 1024),
        "w_out": cols(np.asarray(w_out)[0], P).reshape(KT, P, D),
        "kc": np.asarray(cache_attn_k)[0, 0].transpose(1, 2, 0),
        "vc": np.asarray(cache_attn_v)[0, 0].reshape(P, NH * P),
        "h0": np.asarray(state_rglru)[0, 0].reshape(2, RGT, P).transpose(2, 1, 0),
        "dl": np.asarray(diff_lambda)[0].reshape(4 * DH),
        "subg": np.asarray(subln_g)[0].reshape(P, 1),
        "convw": np.asarray(conv_w)[0].reshape(4, RGT, P).transpose(2, 1, 0),
        "convb": np.asarray(conv_b)[0].reshape(RGT, P).T,
        "gw": gwt.reshape(2, 2, RGT, 2, DH, DH).transpose(3, 4, 2, 1, 0, 5).reshape(P, 1024),
        "gbias": np.stack([np.asarray(rg_b_r)[0], np.asarray(rg_b_i)[0]]).reshape(2, 2, RGT, P).transpose(3, 2, 1, 0),
        "glam": np.asarray(rg_lambda)[0].reshape(2, RGT, P).transpose(2, 1, 0).reshape(P, 2 * RGT),
        "cos": cos,
        "sin": sin,
        "sel": sel,
        "ident": np.eye(P, dtype=np.float32),
    }
    arrays = {name: np.ascontiguousarray(v) for name, v in arrays.items()}
    nc = bacc.Bacc("TRN2", target_bir_lowering=False, num_devices=1)
    program(nc, {name: v.shape for name, v in arrays.items()})
    got = run_bass_kernel_spmd(nc, [{"in_" + name: v for name, v in arrays.items()}], core_ids=[0]).results[0]
    y = got["out_y"].reshape(D, T).T
    return (np.ascontiguousarray(y[:CTX])[None], np.ascontiguousarray(y[CTX:])[None],
            np.ascontiguousarray(got["out_k"].transpose(2, 0, 1))[None, None],
            got["out_v"].reshape(1, 1, P, NH, P),
            np.ascontiguousarray(got["out_h"].transpose(2, 1, 0)).reshape(1, 1, 2, RGT * P))
```
